# Optimizing a Trainium2 kernel written in Bass

```python
import jax, jax.numpy as jnp
from jax import lax
import numpy as np

D_MODEL = 1024
BATCH = 1
SEQ = 1024
DEPTH = 1
DEC_BATCH = 8
DEC_SEQ = 16
PAST_LEN = 256

CHUNK = 64
N_HEADS_A = 16
HEAD_DIM = 64
D_ATT = N_HEADS_A * HEAD_DIM
D_RNN = D_MODEL
N_RNN_BLOCKS = 16
RNN_BLOCK = D_RNN // N_RNN_BLOCKS
CONV_WIDTH = 4
RGLRU_C = 8.0
N_GROUPS = 4
EXPERTS_PER_GROUP = 8
N_EXPERTS = N_GROUPS * EXPERTS_PER_GROUP
TOP_K = 2
D_EXPERT = 512
Q_BLOCK = 128
MOE_BLOCK = 128
FORGET_BIAS_INIT = 2.0
EPS = 1e-6
D_IN = 3 * D_ATT + N_HEADS_A + 2 * D_RNN
SPLITS = [D_ATT, 2 * D_ATT, 3 * D_ATT, 3 * D_ATT + N_HEADS_A, 3 * D_ATT + N_HEADS_A + D_RNN]

kernel_name = 'fox_rglru_hmoe_stream_step'

def rms_norm(x, g):
    xf = x.astype(jnp.float32)
    y = xf * lax.rsqrt(jnp.mean(xf * xf, axis=-1, keepdims=True) + EPS)
    return (y * g.astype(jnp.float32)).astype(x.dtype)

def modulate(h, shift, scale):
    return h * (1 + scale[:, None, :]) + shift[:, None, :]

def fox_attention(q, k_all, v_all, logf_all, past_len):
    B, T, H, dh = q.shape
    L = k_all.shape[1]
    F = jnp.cumsum(logf_all.astype(jnp.float32), axis=1)
    Fk = jnp.transpose(F, (0, 2, 1))
    Fq = Fk[:, :, past_len:]
    qb = min(T, Q_BLOCK)
    nb = T // qb
    k_pos = jnp.arange(L)
    scale = HEAD_DIM ** -0.5
    q_blocks = q.reshape(B, nb, qb, H, dh).transpose(1, 0, 2, 3, 4)
    fq_blocks = Fq.reshape(B, H, nb, qb).transpose(2, 0, 1, 3)
    pos_blocks = (past_len + jnp.arange(T)).reshape(nb, qb)

    def one_block(args):
        qblk, fq, qpos = args
        s = jnp.einsum('bqhd,bkhd->bhqk', qblk, k_all, preferred_element_type=jnp.float32) * scale
        s = s + (fq[..., :, None] - Fk[:, :, None, :])
        s = jnp.where(k_pos[None, :] <= qpos[:, None], s, -jnp.inf)
        p = jax.nn.softmax(s, axis=-1)
        return jnp.einsum('bhqk,bkhd->bqhd', p.astype(v_all.dtype), v_all)

    o = lax.map(one_block, (q_blocks, fq_blocks, pos_blocks))
    return o.transpose(1, 0, 2, 3, 4).reshape(B, T, H * dh)

def linear_scan(a, b, h0):
    b = b.at[:, 0].add(a[:, 0] * h0)

    def comb(l, r):
        return (l[0] * r[0], r[0] * l[1] + r[1])

    _, h = lax.associative_scan(comb, (a, b), axis=1)
    return h

def rglru_branch(xb, gb, conv_buf, h0, p):
    B, T, _ = xb.shape
    xp = jnp.concatenate([conv_buf.astype(xb.dtype), xb], axis=1)
    xc = p['conv_b'] + sum(xp[:, k:k + T] * p['conv_w'][k] for k in range(CONV_WIDTH))
    new_buf = xp[:, -(CONV_WIDTH - 1):]
    xr = xc.reshape(B, T, N_RNN_BLOCKS, RNN_BLOCK)
    r = jax.nn.sigmoid(jnp.einsum('btnc,ncd->btnd', xr, p['w_r']).reshape(B, T, D_RNN) + p['b_r'])
    i = jax.nn.sigmoid(jnp.einsum('btnc,ncd->btnd', xr, p['w_i']).reshape(B, T, D_RNN) + p['b_i'])
    log_a = -RGLRU_C * r.astype(jnp.float32) * jax.nn.softplus(-p['rglru_lambda'].astype(jnp.float32))
    a = jnp.exp(log_a)
    mult = jnp.sqrt(-jnp.expm1(2.0 * log_a))
    b = mult * (i * xc).astype(jnp.float32)
    h = linear_scan(a, b, h0.astype(jnp.float32))
    y = h.astype(xb.dtype) * jax.nn.gelu(gb)
    return y, new_buf, h[:, -1]

def grouped_experts(xf, eid, wts, w1, w3, w2):
    N, D = xf.shape
    A = N * TOP_K
    flat_e = eid.reshape(-1)
    flat_w = wts.reshape(-1)
    order = jnp.argsort(flat_e)
    e_sorted = flat_e[order]
    tok_sorted = order // TOP_K
    counts = jnp.bincount(flat_e, length=N_EXPERTS)
    padded = (counts + MOE_BLOCK - 1) // MOE_BLOCK * MOE_BLOCK
    pad_end = jnp.cumsum(padded)
    pad_start = pad_end - padded
    start = jnp.cumsum(counts) - counts
    dest = pad_start[e_sorted] + jnp.arange(A) - start[e_sorted]
    n_blocks = -(-A // MOE_BLOCK) + N_EXPERTS
    rows = jnp.full((n_blocks * MOE_BLOCK,), N, jnp.int32).at[dest].set(tok_sorted.astype(jnp.int32))
    block_e = jnp.minimum(jnp.searchsorted(pad_end, jnp.arange(n_blocks) * MOE_BLOCK, side='right'), N_EXPERTS - 1)
    x_pad = jnp.concatenate([xf, jnp.zeros((1, D), xf.dtype)], axis=0)
    xb = x_pad[rows].reshape(n_blocks, MOE_BLOCK, D)

    def expert_block(args):
        xblk, e = args
        return (jax.nn.silu(xblk @ w1[e]) * (xblk @ w3[e])) @ w2[e]

    yb = lax.map(expert_block, (xb, block_e)).reshape(-1, D)
    contrib = yb[dest] * flat_w[order][:, None].astype(yb.dtype)
    return jnp.zeros((N, D), yb.dtype).at[tok_sorted].add(contrib)

def hier_moe(h, p):
    B, T, D = h.shape
    xf = h.reshape(-1, D)
    N = xf.shape[0]
    g_prob = jax.nn.softmax((xf @ p['w_rg'] + p['b_rg']).astype(jnp.float32), axis=-1)
    p_g, g_idx = lax.top_k(g_prob, 1)
    e_logits = (xf @ p['w_re'] + p['b_re']).astype(jnp.float32).reshape(N, N_GROUPS, EXPERTS_PER_GROUP)
    e_in = jnp.take_along_axis(e_logits, g_idx[:, :, None], axis=1)[:, 0]
    e_prob = jax.nn.softmax(e_in, axis=-1)
    top_p, top_i = lax.top_k(e_prob, TOP_K)
    wts = p_g * top_p / jnp.sum(top_p, axis=-1, keepdims=True)
    eid = g_idx * EXPERTS_PER_GROUP + top_i
    y = grouped_experts(xf, eid, wts, p['w1'], p['w3'], p['w2'])
    return y.reshape(B, T, D).astype(h.dtype)

def layer(x, c, k_past, v_past, logf_past, conv_buf, h0, p):
    B, T, _ = x.shape
    P = k_past.shape[1]
    mod = jax.nn.silu(c) @ p['w_mod'] + p['b_mod']
    sh1, sc1, g1, sh2, sc2, g2 = jnp.split(mod, 6, axis=-1)
    h = modulate(rms_norm(x, p['norm1']), sh1, sc1)
    q, k, v, fl, xb, gb = jnp.split(h @ p['w_in'], SPLITS, axis=-1)
    logf = jax.nn.log_sigmoid((fl + p['b_f']).astype(jnp.float32))
    q = q.reshape(B, T, N_HEADS_A, HEAD_DIM)
    k = k.reshape(B, T, N_HEADS_A, HEAD_DIM)
    v = v.reshape(B, T, N_HEADS_A, HEAD_DIM)
    k_all = jnp.concatenate([k_past.astype(k.dtype), k], axis=1)
    v_all = jnp.concatenate([v_past.astype(v.dtype), v], axis=1)
    logf_all = jnp.concatenate([logf_past.astype(jnp.float32), logf], axis=1)
    o_a = fox_attention(q, k_all, v_all, logf_all, P)
    o_b, new_buf, h_last = rglru_branch(xb, gb, conv_buf, h0, p)
    g_a, g_b = jnp.split(jax.nn.sigmoid(h @ p['w_gate'] + p['b_gate']), 2, axis=-1)
    mix = g_a * (o_a @ p['w_pa']) + g_b * (o_b @ p['w_pb'])
    x = x + g1[:, None, :] * (mix @ p['w_out'])
    h2 = modulate(rms_norm(x, p['norm2']), sh2, sc2)
    x = x + g2[:, None, :] * hier_moe(h2, p)
    return x, (k, v, logf.astype(x.dtype), new_buf, h_last.astype(x.dtype))

def setup_inputs(seed: int = 0) -> dict:
    key = jax.random.key(seed)
    ks = jax.random.split(key, 40)
    L = DEPTH

    def nrm(i, shape, s):
        return s * jax.random.normal(ks[i], shape, jnp.float32)

    u = jax.random.uniform(ks[20], (L, D_RNN), jnp.float32, 0.9, 0.999)
    sg = u ** (1.0 / RGLRU_C)
    lam = jnp.log(sg) - jnp.log1p(-sg)
    return {
        'x_prompt': nrm(0, (BATCH, SEQ, D_MODEL), 1.0),
        'x_sample': nrm(1, (DEC_BATCH, DEC_SEQ, D_MODEL), 1.0),
        'cache_k': nrm(2, (L, DEC_BATCH, PAST_LEN, N_HEADS_A, HEAD_DIM), 1.0),
        'cache_v': nrm(3, (L, DEC_BATCH, PAST_LEN, N_HEADS_A, HEAD_DIM), 1.0),
        'cache_logf': jax.nn.log_sigmoid(FORGET_BIAS_INIT + nrm(4, (L, DEC_BATCH, PAST_LEN, N_HEADS_A), 0.5)),
        'state_conv': nrm(5, (L, DEC_BATCH, CONV_WIDTH - 1, D_RNN), 1.0),
        'state_h': nrm(6, (L, DEC_BATCH, D_RNN), 0.5),
        'c_prompt': nrm(7, (BATCH, D_MODEL), 1.0),
        'c_sample': nrm(8, (DEC_BATCH, D_MODEL), 1.0),
        'w_mod': nrm(9, (L, D_MODEL, 6 * D_MODEL), 0.5 * D_MODEL ** -0.5),
        'b_mod': nrm(10, (L, 6 * D_MODEL), 0.02),
        'norm1': 1.0 + nrm(11, (L, D_MODEL), 0.05),
        'w_in': nrm(12, (L, D_MODEL, D_IN), D_MODEL ** -0.5),
        'b_f': FORGET_BIAS_INIT + nrm(13, (L, N_HEADS_A), 0.1),
        'conv_w': nrm(14, (L, CONV_WIDTH, D_RNN), CONV_WIDTH ** -0.5),
        'conv_b': nrm(15, (L, D_RNN), 0.02),
        'w_r': nrm(16, (L, N_RNN_BLOCKS, RNN_BLOCK, RNN_BLOCK), RNN_BLOCK ** -0.5),
        'b_r': nrm(17, (L, D_RNN), 0.02),
        'w_i': nrm(18, (L, N_RNN_BLOCKS, RNN_BLOCK, RNN_BLOCK), RNN_BLOCK ** -0.5),
        'b_i': nrm(19, (L, D_RNN), 0.02),
        'rglru_lambda': lam,
        'w_gate': nrm(21, (L, D_MODEL, 2 * D_MODEL), D_MODEL ** -0.5),
        'b_gate': nrm(22, (L, 2 * D_MODEL), 0.02),
        'w_pa': nrm(23, (L, D_ATT, D_MODEL), D_ATT ** -0.5),
        'w_pb': nrm(24, (L, D_RNN, D_MODEL), D_RNN ** -0.5),
        'w_out': nrm(25, (L, D_MODEL, D_MODEL), D_MODEL ** -0.5),
        'norm2': 1.0 + nrm(26, (L, D_MODEL), 0.05),
        'w_rg': nrm(27, (L, D_MODEL, N_GROUPS), D_MODEL ** -0.5),
        'b_rg': nrm(28, (L, N_GROUPS), 0.01),
        'w_re': nrm(29, (L, D_MODEL, N_EXPERTS), D_MODEL ** -0.5),
        'b_re': nrm(30, (L, N_EXPERTS), 0.01),
        'w1': nrm(31, (L, N_EXPERTS, D_MODEL, D_EXPERT), D_MODEL ** -0.5),
        'w3': nrm(32, (L, N_EXPERTS, D_MODEL, D_EXPERT), D_MODEL ** -0.5),
        'w2': nrm(33, (L, N_EXPERTS, D_EXPERT, D_MODEL), D_EXPERT ** -0.5),
        'norm_f': 1.0 + nrm(34, (D_MODEL,), 0.05),
    }

def reference(x_prompt, x_sample, cache_k, cache_v, cache_logf, state_conv, state_h, c_prompt, c_sample,
              w_mod, b_mod, norm1, w_in, b_f, conv_w, conv_b, w_r, b_r, w_i, b_i, rglru_lambda,
              w_gate, b_gate, w_pa, w_pb, w_out, norm2, w_rg, b_rg, w_re, b_re, w1, w3, w2, norm_f):
    yp, ys = x_prompt, x_sample
    Bp = x_prompt.shape[0]
    dt = x_prompt.dtype
    outs_p, outs_s = [], []
    for l in range(DEPTH):
        p = {'w_mod': w_mod[l], 'b_mod': b_mod[l], 'norm1': norm1[l], 'w_in': w_in[l], 'b_f': b_f[l],
             'conv_w': conv_w[l], 'conv_b': conv_b[l], 'w_r': w_r[l], 'b_r': b_r[l], 'w_i': w_i[l], 'b_i': b_i[l],
             'rglru_lambda': rglru_lambda[l], 'w_gate': w_gate[l], 'b_gate': b_gate[l], 'w_pa': w_pa[l],
             'w_pb': w_pb[l], 'w_out': w_out[l], 'norm2': norm2[l], 'w_rg': w_rg[l], 'b_rg': b_rg[l],
             'w_re': w_re[l], 'b_re': b_re[l], 'w1': w1[l], 'w3': w3[l], 'w2': w2[l]}
        yp, sp = layer(yp, c_prompt,
                       jnp.zeros((Bp, 0, N_HEADS_A, HEAD_DIM), dt), jnp.zeros((Bp, 0, N_HEADS_A, HEAD_DIM), dt),
                       jnp.zeros((Bp, 0, N_HEADS_A), jnp.float32), jnp.zeros((Bp, CONV_WIDTH - 1, D_RNN), dt),
                       jnp.zeros((Bp, D_RNN), jnp.float32), p)
        ys, ss = layer(ys, c_sample, cache_k[l], cache_v[l], cache_logf[l], state_conv[l], state_h[l], p)
        outs_p.append(sp)
        outs_s.append(ss)
    y_prompt = rms_norm(yp, norm_f)
    y_sample = rms_norm(ys, norm_f)
    k_prompt = jnp.stack([s[0] for s in outs_p])
    v_prompt = jnp.stack([s[1] for s in outs_p])
    logf_prompt = jnp.stack([s[2] for s in outs_p])
    conv_prompt = jnp.stack([s[3] for s in outs_p])
    h_prompt = jnp.stack([s[4] for s in outs_p])
    k_sample = jnp.stack([s[0] for s in outs_s])
    v_sample = jnp.stack([s[1] for s in outs_s])
    logf_sample = jnp.stack([s[2] for s in outs_s])
    conv_sample = jnp.stack([s[3] for s in outs_s])
    h_sample = jnp.stack([s[4] for s in outs_s])
    return (y_prompt, y_sample, k_prompt, v_prompt, logf_prompt, conv_prompt, h_prompt,
            k_sample, v_sample, logf_sample, conv_sample, h_sample)


_drawn_inputs = setup_inputs


def setup_inputs(seed=0):
    import zlib

    import numpy as np

    out = dict(_drawn_inputs(seed))
    spreads = {}
    factors = {'cache_logf': 37.978,
     'b_r': 8.0,
     'b_i': 7.162,
     'b_gate': 8.0,
     'norm2': 2.847,
     'b_rg': 64.0,
     'b_re': 5.736}
    for name, (base, spread) in spreads.items():
        noise = np.random.default_rng([zlib.crc32(name.encode()), seed]).standard_normal(out[name].shape)
        drawn = base * np.exp(spread * noise) if base else spread * noise
        out[name] = __import__('jax').numpy.asarray(drawn.astype(out[name].dtype))
    for name, factor in factors.items():
        out[name] = (out[name] * factor).astype(out[name].dtype)
    return out
```

```python
from contextlib import ExitStack

import concourse.bass as bass
from concourse import mybir
from concourse.alu_op_type import AluOpType as ALU

F32 = mybir.dt.float32
I32 = mybir.dt.int32
U32 = mybir.dt.uint32
ACT = mybir.ActivationFunctionType
AX_X = mybir.AxisListType.X

P = 128
D = 1024
CH = D // P
SEQ = 1024
DB, DS = 8, 16
SMP = DB * DS
TOK = SEQ + SMP
NT = TOK // P
PT_ = SEQ // P
PAST = 256
LK = PAST + DS
H, HD = 16, 64
NC_ = DB + 1
G3 = 3
NG = TOK // G3
GR, EG = 4, 8
NE = GR * EG
DE = 512
NA = 2 * TOK
SLOTS = NA // P + NE
EPS = 1e-6
BIG = 3.0e38
W_Q, W_K, W_V, W_F = 0, D, 2 * D, 3 * D
W_X, W_G = 3 * D + H, 4 * D + H
R_CW, R_CB, R_BR, R_BI, R_LAM, R_BG, R_H0, R_CV = 0, 4, 5, 6, 7, 8, 10, 18
NR = 42


class Steps:

    def __init__(self, eng, sem):
        self.eng, self.sem, self.base, self.n = eng, sem, 0, 0

    def turn(self, i, per):
        self.base, self.n = i * per, 0

    def did(self, ins):
        ins.then_inc(self.sem, 1)
        self.n += 1

    def wait(self):
        self.eng.wait_ge(self.sem, self.base + self.n)


def trunk(nc, a, o):
    (y_p, y_s, k_p, v_p, lf_p, cv_p, h_p, k_s, v_s, lf_s, cv_s, h_s) = o
    with ExitStack() as ctx:
        sems = {}

        def sem(name):
            if name not in sems:
                sems[name] = nc.alloc_semaphore(name=name)
            return sems[name]

        def clear_semaphores():
            nc.all_engine_barrier()
            nc.clear_and_free_semaphores(list(sems.values()))
            nc.all_engine_barrier()
            sems.clear()

        def sb(name, shape, dt=F32):
            return ctx.enter_context(nc.sbuf_tensor(name, shape, dt))

        def dram(name, shape):
            return nc.dram_tensor(name, shape, F32, kind="Internal").ap()

        RW = CH * TOK
        R1, R2, R3, R4 = (sb(f"region{i}", [P, RW]) for i in range(1, 5))
        WR = sb("weights", [P, 8192])

        def view(region, off, *dims):
            n = 1
            for d in dims:
                n *= d
            assert off + n <= region.shape[1], (off, n)
            v = region[:, off:off + n]
            if len(dims) == 2:
                v = v.rearrange("p (x y) -> p x y", x=dims[0])
            if len(dims) == 3:
                v = v.rearrange("p (x y z) -> p x y z", x=dims[0], y=dims[1])
            return v

        hT = view(R1, 0, CH, TOK)
        oaT = view(R2, 0, CH, TOK)
        vtok = view(R3, 0, NT, D)
        obT = view(R3, 0, CH, TOK)
        mixT = view(R4, 0, CH, TOK)
        x1b = view(R2, 0, NT, D)


        ident = sb("ident", [P, P])
        upper = sb("upper", [P, P])
        ones = sb("ones", [P, P])
        causal = sb("causal", [P, P])
        causal16 = sb("causal16", [P, DS])
        cT = sb("cT", [P, CH, NC_])
        pT = sb("pT", [P, CH, NR])
        qTs = sb("qTs", [P, CH, SMP])
        kTs = sb("kTs", [P, CH, SMP])
        small = sb("small", [P, 64])
        mixtmp = sb("mixtmp", [P, 3072])
        eps = small[:, 6:7]
        sp4 = small[:, 8:16]

        mod_d = dram("mod_d", [NC_, 6 * D])
        F_d = dram("F_d", [H, SEQ])
        Fs_d = dram("Fs_d", [DB, H // 2, 2, LK])
        h2_d = dram("h2_d", [TOK, D])
        yb_d = dram("yb_d", [SLOTS * P, D])

        PS = ctx.enter_context(nc.psum_tensor("PS", [P, 8, 512], F32))

        def banks(b, n, parts=P):
            return PS[0:parts, b:b + n, :].rearrange("p b n -> p (b n)")

        xp, xs = a["x_prompt"][0], a["x_sample"].rearrange("b t d -> (b t) d")
        w_in, w_mod, w_gate, w_pa, w_pb, w_out = (
            a[n][0].rearrange("(c p) n -> p c n", p=P) for n in ("w_in", "w_mod", "w_gate", "w_pa", "w_pb", "w_out"))
        w1, w3, w2 = a["w1"][0], a["w3"][0], a["w2"][0]

        def tcols(t):
            return bass.ds(SEQ, P) if t is None else bass.ds(t * P, P)

        def spread(row, parts=P):
            return row.broadcast_to([parts, row.shape[-1]])

        def mod_load(e, dst, piece, name):
            cols = bass.ds(piece * D, D)
            e.dma_start(dst[0], spread(mod_d[0:1, cols])).then_inc(sem(name), 16)
            for b in range(DB):
                e.dma_start(dst[1][b * DS:(b + 1) * DS, :], spread(mod_d[b + 1:b + 2, cols], DS)).then_inc(sem(name), 16)
        MOD_LOAD = 16 * NC_

        crow, prow = view(R3, 0, D)[0:NC_, :], view(R3, D, D)[0:NR, :]
        mrow = view(R3, 2 * D, 2, 512)[0:NC_]
        bmod = view(R3, 3 * D, 2, 512)[0:NC_]
        csig = view(R3, 4 * D, D)[0:NC_, :]
        wmod_r = [view(WR, 4096 * j, CH, 512) for j in range(2)]
        A1 = [view(R2, 0, D), view(R2, D, D)]
        B1 = [view(R2, 2 * D, D), view(R2, 3 * D, D)]
        N1 = view(R2, 4 * D, D)
        xt = [view(R4, D * j, D) for j in range(2)]
        xn = [view(R4, D * (2 + j), D) for j in range(2)]
        ssq, rms, rst = small[:, 0:2], small[:, 2:4], small[:, 4:6]
        wv = wmod_r
        wf = sb("wf", [P, CH, H])
        bf = sb("bf", [H, 1])
        fz, fa, lf, onesw = (view(R4, TOK * k, TOK)[0:H, :] for k in range(4))
        Fp = fz[:, 0:SEQ]
        Fs = view(R4, 4 * TOK, DB, LK)[0:H]
        Fso = view(R4, 4 * TOK + DB * LK, DB, LK)[0:H]
        lfT = sb("lfT", [P, NT, H])
        clf = sb("clf", [P, DB, 2, H])
        wq, wk = view(WR, 0, CH, P), view(WR, 1024, CH, P)
        qb, kb = ([view(WR, 2048 + TOK * (2 * j + k), TOK) for j in range(2)] for k in range(2))
        sP = [view(R4, D * k, D) for k in range(3)]
        PTb = [view(R4, D * (3 + k), D) for k in range(2)]
        Bt = [view(R4, D * (5 + 2 * j), 2, D) for j in range(2)]
        kst = view(mixtmp, 2 * P, NT, P)
        ot = [view(mixtmp, P * k, P) for k in range(2)]
        mn, ls, rl = small[:, 16:32], small[:, 32:48], small[:, 48:64]
        kc = [view(WR, 4096 * j, 2, D) for j in range(2)]
        vc = [view(WR, 4096 * j + 2048, 2, D) for j in range(2)]
        kcT = [view(R4, CH * LK * j, CH, LK) for j in range(2)]
        v16 = [view(R4, 2 * CH * LK + D * j, D)[0:DS, :] for j in range(2)]
        Bs = [view(R4, 2 * CH * LK + 2 * D + 2 * LK * j, 2, LK) for j in range(2)]
        sS = [view(R4, 2 * CH * LK + 2 * D + 4 * LK + 2 * LK * j, 2, LK) for j in range(2)]
        qbd = [view(R4, 2 * CH * LK + 2 * D + 8 * LK + 256 * j, CH, 32) for j in range(2)]
        PTs = [view(mixtmp, 768 * j, 2, 3, P) for j in range(2)]
        osb = [view(mixtmp, 1536 + 2 * P * j, 2, P) for j in range(2)]
        XW = 3 + SEQ + DB * (DS + 3)
        wx = [[view(WR, 2048 * j + 1024 * k, CH, P) for k in range(2)] for j in range(2)]
        rr, ii, Rr = (view(WR, 4096 + TOK * k, TOK) for k in range(3))
        bw = [view(WR, 4096 + 3 * TOK + 256 * j, 2, P) for j in range(2)]
        xbuf = [view(R4, 1184 * j, XW) for j in range(2)]
        xbs = [xbuf[j][:, 3 + SEQ:].rearrange("p (b t) -> p b t", b=DB) for j in range(2)]
        xc = [view(R4, 2368 + TOK * j, TOK) for j in range(2)]
        gel = [view(R4, 2368 + TOK * (2 + j), TOK) for j in range(2)]
        hb = view(R4, 2368 + 4 * TOK, TOK)
        hc = sb("hc", [P, CH, 36])
        hrow = mixtmp[0:36, 0:D]
        t8 = sb("t8", [P, DB])
        wm = [[view(WR, 4096 * j + 1024 * k, CH, P) for k in range(4)] for j in range(2)]
        sg = [[view(mixtmp, 1536 * s + NG * k, NG) for k in range(2)] for s in range(2)]
        tm = [[view(mixtmp, 1536 * s + NG * (2 + k), NG) for k in range(2)] for s in range(2)]
        wo = [view(WR, 4096 * k, CH, 512) for k in range(2)]
        A2, B2, G1 = ([view(R1, D * (2 * q + k), D) for k in range(2)] for q in range(3))
        xo = [view(R1, D * (6 + j), D) for j in range(2)]
        N2 = view(R1, D * 8, D)
        mt = [view(R3, D * j, CH, P) for j in range(2)]
        h2 = [view(R3, D * (2 + j), D) for j in range(2)]
        h2T = [view(R3, D * (4 + j), CH, P) for j in range(2)]
        junk = view(R3, D * 6, D)
        wr = sb("wr", [P, CH, GR + NE])
        br = sb("br", [P, GR + NE])
        lg = sb("lg", [P, NT, GR + NE])
        _o = [0]

        def rt(*dims):
            v = view(WR, _o[0], *dims)
            n = 1
            for d in dims:
                n *= d
            _o[0] += n
            return v
        g8, gm, e8, em = (rt(NT, 8) for _ in range(4))
        gi, ei = rt(NT, 8).bitcast(U32), rt(NT, 8).bitcast(U32)
        gif, pg, ed, den = (rt(NT) for _ in range(4))
        oh4 = rt(NT, GR)
        gx = rt(NT, NE)
        E = [rt(NT, NE) for _ in range(2)]
        M, cs, pre, rk, ex = (rt(NT, NE) for _ in range(5))
        eidf, rj, sj, qj, slj, roj, dej = (rt(2, NT) for _ in range(7))
        cmp9 = rt(NE, 9)
        cmp8 = rt(2 * NT, 8)
        tot, nb, endb, startb = (rt(NE) for _ in range(4))
        iotaf = rt(P)
        thr = rt(9)
        tokf = rt(NT)
        cmpb = rt(SLOTS, NE)[0:1]
        OP = [rt(P) for _ in range(2)]
        OS = [rt(SLOTS) for _ in range(2)]
        wts = sb("wts", [P, 2, NT])
        dest = sb("dest", [P, 2, NT], U32)
        rows = sb("rows", [P, SLOTS + 1], U32)
        meta = sb("meta", [1, SLOTS + 1], I32)
        w1b = [view(R, 0, CH, DE) for R in (R1, R4)]
        w3b = [view(R, 4096, CH, DE) for R in (R1, R4)]
        w2b = [view(R3, 4096 * j, DE // P, D) for j in range(2)]
        xg = [view(WR, D * j, D) for j in range(2)]
        xT = [view(WR, D * (2 + j), CH, P) for j in range(2)]
        yo = [view(WR, D * (4 + j), D) for j in range(2)]
        hs, hh_ = view(WR, D * 6, DE), view(WR, D * 6 + DE, DE)
        hhT = view(WR, D * 7, DE // P, P)
        gidx = [sb(f"gidx{j}", [P, 1], U32) for j in range(2)]
        G2 = [view(R1, D * k, D) for k in range(2)]
        NF = view(R1, D * 2, D)
        y0, y1 = ([view(R1, D * (3 + 2 * k + j), D) for j in range(2)] for k in range(2))
        acc = [view(R3, D * j, D) for j in range(2)]
        out_t = [view(R3, D * (2 + j), D) for j in range(2)]
        cidx = [[sb(f"cidx{k}{j}", [P, 1], U32) for j in range(2)] for k in range(2)]

        copy, tt, ts, stt = nc.vector.tensor_copy, nc.vector.tensor_tensor, nc.vector.tensor_scalar, nc.vector.scalar_tensor_tensor
        act, mm, tr = nc.scalar.activation, nc.tensor.matmul, nc.tensor.transpose

        def product(out, lhs, rhs):
            for c in range(CH):
                last = mm(out, lhs(c), rhs(c), start=c == 0, stop=c == CH - 1)
            return last

        with nc.Block() as block:

            @block.sync
            def _(e):
                e.dma_start(crow[0:1, :], a["c_prompt"]).then_inc(sem("c_in"), 16)
                e.dma_start(crow[1:NC_, :], a["c_sample"]).then_inc(sem("c_in"), 16)


                def mod_weights(j, i):
                    cols = bass.ds(i * 1024 + j * 512, 512)
                    e.wait_ge(sem(f"mod_mm{j}"), i)
                    e.dma_start(wmod_r[j], w_mod[:, :, cols]).then_inc(sem(f"mod_w{j}"), 16)
                    e.wait_ge(sem(f"mod_row{j}"), i)
                    e.dma_start(bmod[:, j, :], spread(a["b_mod"][:, cols], NC_)).then_inc(sem(f"mod_b{j}"), 16)
                for i in range(2):
                    for j in range(2):
                        mod_weights(j, i)
                for r, nm in ((R_CB, "conv_b"), (R_BR, "b_r"), (R_BI, "b_i"), (R_LAM, "rglru_lambda")):
                    e.dma_start(prow[r:r + 1, :], a[nm]).then_inc(sem("p_in"), 16)
                e.dma_start(prow[R_CW:R_CW + 4, :], a["conv_w"][0]).then_inc(sem("p_in"), 16)
                e.dma_start(prow[R_BG:R_BG + 2, :], a["b_gate"].rearrange("a (r d) -> (a r) d", r=2)).then_inc(sem("p_in"), 16)
                e.dma_start(prow[R_H0:R_H0 + DB, :], a["state_h"][0]).then_inc(sem("p_in"), 16)
                e.dma_start(prow[R_CV:NR, :], a["state_conv"][0].rearrange("b k d -> (b k) d")).then_inc(sem("p_in"), 16)
                e.dma_start(wf[:], w_in[:, :, W_F:W_F + H]).then_inc(sem("wf_in"), 16)
                e.dma_start(bf[:], a["b_f"].rearrange("a h -> h a")).then_inc(sem("wf_in"), 16)
                for b in range(DB):
                    e.dma_start(clf[:, b], a["cache_logf"][0, b].rearrange("(t p) h -> p t h", p=P)).then_inc(sem("clf_in"), 16)
                for j in range(2):
                    e.wait_ge(sem(f"mod_st{j}"), 16 * 2)
                mod_load(e, A1, 1, "ab1_in")
                mod_load(e, B1, 0, "ab1_in")
                e.dma_start(N1, spread(a["norm1"])).then_inc(sem("ab1_in"), 16)
                with e.Fori(0, PT_ // 2) as i:
                    for j in range(2):
                        e.wait_ge(sem(f"xn_made{j}"), i)
                        e.dma_start(xt[j], xp[bass.ds(i * 256 + j * P, P), :]).then_inc(sem(f"x_in{j}"), 16)
                    for j in range(2):
                        mod_weights(j, i + 2)
                e.wait_ge(sem("xn_made0"), PT_ // 2)
                e.dma_start(xt[0], xs).then_inc(sem("x_in0"), 16)
                for n in range(2):
                    e.wait_ge(sem(f"mod_mm{n}"), 6)
                    e.dma_start(wv[n], w_in[:, :, W_V + 512 * n:W_V + 512 * (n + 1)]).then_inc(sem(f"wv_in{n}"), 16)
                e.wait_ge(sem("v_evA"), NT)
                e.wait_ge(sem("v_evD"), NT)
                e.dma_start(v_p[0, 0].rearrange("(t p) h d -> p t (h d)", p=P), vtok[:, 0:PT_, :]).then_inc(sem("v_out"), 16)
                e.dma_start(v_s[0].rearrange("b t h d -> (b t) (h d)"), vtok[:, PT_, :]).then_inc(sem("v_out"), 16)
                e.wait_ge(sem("lfT"), 1)
                e.dma_start(lf_p[0, 0].rearrange("(t p) h -> p t h", p=P), lfT[:, 0:PT_, :]).then_inc(sem("lf_out"), 16)
                e.dma_start(lf_s[0].rearrange("b t h -> (b t) h"), lfT[:, PT_, :]).then_inc(sem("lf_out"), 16)
                e.wait_ge(sem("F_made"), 1 + DB)
                e.dma_start(F_d, Fp).then_inc(sem("F_out"), 16)
                for g in range(2):
                    e.dma_start(Fs_d[:, :, g, :].rearrange("b h l -> h b l"), Fso[g * H // 2:(g + 1) * H // 2]).then_inc(sem("F_out"), 16)
                e.wait_ge(sem("F_out"), 48)
                for j in range(2):
                    e.wait_ge(sem(f"mod_st{j}"), 16 * 6)
                e.wait_ge(sem("v_out"), 32)
                e.wait_ge(sem("lf_out"), 32)

            @block.gpsimd
            def _(e):
                st = Steps(e, sem("pool_setup"))
                st.did(e.memset(ident[:], 0.0))
                st.did(e.memset(upper[:], 1.0))
                st.did(e.memset(causal[:], 0.0))
                st.did(e.memset(ones[:], 1.0))
                st.did(e.memset(eps, EPS))
                st.wait()
                st.did(e.affine_select(out=ident[:], in_=ident[:], compare_op=ALU.not_equal, fill=1.0, base=0,
                                       pattern=[[-1, P]], channel_multiplier=1))
                st.did(e.affine_select(out=upper[:], in_=upper[:], compare_op=ALU.is_gt, fill=0.0, base=0,
                                       pattern=[[1, P]], channel_multiplier=-1))
                st.did(e.affine_select(out=causal[:], in_=causal[:], compare_op=ALU.is_ge, fill=BIG, base=0,
                                       pattern=[[-1, P]], channel_multiplier=1))

            @block.scalar
            def _(e):
                e.wait_ge(sem("c_in"), 32)
                act(csig, crow, ACT.Sigmoid).then_inc(sem("c_sig"), 1)

                def mod_out(j, i):
                    e.wait_ge(sem(f"mod_row{j}"), i + 1)
                    e.dma_start(mod_d[:, bass.ds(i * 1024 + j * 512, 512)], mrow[:, j, :]).then_inc(sem(f"mod_st{j}"), 16)
                for i in range(2):
                    for j in range(2):
                        mod_out(j, i)

                def rms_tile(j, n):
                    e.wait_ge(sem(f"x_in{j}"), n * 16 + 16)
                    e.wait_ge(sem(f"xn_T{j}"), n)
                    act(xn[j], xt[j], ACT.Square, accum_out=ssq[:, j:j + 1]).then_inc(sem(f"ssq{j}"), 1)
                    e.wait_ge(sem(f"ssq{j}"), n + 1)
                    act(rms[:, j:j + 1], ssq[:, j:j + 1], ACT.Sqrt, scale=1.0 / D, bias=eps).then_inc(sem(f"rms{j}"), 1)

                def put_h(cols, j, n):
                    e.wait_ge(sem("pool_setup"), 8)
                    e.wait_ge(sem(f"xn_T{j}"), n + 1)
                    act(hT[:, 4:8, cols], PS[:, 5 + 2 * j, :].rearrange("p (c n) -> p c n", c=4), ACT.Copy).then_inc(sem(f"h_evA{j}"), 1)
                e.wait_ge(sem("pool_setup"), 8)
                with e.Fori(0, PT_ // 2) as i:
                    for j in range(2):
                        rms_tile(j, i)
                    for j in range(2):
                        mod_out(j, i + 2)
                        put_h(bass.ds(i * 256 + j * P, P), j, i)
                rms_tile(0, PT_ // 2)
                put_h(bass.ds(SEQ, P), 0, PT_ // 2)

                e.wait_ge(sem("pT"), 1)
                act(t8[:], pT[:, :, R_LAM], ACT.Abs).then_inc(sem("sp"), 1)
                e.wait_ge(sem("sp"), 1)
                act(t8[:], t8[:], ACT.Exp, scale=-1.0).then_inc(sem("sp"), 1)
                e.wait_ge(sem("sp"), 2)
                act(t8[:], t8[:], ACT.Ln, bias=ones[:, 0:1]).then_inc(sem("sp"), 1)

                for j in range(2):
                    e.wait_ge(sem(f"mod_st{j}"), 16 * 6)
                for q in range(0, 2 * NT, 2):
                    n, t = q // NT, q % NT
                    e.wait_ge(sem("v_mm"), q + 1)
                    act(vtok[:, t, 512 * n:512 * (n + 1)], PS[:, q % 4, :], ACT.Copy).then_inc(sem("v_evA"), 1)
                for n in range(G3):
                    e.wait_ge(sem("f_mm"), n + 1)
                    act(fz[:, n * NG:(n + 1) * NG], PS[0:H, 4 + n, 0:NG], ACT.Identity, bias=bf[:]).then_inc(sem("fz"), 1)
                e.wait_ge(sem("fz"), 3)
                act(fa, fz, ACT.Abs).then_inc(sem("fa"), 1)
                e.wait_ge(sem("fa"), 1)
                act(fa, fa, ACT.Exp, scale=-1.0).then_inc(sem("fa"), 1)
                e.wait_ge(sem("fa"), 2)
                act(fa, fa, ACT.Ln, bias=ones[0:H, 0:1]).then_inc(sem("fa"), 1)
                e.wait_ge(sem("clf_ps"), 1)
                act(Fs[:, :, 0:PAST], banks(0, 4, H).rearrange("p (b n) -> p b n", b=DB), ACT.Copy).then_inc(sem("Fs_old"), 1)

            @block.vector
            def _(e):
                e.wait_ge(sem("c_sig"), 1)
                tt(crow, crow, csig, ALU.mult).then_inc(sem("c_silu"), 1)
                e.wait_ge(sem("cT_ps"), 1)
                copy(cT[:].rearrange("p c r -> p (c r)"), PS[:, 0, 0:CH * NC_]).then_inc(sem("cT"), 1)

                def mod_rows(j, i):
                    e.wait_ge(sem(f"mod_b{j}"), i * 16 + 16)
                    e.wait_ge(sem(f"mod_st{j}"), i * 16)
                    e.wait_ge(sem(f"mod_mm{j}"), i + 1)
                    tt(mrow[:, j, :], PS[0:NC_, 2 + j, :], bmod[:, j, :], ALU.add).then_inc(sem(f"mod_row{j}"), 1)
                for i in range(2):
                    for j in range(2):
                        mod_rows(j, i)
                e.wait_ge(sem("pT_ps"), 1)
                copy(pT[:].rearrange("p c r -> p (c r)"), PS[:, 1, 0:CH * NR]).then_inc(sem("pT"), 1)

                e.wait_ge(sem("ab1_in"), 2 * MOD_LOAD + 16)
                for k in range(2):
                    stt(out=A1[k], in0=A1[k], scalar=1.0, in1=N1, op0=ALU.add, op1=ALU.mult).then_inc(sem("a1"), 1)
                e.wait_ge(sem("a1"), 2)
                st = Steps(e, sem("dve_norm1"))

                def norm_tile(j, k, n):
                    e.wait_ge(sem(f"rms{j}"), n + 1)
                    st.did(nc.vector.reciprocal(rst[:, j:j + 1], rms[:, j:j + 1]))
                    st.wait()
                    st.did(stt(out=xn[j], in0=xt[j], scalar=rst[:, j:j + 1], in1=A1[k], op0=ALU.mult, op1=ALU.mult))
                    st.wait()
                    tt(xn[j], xn[j], B1[k], ALU.add).then_inc(sem(f"xn_made{j}"), 1)

                def put_h(cols, j, n):
                    e.wait_ge(sem(f"xn_T{j}"), n + 1)
                    copy(hT[:, 0:4, cols], PS[:, 4 + 2 * j, :].rearrange("p (c n) -> p c n", c=4)).then_inc(sem(f"h_evD{j}"), 1)
                with e.Fori(0, PT_ // 2) as i:
                    st.turn(i, 4)
                    for j in range(2):
                        norm_tile(j, 0, i)
                    for j in range(2):
                        mod_rows(j, i + 2)
                        put_h(bass.ds(i * 256 + j * P, P), j, i)
                st.turn(PT_ // 2, 4)
                norm_tile(0, 1, PT_ // 2)
                put_h(bass.ds(SEQ, P), 0, PT_ // 2)

                e.wait_ge(sem("sp"), 3)
                ts(sp4, pT[:, :, R_LAM], -1.0, 0.0, ALU.mult, ALU.max).then_inc(sem("spd"), 1)
                e.wait_ge(sem("spd"), 1)
                tt(sp4, sp4, t8[:], ALU.add).then_inc(sem("spd"), 1)
                e.wait_ge(sem("spd"), 2)
                ts(sp4, sp4, 4.0, None, ALU.mult).then_inc(sem("sp4"), 1)

                for j in range(2):
                    e.wait_ge(sem(f"mod_st{j}"), 16 * 6)
                for q in range(1, 2 * NT, 2):
                    n, t = q // NT, q % NT
                    e.wait_ge(sem("v_mm"), q + 1)
                    copy(vtok[:, t, 512 * n:512 * (n + 1)], PS[:, q % 4, :]).then_inc(sem("v_evD"), 1)
                nc.vector.memset(onesw, 1.0).then_inc(sem("onesw"), 1)
                e.wait_ge(sem("fz"), 3)
                ts(lf, fz, 0.0, None, ALU.min).then_inc(sem("lf0"), 1)
                e.wait_ge(sem("fa"), 3)
                e.wait_ge(sem("lf0"), 1)
                tt(lf, lf, fa, ALU.subtract).then_inc(sem("lf"), 1)
                e.wait_ge(sem("lfT_ps"), 1)
                copy(lfT[:].rearrange("p t h -> p (t h)"), PS[:, 7, 0:NT * H]).then_inc(sem("lfT"), 1)
                e.wait_ge(sem("lf"), 1)
                e.wait_ge(sem("onesw"), 1)
                nc.vector.tensor_tensor_scan(Fp, onesw[:, 0:SEQ], lf[:, 0:SEQ], 0.0, ALU.mult, ALU.add).then_inc(sem("F_made"), 1)
                copy(Fs[:, :, PAST:LK], lf[:, SEQ:TOK].rearrange("p (b t) -> p b t", b=DB)).then_inc(sem("Fs_new"), 1)
                e.wait_ge(sem("Fs_old"), 1)
                e.wait_ge(sem("Fs_new"), 1)
                for b in range(DB):
                    nc.vector.tensor_tensor_scan(Fso[:, b, :], onesw[:, 0:LK], Fs[:, b, :], 0.0, ALU.mult, ALU.add).then_inc(sem("F_made"), 1)

            @block.tensor
            def _(e):
                e.wait_ge(sem("pool_setup"), 8)
                e.wait_ge(sem("c_silu"), 1)
                for c in range(CH):
                    last = tr(PS[:, 0, c * NC_:(c + 1) * NC_], crow[:, c * P:(c + 1) * P], ident[0:NC_, 0:NC_])
                last.then_inc(sem("cT_ps"), 1)
                e.wait_ge(sem("cT"), 1)

                def modulation(j, i):
                    e.wait_ge(sem(f"mod_row{j}"), i)
                    e.wait_ge(sem(f"mod_w{j}"), i * 16 + 16)
                    product(PS[0:NC_, 2 + j, :], lambda c: cT[:, c, :], lambda c: wmod_r[j][:, c, :]).then_inc(sem(f"mod_mm{j}"), 1)
                for i in range(2):
                    for j in range(2):
                        modulation(j, i)
                e.wait_ge(sem("p_in"), 16 * 8)
                for c in range(CH):
                    last = tr(PS[:, 1, c * NR:(c + 1) * NR], prow[:, c * P:(c + 1) * P], ident[0:NR, 0:NR])
                last.then_inc(sem("pT_ps"), 1)

                def turn_tile(j, n):
                    e.wait_ge(sem(f"xn_made{j}"), n + 1)
                    e.wait_ge(sem(f"h_evA{j}"), n)
                    e.wait_ge(sem(f"h_evD{j}"), n)
                    for c in range(CH):
                        last = tr(PS[:, 4 + 2 * j + c // 4, (c % 4) * P:(c % 4 + 1) * P], xn[j][:, c * P:(c + 1) * P], ident[:])
                    last.then_inc(sem(f"xn_T{j}"), 1)
                with e.Fori(0, PT_ // 2) as i:
                    for j in range(2):
                        modulation(j, i + 2)
                        turn_tile(j, i)
                turn_tile(0, PT_ // 2)

                for s, n in (("h_evA0", 5), ("h_evD0", 5), ("h_evA1", 4), ("h_evD1", 4)):
                    e.wait_ge(sem(s), n)
                e.wait_ge(sem("pT"), 1)
                for n in range(2):
                    e.wait_ge(sem(f"wv_in{n}"), 16)
                    for t in range(NT):
                        q = n * NT + t
                        if q >= 4:
                            e.wait_ge(sem("v_evD" if q % 2 else "v_evA"), (q - 4) // 2 + 1)
                        product(PS[:, q % 4, :], lambda c: hT[:, c, t * P:(t + 1) * P], lambda c: wv[n][:, c, :]).then_inc(sem("v_mm"), 1)

                e.wait_ge(sem("wf_in"), 32)
                for n in range(G3):
                    product(PS[0:H, 4 + n, 0:NG], lambda c: wf[:, c, :], lambda c: hT[:, c, n * NG:(n + 1) * NG]).then_inc(sem("f_mm"), 1)
                e.wait_ge(sem("clf_in"), 16 * DB)
                e.wait_ge(sem("v_evA"), NT)
                e.wait_ge(sem("v_evD"), NT)
                for b in range(DB):
                    for k in range(2):
                        last = tr(PS[0:H, b // 2, (b % 2) * PAST + k * P:(b % 2) * PAST + (k + 1) * P], clf[:, b, k, :], ident[:])
                last.then_inc(sem("clf_ps"), 1)
                e.wait_ge(sem("lf"), 1)
                for t in range(NT):
                    last = tr(PS[:, 7, t * H:(t + 1) * H], lf[:, t * P:(t + 1) * P], ident[0:H, 0:H])
                last.then_inc(sem("lfT_ps"), 1)
        clear_semaphores()

        with nc.Block() as block:

            @block.sync
            def _(e):
                count = e.alloc_register("count")
                for hh in range(P // DS):
                    e.dma_start(causal16[hh * DS:(hh + 1) * DS, :], causal[0:DS, 0:DS]).then_inc(sem("c16_in"), 16)
                def pair_weights(p):
                    e.dma_start(wq, w_in[:, :, bass.ds(p * P + W_Q, P)]).then_inc(sem("qk_w"), 16)
                    e.dma_start(wk, w_in[:, :, bass.ds(p * P + W_K, P)]).then_inc(sem("qk_w"), 16)

                def pair_sums(p, j):
                    for hh in range(2):
                        e.dma_start(Bt[j][:, hh, :], spread(F_d[bass.ds(p * 2 + hh, 1), :])).then_inc(sem(f"Bt_in{j}"), 16)

                def pair(i, j, more):
                    p = i * 2 + j
                    if more:
                        e.wait_ge(sem("kg_mm"), p * 3 + 3)
                        pair_weights(p + 1)
                    e.reg_mov(count, p + 1)
                    e.wait_ge(sem("kst_A"), p * 2 + 2)
                    e.wait_ge(sem("kst_D"), count)
                    e.dma_start(k_p[0, 0].rearrange("(t p) h d -> p t (h d)", p=P)[:, :, bass.ds(p * P, P)], kst[:, 0:PT_, :]).then_inc(sem("k_out"), 16)
                    e.dma_start(k_s[0].rearrange("b t h d -> (b t) (h d)")[:, bass.ds(p * P, P)], kst[:, PT_, :]).then_inc(sem("k_out"), 16)
                    e.dma_start(yb_d[bass.ds(p * (NE * P // CH) + NA, NE * P // CH), :].rearrange("(p s) (k n) -> p (s k) n", p=P, n=P),
                                ones[:].rearrange("p (a n) -> p a n", a=1).broadcast_to([P, NE, P])).then_inc(sem("yb_fill"), 16)
                    if more == 2:
                        e.wait_ge(sem("ttr"), p * 16 + 16)
                        pair_sums(p + 2, j)
                pair_weights(0)
                pair_sums(0, 0)
                pair_sums(1, 1)
                with e.Fori(0, CH // 2 - 1) as i:
                    pair(i, 0, 2)
                    pair(i, 1, 2)
                pair(CH // 2 - 1, 0, 1)
                pair(CH // 2 - 1, 1, 0)
                e.wait_ge(sem("k_out"), CH * 32)
                e.wait_ge(sem("yb_fill"), 16 * CH)
                e.wait_ge(sem("ot_ev"), CH * 8)
                e.wait_ge(sem("qs_cp"), CH * 2)

                def sample_loads(i, j, first):
                    b = i * 2 + j
                    if not first:
                        e.wait_ge(sem("kc_ps"), b * 2 - 2)
                    e.dma_start(kc[j], a["cache_k"][0, bass.ds(b, 1)].rearrange("a (t p) h d -> p (a t) (h d)", p=P)).then_inc(sem(f"sk_in{j}"), 16)
                    if not first:
                        e.wait_ge(sem("s_ttr"), b * 2 - 2)
                    e.dma_start(Bs[j].rearrange("p g l -> p (g l)"),
                                Fs_d[bass.ds(b, 1)].rearrange("a h g l -> (a h) (g l)").unsqueeze(1).broadcast_to([H // 2, DS, 2 * LK])).then_inc(sem(f"sB_in{j}"), 16)
                    if not first:
                        e.wait_ge(sem(f"spv{j}"), i)
                    e.dma_start(vc[j], a["cache_v"][0, bass.ds(b, 1)].rearrange("a (t p) h d -> p (a t) (h d)", p=P)).then_inc(sem(f"sv_in{j}"), 16)
                    e.dma_start(v16[j], v_s[0, bass.ds(b, 1)].rearrange("a t h d -> (a t) (h d)")).then_inc(sem(f"sv_in{j}"), 16)
                for j in range(2):
                    sample_loads(0, j, True)
                with e.Fori(1, DB // 2) as i:
                    for j in range(2):
                        sample_loads(i, j, False)
                e.wait_ge(sem("so_A"), DB)
                e.wait_ge(sem("so_D"), DB)
                e.wait_ge(sem("bw_zero"), 2)
                with e.Fori(0, CH // 2) as i:
                    for j in range(2):
                        m = i * 2 + j
                        e.wait_ge(sem(f"gb_done{j}"), i)
                        e.dma_start(wx[j][0], w_in[:, :, bass.ds(m * P + W_X, P)]).then_inc(sem(f"wx_in{j}"), 16)
                        e.dma_start(wx[j][1], w_in[:, :, bass.ds(m * P + W_G, P)]).then_inc(sem(f"wx_in{j}"), 16)
                        e.wait_ge(sem(f"ri_done{j}"), i)
                        for k, nm in enumerate(("w_r", "w_i")):
                            for q in range(2):
                                e.dma_start(bw[j][q * HD:(q + 1) * HD, k, q * HD:(q + 1) * HD],
                                            a[nm][0, bass.ds(m * 2 + q, 1)].rearrange("a c d -> (a c) d")).then_inc(sem(f"bw_in{j}"), 16)
                for j in range(2):
                    e.wait_ge(sem(f"y_made{j}"), CH // 2)
                with e.Fori(0, CH // 2) as i:
                    for j in range(2):
                        m = i * 2 + j
                        e.wait_ge(sem(f"mp_mm{j}"), i * 2 * G3)
                        for k, (w, off) in enumerate(((w_pa, 0), (w_gate, 0), (w_pb, 0), (w_gate, D))):
                            e.dma_start(wm[j][k], w[:, :, bass.ds(m * P + off, P)]).then_inc(sem(f"wm_in{j}"), 16)

            @block.gpsimd
            def _(e):
                with e.Fori(0, CH // 2) as i:
                    for j in range(2):
                        p = i * 2 + j
                        e.wait_ge(sem("q_ev"), p * 3 + 3)
                        e.tensor_copy(qTs[:, bass.ds(p, 1), :], qb[j][:, SEQ:TOK].rearrange("p (a n) -> p a n", a=1)).then_inc(sem("qs_cp"), 1)
                        e.wait_ge(sem("k_ev"), p * 3 + 3)
                        e.tensor_copy(kTs[:, bass.ds(p, 1), :], kb[j][:, SEQ:TOK].rearrange("p (a n) -> p a n", a=1)).then_inc(sem("qs_cp"), 1)
                e.wait_ge(sem("ot_ev"), CH * 8)
                e.wait_ge(sem("k_out"), CH * 32)
                for j in range(2):
                    e.memset(qbd[j], 0.0).then_inc(sem("qbd_zero"), 1)
                e.wait_ge(sem("qbd_zero"), 2)
                e.wait_ge(sem("qs_cp"), CH * 2)
                with e.Fori(0, DB // 2) as i:
                    for j in range(2):
                        b = i * 2 + j
                        e.wait_ge(sem(f"sqk{j}"), i * 2)
                        cols = bass.ds(b * DS, DS)
                        e.wait_ge(sem(f"qbd{1 - j}"), (i + j) * 3)
                        e.tensor_copy(qbd[j][0:HD, :, 0:DS], qTs[0:HD, :, cols]).then_inc(sem(f"qbd{j}"), 1)
                        e.tensor_copy(qbd[j][HD:P, :, DS:2 * DS], qTs[HD:P, :, cols]).then_inc(sem(f"qbd{j}"), 1)
                        e.wait_ge(sem(f"qbd{j}"), i * 3 + 2)
                        e.tensor_copy(kcT[j][:, :, PAST:LK], kTs[:, :, cols]).then_inc(sem(f"qbd{j}"), 1)
                e.wait_ge(sem("so_A"), DB)
                e.wait_ge(sem("so_D"), DB)
                for j in range(2):
                    e.memset(bw[j], 0.0).then_inc(sem("bw_zero"), 1)
                    e.memset(xbuf[j][:, 0:3], 0.0).then_inc(sem("bw_zero2"), 1)
                def pads(i, j):
                    m = i * 2 + j
                    e.wait_ge(sem(f"conv{j}"), i)
                    e.tensor_copy(xbs[j][:, :, 0:3], pT[:, bass.ds(m, 1), R_CV:NR].rearrange("p a (b k) -> p (a b) k", b=DB)).then_inc(sem(f"xpad{j}"), 1)
                    e.wait_ge(sem(f"xb_ev{j}"), i * 4 + 4)
                    e.wait_ge(sem(f"xpad{j}"), i + 1)
                    e.tensor_copy(hc[:, bass.ds(m, 1), 9:12], xbuf[j][:, SEQ:SEQ + 3].rearrange("p (a n) -> p a n", a=1)).then_inc(sem(f"tails{j}"), 1)
                    e.wait_ge(sem(f"tails{j}"), i * 2 + 1)
                    e.tensor_copy(hc[:, bass.ds(m, 1), 12:36].rearrange("p a (b k) -> p (a b) k", b=DB), xbs[j][:, :, DS:DS + 3]).then_inc(sem(f"tails{j}"), 1)
                    e.wait_ge(sem(f"tails{j}"), i * 2 + 2)

                def states(i, j):
                    m = i * 2 + j
                    e.wait_ge(sem("scan"), m + 1)
                    e.tensor_copy(hc[:, bass.ds(m, 1), 0:1], hb[:, SEQ - 1:SEQ].rearrange("p (a n) -> p a n", a=1)).then_inc(sem("h_cp"), 1)
                    e.wait_ge(sem("h_cp"), m * 2 + 1)
                    e.tensor_copy(hc[:, bass.ds(m, 1), 1:9], hb[:, SEQ:TOK].rearrange("p (a b t) -> p a b t", a=1, b=DB)[:, :, :, DS - 1]).then_inc(sem("h_cp"), 1)
                    e.wait_ge(sem("h_cp"), m * 2 + 2)
                pads(0, 0)
                with e.Fori(0, CH // 2 - 1) as i:
                    pads(i, 1)
                    states(i, 0)
                    pads(i + 1, 0)
                    states(i, 1)
                pads(CH // 2 - 1, 1)
                states(CH // 2 - 1, 0)
                states(CH // 2 - 1, 1)
                for j in range(2):
                    e.wait_ge(sem(f"y_made{j}"), CH // 2)
                e.wait_ge(sem("h_cp"), 2 * CH)
                for j in range(2):
                    e.wait_ge(sem(f"tails{j}"), CH)
                with e.Fori(0, CH // 2) as i:
                    for j in range(2):
                        for n in range(G3):
                            s, k = (3 * j + n) % 2, (3 * j + n) // 2
                            e.wait_ge(sem(f"mixd{s}"), i * 3 + k + 1)
                            e.tensor_tensor(mixT[:, bass.ds(i * 2 + j, 1), n * NG:(n + 1) * NG], tm[s][0].rearrange("p (a n) -> p a n", a=1),
                                            tm[s][1].rearrange("p (a n) -> p a n", a=1), ALU.add).then_inc(sem(f"mixa{s}"), 1)

            @block.scalar
            def _(e):
                count = e.alloc_register("count")
                def put_q(i, j, n):
                    e.wait_ge(sem("qg_mm"), (i * 2 + j) * 3 + n + 1)
                    act(qb[j][:, n * NG:(n + 1) * NG], PS[:, 1 + 2 * n, 0:NG], ACT.Copy, scale=-(HD ** -0.5)).then_inc(sem("q_ev"), 1)

                def pair(i, j, more):
                    p = i * 2 + j
                    following = (i, 1) if j == 0 else (i + 1, 0)
                    e.wait_ge(sem("kt_ps"), p * 3 + 1)
                    e.wait_ge(sem("k_out"), p * 32)
                    act(kst[:, 0:4, :], PS[:, 4, :].rearrange("p (t n) -> p t n", t=4), ACT.Copy).then_inc(sem("kst_A"), 1)
                    e.wait_ge(sem("kt_ps"), p * 3 + 3)
                    act(kst[:, 8, :], PS[:, 7, 0:P], ACT.Copy).then_inc(sem("kst_A"), 1)

                    def norm(u):
                        k, hh = u // 2, u % 2
                        e.wait_ge(sem("recip"), p * 16 + u + 1)
                        e.wait_ge(sem("pv_mm"), p * 16 + u + 1)
                        if k >= 2:
                            e.wait_ge(sem("ot_mm"), p * 8 + k - 1)
                        act(ot[k % 2][:, hh * HD:(hh + 1) * HD], PS[:, 6, (u % 4) * HD:(u % 4 + 1) * HD], ACT.Copy, scale=rl[:, u:u + 1]).then_inc(sem("norm"), 1)
                    for u in range(16):
                        n = (8 - u // 2) * P
                        e.wait_ge(sem("ttr"), p * 16 + u + 1)
                        act(sP[u % 3][:, 0:n], sP[u % 3][:, 0:n], ACT.Exp, scale=-1.0, bias=mn[:, u:u + 1], accum_out=ls[:, u:u + 1]).then_inc(sem("exp"), 1)
                        if u >= 1 and 7 - (u - 1) // 2 >= 4:
                            m = (8 - (u - 1) // 2) * P - 512
                            e.wait_ge(sem("t1_mm"), p * 8 + u)
                            if u >= 3:
                                e.wait_ge(sem("pv_mm"), p * 16 + u - 2)
                            act(PTb[(u - 1) % 2][:, 512:512 + m], PS[:, 5, 0:m], ACT.Copy).then_inc(sem("evB"), 1)
                        if u >= 2:
                            norm(u - 2)
                        if more and 11 <= u < 14:
                            if u == 11:
                                e.wait_ge(sem("qs_cp"), p * 2)
                            put_q(*following, u - 11)
                    norm(14)
                    norm(15)
                for n in range(G3):
                    put_q(0, 0, n)
                with e.Fori(0, CH // 2 - 1) as i:
                    pair(i, 0, True)
                    pair(i, 1, True)
                pair(CH // 2 - 1, 0, True)
                pair(CH // 2 - 1, 1, False)

                e.wait_ge(sem("qs_cp"), CH * 2)

                def put_keys(i, j):
                    e.wait_ge(sem("kc_ps"), (i * 2 + j) * 2 + 1)
                    act(kcT[j][:, 0:4, 0:PAST], banks(0, 2).rearrange("p (c n) -> p c n", c=4), ACT.Copy).then_inc(sem("kc_A"), 1)

                def exps(i, j):
                    for g in range(2):
                        e.wait_ge(sem("s_ttr"), (i * 2 + j) * 2 + g + 1)
                        act(sS[j][:, g, :], sS[j][:, g, :], ACT.Exp, scale=-1.0, bias=mn[:, 2 * j + g:2 * j + g + 1],
                            accum_out=ls[:, 2 * j + g:2 * j + g + 1]).then_inc(sem("s_exp"), 1)

                def put_o(i, j):
                    b = i * 2 + j
                    e.reg_mov(count, b + 1)
                    e.wait_ge(sem("ot_ev"), CH * 8)
                    e.wait_ge(sem("ot2_mm"), count)
                    act(oaT[0:HD, :, bass.ds(b * DS + SEQ, DS)], PS[0:HD, 7, 256:512].rearrange("p (c n) -> p c n", c=CH)[:, :, 0:DS], ACT.Copy).then_inc(sem("so_A"), 1)

                def batch(i, j, before, nxt):
                    b = i * 2 + j
                    if nxt:
                        put_keys(*nxt)
                    for g in range(2):
                        e.wait_ge(sem("s_tp"), b * 2 + g + 1)
                        act(PTs[j][:, g, 0:2, :], PS[:, 6, 0:2 * P].rearrange("p (k n) -> p k n", k=2), ACT.Copy).then_inc(sem("s_ptA"), 1)
                    if before:
                        put_o(*before)
                    if nxt:
                        exps(*nxt)
                    e.wait_ge(sem(f"spv{j}"), i + 1)
                    if before:
                        e.wait_ge(sem("so_D"), b)
                    act(osb[j].rearrange("p g n -> p (g n)"), PS[:, 7, 0:256], ACT.Copy).then_inc(sem("o_ev"), 1)
                put_keys(0, 0)
                exps(0, 0)
                batch(0, 0, None, (0, 1))
                with e.Fori(0, DB // 2 - 1) as i:
                    batch(i, 1, (i, 0), (i + 1, 0))
                    batch(i + 1, 0, (i, 1), (i + 1, 1))
                batch(DB // 2 - 1, 1, (DB // 2 - 1, 0), None)
                put_o(DB // 2 - 1, 1)

                def inputs(i, j):
                    m = i * 2 + j
                    e.wait_ge(sem(f"conv{j}"), i)
                    e.wait_ge(sem(f"tails{j}"), i * 2)
                    for n in range(G3):
                        e.wait_ge(sem("xb_mm"), m * 3 + n + 1)
                        if n < 2:
                            act(xbuf[j][:, 3 + n * NG:3 + (n + 1) * NG], PS[:, n, 0:NG], ACT.Copy).then_inc(sem(f"xb_ev{j}"), 1)
                        else:
                            act(xbuf[j][:, 3 + n * NG:3 + SEQ], PS[:, n, 0:SEQ - n * NG], ACT.Copy).then_inc(sem(f"xb_ev{j}"), 1)
                            act(xbs[j][:, :, 3:3 + DS], PS[:, n, SEQ - n * NG:NG].rearrange("p (b t) -> p b t", b=DB), ACT.Copy).then_inc(sem(f"xb_ev{j}"), 1)
                    e.wait_ge(sem(f"y_made{j}"), i)
                    for n in range(G3):
                        if n < 2:
                            e.wait_ge(sem("gb_mm"), m * 2 + n + 1)
                        else:
                            e.wait_ge(sem(f"gb_done{j}"), i + 1)
                        act(gel[j][:, n * NG:(n + 1) * NG], PS[:, 3 + n, 0:NG], ACT.Gelu_apprx_tanh).then_inc(sem(f"gb_ev{j}"), 1)

                def gates(i, j):
                    m = i * 2 + j
                    e.wait_ge(sem("scan"), m)
                    for n in range(G3):
                        e.reg_mov(count, m * 2 + n + 1 if n < 2 else i + 1)
                        e.wait_ge(sem("bw_zero2"), 2)
                        e.wait_ge(sem("ri_mm" if n < 2 else f"ri_done{j}"), count)
                        cols = slice(n * NG, (n + 1) * NG)
                        act(rr[:, cols], PS[:, 6, 0:NG], ACT.Sigmoid, bias=pT[:, bass.ds(m, 1), R_BR]).then_inc(sem("sig"), 1)
                        act(ii[:, cols], PS[:, 7, 0:NG], ACT.Sigmoid, bias=pT[:, bass.ds(m, 1), R_BI]).then_inc(sem("sig"), 1)
                    e.wait_ge(sem("bw_zero2"), 2)
                    e.wait_ge(sem("sig"), m * 6 + 6)
                    act(rr, rr, ACT.Tanh, scale=sp4[:, bass.ds(m, 1)]).then_inc(sem("tanh"), 1)
                    e.wait_ge(sem("Rs"), m + 1)
                    act(rr, rr, ACT.Sqrt, scale=4.0).then_inc(sem("root"), 1)
                e.wait_ge(sem("bw_zero2"), 2)
                inputs(0, 0)
                with e.Fori(0, CH // 2 - 1) as i:
                    inputs(i, 1)
                    gates(i, 0)
                    inputs(i + 1, 0)
                    gates(i, 1)
                inputs(CH // 2 - 1, 1)
                gates(CH // 2 - 1, 0)
                gates(CH // 2 - 1, 1)
                e.wait_ge(sem("hc_ps"), 1)
                act(hrow, banks(6, 2, 36), ACT.Copy).then_inc(sem("hrow"), 1)
                e.wait_ge(sem("hrow"), 1)
                e.dma_start(h_p[0], hrow[0:1, :]).then_inc(sem("hc_out"), 16)
                e.dma_start(h_s[0], hrow[1:9, :]).then_inc(sem("hc_out"), 16)
                e.dma_start(cv_p[0, 0], hrow[9:12, :]).then_inc(sem("hc_out"), 16)
                e.dma_start(cv_s[0].rearrange("b k d -> (b k) d"), hrow[12:36, :]).then_inc(sem("hc_out"), 16)
                e.wait_ge(sem("hc_out"), 64)

                with e.Fori(0, CH // 2) as i:
                    for j in range(2):
                        m = i * 2 + j
                        for n in range(G3):
                            s, k = (3 * j + n) % 2, (3 * j + n) // 2
                            e.wait_ge(sem(f"mixd{s}"), i * 3 + k)
                            for q in range(2):
                                e.reg_mov(count, (i * 6 + 3 * j + n) * 2 + q + 1)
                                e.wait_ge(sem("hc_out"), 64)
                                e.wait_ge(sem("mg_mm"), count)
                                act(sg[s][q], PS[:, 4 * s + 2 * q, 0:NG], ACT.Sigmoid, bias=pT[:, bass.ds(m, 1), R_BG + q]).then_inc(sem("sg"), 1)

            @block.vector
            def _(e):
                count, count2 = e.alloc_register("count"), e.alloc_register("count2")
                def put_k(i, j, n):
                    e.wait_ge(sem("kg_mm"), (i * 2 + j) * 3 + n + 1)
                    copy(kb[j][:, n * NG:(n + 1) * NG], PS[:, 1 + 2 * n, 0:NG]).then_inc(sem("k_ev"), 1)

                def pair(i, j, more):
                    p = i * 2 + j
                    following = (i, 1) if j == 0 else (i + 1, 0)
                    e.wait_ge(sem("kt_ps"), p * 3 + 2)
                    e.wait_ge(sem("k_out"), p * 32)
                    copy(kst[:, 4:8, :], PS[:, 5, :].rearrange("p (t n) -> p t n", t=4)).then_inc(sem("kst_D"), 1)
                    e.wait_ge(sem(f"Bt_in{j}"), i * 32 + 32)

                    def recip_and_turned(u):
                        m = min(8 - u // 2, 4) * P
                        e.wait_ge(sem("exp"), p * 16 + u + 1)
                        nc.vector.reciprocal(rl[:, u:u + 1], ls[:, u:u + 1]).then_inc(sem("recip"), 1)
                        e.wait_ge(sem("t0_mm"), p * 16 + u + 1)
                        if u >= 2:
                            e.wait_ge(sem("pv_mm"), p * 16 + u - 1)
                        copy(PTb[u % 2][:, 0:m], PS[:, 4, 0:m]).then_inc(sem("evA"), 1)

                    def put_o(k):
                        e.wait_ge(sem("ot_mm"), p * 8 + k + 1)
                        copy(oaT[:, bass.ds(p, 1), (7 - k) * P:(8 - k) * P], PS[:, 7, (k % 4) * P:(k % 4 + 1) * P].rearrange("p (a n) -> p a n", a=1)).then_inc(sem("ot_ev"), 1)
                    for u in range(16):
                        r, hh = 7 - u // 2, u % 2
                        n = (r + 1) * P
                        if u < 2:
                            e.wait_ge(sem("kst_D"), p + 1)
                        else:
                            e.wait_ge(sem("ttr"), p * 16 + u - 1)
                        tt(Bt[j][:, hh, r * P:n], Bt[j][:, hh, r * P:n], causal[:], ALU.add).then_inc(sem("mask"), 1)
                        if u >= 3:
                            e.wait_ge(sem("t0_mm"), p * 16 + u - 2)
                        if 3 <= u < 11:
                            e.wait_ge(sem("t1_mm"), p * 8 + u - 2)
                        e.reg_mov(count, p * 16 + u + 1)
                        e.wait_ge(sem(f"Bt_in{j}"), 32)
                        e.wait_ge(sem("mask"), count)
                        e.wait_ge(sem("s_mm"), count)
                        nc.vector.tensor_tensor_reduce(out=sP[u % 3][:, 0:n], in0=banks(2 * (u % 2), 2)[:, 0:n], in1=Bt[j][:, hh, 0:n], scale=1.0, scalar=BIG,
                                                       op0=ALU.add, op1=ALU.min, accum_out=mn[:, u:u + 1]).then_inc(sem("ttr"), 1)
                        if u >= 1:
                            recip_and_turned(u - 1)
                        if u >= 4 and u % 2 == 0:
                            put_o((u - 4) // 2)
                        if more and u >= 14:
                            if u == 14:
                                e.wait_ge(sem("qs_cp"), p * 2)
                            put_k(*following, u - 14)
                    recip_and_turned(15)
                    if more:
                        put_k(*following, 2)
                    put_o(6)
                    put_o(7)
                for n in range(G3):
                    put_k(0, 0, n)
                with e.Fori(0, CH // 2 - 1) as i:
                    pair(i, 0, True)
                    pair(i, 1, True)
                pair(CH // 2 - 1, 0, True)
                pair(CH // 2 - 1, 1, False)

                e.wait_ge(sem("c16_in"), 16 * (P // DS))

                def put_keys(i, j):
                    b = i * 2 + j
                    e.wait_ge(sem("kc_ps"), b * 2 + 2)
                    copy(kcT[j][:, 4:8, 0:PAST], banks(2, 2).rearrange("p (c n) -> p c n", c=4)).then_inc(sem("kc_D"), 1)
                    e.wait_ge(sem(f"sB_in{j}"), i * 16 + 16)
                    tt(Bs[j][:, :, PAST:LK], Bs[j][:, :, PAST:LK], causal16[:].rearrange("p (a n) -> p a n", a=1).broadcast_to([P, 2, DS]), ALU.add).then_inc(sem("s_mask"), 1)

                def scores(i, j):
                    for g in range(2):
                        q = 2 * j + g
                        e.reg_mov(count, i * 2 + j + 1)
                        e.reg_mov(count2, i * 2 + g + 1)
                        e.wait_ge(sem("c16_in"), 16 * (P // DS))
                        e.wait_ge(sem("s_mask"), count)
                        e.wait_ge(sem(f"sqk{j}"), count2)
                        nc.vector.tensor_tensor_reduce(out=sS[j][:, g, :], in0=PS[:, 4 + g, 0:LK], in1=Bs[j][:, g, :], scale=1.0, scalar=BIG,
                                                       op0=ALU.add, op1=ALU.min, accum_out=mn[:, q:q + 1]).then_inc(sem("s_ttr"), 1)

                def put_probs(b, j, g):
                    e.wait_ge(sem("s_ptA"), b * 2 + g + 1)
                    e.wait_ge(sem("s_tp"), b * 2 + g + 1)
                    copy(PTs[j][0:DS, g, 2, :], PS[0:DS, 6, 2 * P:3 * P]).then_inc(sem("s_ptD"), 1)

                def put_o(i, j):
                    b = i * 2 + j
                    e.wait_ge(sem("ot2_mm"), b + 1)
                    copy(oaT[HD:P, :, bass.ds(b * DS + SEQ, DS)], PS[HD:P, 7, 256:512].rearrange("p (c n) -> p c n", c=CH)[:, :, DS:2 * DS]).then_inc(sem("so_D"), 1)

                def batch(i, j, before, nxt):
                    b = i * 2 + j
                    for g in range(2):
                        q = 2 * j + g
                        e.wait_ge(sem("s_exp"), b * 2 + g + 1)
                        nc.vector.reciprocal(rl[:, q:q + 1], ls[:, q:q + 1]).then_inc(sem("s_rl"), 1)
                        e.wait_ge(sem("s_rl"), b * 2 + g + 1)
                        ts(sS[j][:, g, :], sS[j][:, g, :], rl[:, q:q + 1], None, ALU.mult).then_inc(sem("s_pn"), 1)
                    if nxt:
                        put_keys(*nxt)
                    put_probs(b, j, 0)
                    if nxt:
                        scores(*nxt)
                    put_probs(b, j, 1)
                    if before:
                        put_o(*before)
                put_keys(0, 0)
                scores(0, 0)
                batch(0, 0, None, (0, 1))
                with e.Fori(0, DB // 2 - 1) as i:
                    batch(i, 1, (i, 0), (i + 1, 0))
                    batch(i + 1, 0, (i, 1), (i + 1, 1))
                batch(DB // 2 - 1, 1, (DB // 2 - 1, 0), None)
                put_o(DB // 2 - 1, 1)

                st = Steps(e, sem("dve_rnn"))

                def conv(i, j):
                    m = i * 2 + j
                    e.wait_ge(sem(f"xb_ev{j}"), i * 4 + 4)
                    e.wait_ge(sem(f"xpad{j}"), i + 1)
                    par = lambda r: pT[:, bass.ds(m, 1), r]
                    xcs = xc[j][:, SEQ:TOK].rearrange("p (b t) -> p b t", b=DB)
                    for k in range(4):
                        if k:
                            st.wait()
                        for dst, src in ((xc[j][:, 0:SEQ], xbuf[j][:, k:k + SEQ]), (xcs, xbs[j][:, :, k:k + DS])):
                            if k == 0:
                                st.did(ts(dst, src, par(R_CW), par(R_CB), ALU.mult, ALU.add))
                            elif k < 3 or dst is not xcs:
                                st.did(stt(out=dst, in0=src, scalar=par(R_CW + k), in1=dst, op0=ALU.mult, op1=ALU.add))
                            else:
                                stt(out=dst, in0=src, scalar=par(R_CW + k), in1=dst, op0=ALU.mult, op1=ALU.add).then_inc(sem(f"conv{j}"), 1)
                CONV = 7

                def recur(i, j):
                    m = i * 2 + j
                    e.wait_ge(sem("tanh"), m + 1)
                    ts(Rr, rr, 1.0, None, ALU.add).then_inc(sem("Rs"), 1)
                    e.wait_ge(sem("Rs"), m + 1)
                    st.did(nc.vector.reciprocal(Rr, Rr))
                    st.did(tt(ii, ii, xc[j], ALU.mult))
                    st.wait()
                    st.did(tt(ii, ii, Rr, ALU.mult))
                    st.wait()
                    st.did(ts(Rr, Rr, 2.0, -1.0, ALU.mult, ALU.add))
                    e.wait_ge(sem("root"), m + 1)
                    st.wait()
                    st.did(tt(ii, ii, rr, ALU.mult))
                    st.wait()
                    a0 = Rr[:, SEQ:TOK].rearrange("p (b t) -> p b t", b=DB)[:, :, 0]
                    b0 = ii[:, SEQ:TOK].rearrange("p (b t) -> p b t", b=DB)[:, :, 0]
                    st.did(tt(t8[:], a0, pT[:, bass.ds(m, 1), R_H0:R_H0 + DB].rearrange("p a b -> p (a b)"), ALU.mult))
                    st.wait()
                    st.did(tt(b0, b0, t8[:], ALU.add))
                    st.did(nc.vector.memset(a0, 0.0))
                    st.wait()
                    e.wait_ge(sem("h_cp"), m * 2)
                    nc.vector.tensor_tensor_scan(hb, Rr, ii, 0.0, ALU.mult, ALU.add).then_inc(sem("scan"), 1)
                    e.wait_ge(sem(f"gb_ev{j}"), i * 3 + 3)
                    e.wait_ge(sem("scan"), m + 1)
                    tt(obT[:, bass.ds(m, 1), :], hb.rearrange("p (a n) -> p a n", a=1), gel[j].rearrange("p (a n) -> p a n", a=1), ALU.mult).then_inc(sem(f"y_made{j}"), 1)
                RECUR = 8
                PER = 2 * (CONV + RECUR)
                conv(0, 0)
                with e.Fori(0, CH // 2 - 1) as i:
                    st.base, st.n = i * PER + CONV, 0
                    conv(i, 1)
                    recur(i, 0)
                    conv(i + 1, 0)
                    recur(i, 1)
                st.base, st.n = (CH // 2 - 1) * PER + CONV, 0
                conv(CH // 2 - 1, 1)
                recur(CH // 2 - 1, 0)
                recur(CH // 2 - 1, 1)

                e.wait_ge(sem("hrow"), 1)
                e.wait_ge(sem("hc_out"), 64)
                with e.Fori(0, CH // 2) as i:
                    for j in range(2):
                        for n in range(G3):
                            s, k = (3 * j + n) % 2, (3 * j + n) // 2
                            e.wait_ge(sem(f"mixa{s}"), i * 3 + k)
                            for q in range(2):
                                e.wait_ge(sem("sg"), (i * 6 + 3 * j + n) * 2 + q + 1)
                                e.wait_ge(sem(f"mp_mm{j}"), i * 6 + n * 2 + q + 1)
                                tt(tm[s][q], PS[:, 4 * s + 2 * q + 1, 0:NG], sg[s][q], ALU.mult).then_inc(sem(f"mixd{s}" if q else "mixp"), 1)

            @block.tensor
            def _(e):
                def project(i, j, g):
                    p = i * 2 + j
                    n = g % G3
                    if g == 0:
                        e.wait_ge(sem("qk_w"), p * 32 + 32)
                    if g >= G3:
                        e.wait_ge(sem("q_ev"), p * 3 + n + 1)
                    product(PS[:, 1 + 2 * n, 0:NG], lambda c: (wk if g >= G3 else wq)[:, c, :],
                            lambda c: hT[:, c, n * NG:(n + 1) * NG]).then_inc(sem("kg_mm" if g >= G3 else "qg_mm"), 1)

                def pair(i, j, more):
                    p = i * 2 + j
                    e.wait_ge(sem("k_ev"), p * 3 + 3)
                    e.wait_ge(sem("evA"), p * 16)
                    e.wait_ge(sem("evB"), p * 8)
                    e.wait_ge(sem("ot_ev"), p * 8)
                    for t in range(NT):
                        last = tr(PS[:, (4, 5, 7)[t // 4], (t % 4) * P:(t % 4 + 1) * P], kb[j][:, t * P:(t + 1) * P], ident[:])
                        if t in (3, 7, 8):
                            last.then_inc(sem("kt_ps"), 1)
                    e.wait_ge(sem("q_ev"), p * 3 + 3)

                    def scores(u):
                        k, hh = u // 2, u % 2
                        i, rows_ = 7 - k, slice(hh * HD, (hh + 1) * HD)
                        if u >= 2:
                            e.wait_ge(sem("ttr"), p * 16 + u - 1)
                        n = (i + 1) * P
                        for c0 in range(0, n, 512):
                            c1 = min(n, c0 + 512)
                            last = mm(PS[:, 2 * (u % 2) + c0 // 512, 0:c1 - c0], qb[j][rows_, i * P:(i + 1) * P], kb[j][rows_, c0:c1], start=True, stop=True)
                        last.then_inc(sem("s_mm"), 1)

                    def turn_probs(u):
                        i = 7 - u // 2
                        e.wait_ge(sem("exp"), p * 16 + u + 1)
                        e.wait_ge(sem("evA"), p * 16 + u)
                        if u == 0:
                            e.wait_ge(sem("kst_A"), p * 2 + 1)
                            e.wait_ge(sem("kst_D"), p + 1)
                        elif i >= 4:
                            e.wait_ge(sem("evB"), p * 8 + u)
                        for b in range(i + 1):
                            last = tr(PS[:, 4 + b // 4, (b % 4) * P:(b % 4 + 1) * P], sP[u % 3][:, b * P:(b + 1) * P], ident[:])
                            if b == min(i, 3):
                                last.then_inc(sem("t0_mm"), 1)
                        if i >= 4:
                            last.then_inc(sem("t1_mm"), 1)

                    def values(u):
                        k, hh = u // 2, u % 2
                        i = 7 - k
                        e.wait_ge(sem("evA"), p * 16 + u + 1)
                        if i >= 4:
                            e.wait_ge(sem("evB"), p * 8 + u + 1)
                        e.wait_ge(sem("norm"), p * 16 + u)
                        for b in range(i + 1):
                            last = mm(PS[:, 6, (u % 4) * HD:(u % 4 + 1) * HD], PTb[u % 2][:, b * P:(b + 1) * P],
                                      vtok[:, b, bass.ds(p * P + hh * HD, HD)], start=b == 0, stop=b == i)
                        last.then_inc(sem("pv_mm"), 1)

                    def turn_out(k):
                        e.wait_ge(sem("norm"), p * 16 + 2 * k + 2)
                        e.wait_ge(sem("ot_ev"), p * 8 + k)
                        if k == 0:
                            e.wait_ge(sem("kst_A"), p * 2 + 2)
                        tr(PS[:, 7, (k % 4) * P:(k % 4 + 1) * P], ot[k % 2], ident[:]).then_inc(sem("ot_mm"), 1)

                    following = (i, 1) if j == 0 else (i + 1, 0)
                    scores(0)
                    scores(1)
                    for u in range(16):
                        turn_probs(u)
                        if u + 2 < 16:
                            scores(u + 2)
                        if u >= 1:
                            values(u - 1)
                        if u >= 3 and u % 2 == 1:
                            turn_out((u - 3) // 2)
                        if more and u >= 10:
                            project(*following, u - 10)
                    values(15)
                    turn_out(7)
                for g in range(2 * G3):
                    project(0, 0, g)
                with e.Fori(0, CH // 2 - 1) as i:
                    pair(i, 0, True)
                    pair(i, 1, True)
                pair(CH // 2 - 1, 0, True)
                pair(CH // 2 - 1, 1, False)

                e.wait_ge(sem("ot_ev"), CH * 8)
                e.wait_ge(sem("norm"), CH * 16)

                def turn_keys(i, j):
                    e.wait_ge(sem(f"sk_in{j}"), i * 16 + 16)
                    e.wait_ge(sem("kc_A"), i * 2 + j)
                    e.wait_ge(sem("kc_D"), i * 2 + j)
                    for c in range(CH):
                        for k in range(2):
                            o_ = (c % 2) * PAST + k * P
                            last = tr(PS[:, c // 2, o_:o_ + P], kc[j][:, k, c * P:(c + 1) * P], ident[:])
                        if c in (3, 7):
                            last.then_inc(sem("kc_ps"), 1)

                def sample_scores(i, j):
                    e.wait_ge(sem("kc_A"), i * 2 + j + 1)
                    e.wait_ge(sem("kc_D"), i * 2 + j + 1)
                    e.wait_ge(sem(f"qbd{j}"), i * 3 + 3)
                    for g in range(2):
                        e.wait_ge(sem("s_ttr"), i * 4 + j * 2 + g)
                        for q in range(4):
                            last = mm(PS[32 * q:32 * q + 32, 4 + g, 0:LK], qbd[j][:, 4 * g + q, :], kcT[j][:, 4 * g + q, :], start=True, stop=True)
                        last.then_inc(sem(f"sqk{j}"), 1)

                def turn_sample_probs(i, j, g):
                    e.wait_ge(sem("s_pn"), i * 4 + j * 2 + g + 1)
                    e.wait_ge(sem("s_ptA"), i * 4 + j * 2 + g)
                    e.wait_ge(sem("s_ptD"), i * 4 + j * 2 + g)
                    for k in range(2):
                        tr(PS[:, 6, k * P:(k + 1) * P], sS[j][:, g, k * P:(k + 1) * P], ident[:])
                    tr(PS[0:DS, 6, 2 * P:3 * P], sS[j][:, g, PAST:LK], ident[:]).then_inc(sem("s_tp"), 1)

                def turn_values(i, j):
                    e.wait_ge(sem("o_ev"), i * 2 + j + 1)
                    e.wait_ge(sem("so_A"), i * 2 + j)
                    e.wait_ge(sem("so_D"), i * 2 + j)
                    for g in range(2):
                        last = tr(PS[:, 7, 256 + g * P:256 + (g + 1) * P], osb[j][:, g, :], ident[:])
                    last.then_inc(sem("ot2_mm"), 1)

                def batch(i, j, before, nxt):
                    if nxt:
                        turn_keys(*nxt)
                    turn_sample_probs(i, j, 0)
                    if before:
                        turn_values(*before)
                    if nxt:
                        sample_scores(*nxt)
                    turn_sample_probs(i, j, 1)
                    e.wait_ge(sem(f"sv_in{j}"), i * 32 + 32)
                    if before:
                        e.wait_ge(sem("so_A"), i * 2 + j)
                        e.wait_ge(sem("so_D"), i * 2 + j)
                    for g in range(2):
                        e.wait_ge(sem("s_ptA"), i * 4 + j * 2 + g + 1)
                        e.wait_ge(sem("s_ptD"), i * 4 + j * 2 + g + 1)
                        for q in range(4):
                            c, qs = 4 * g + q, slice(q * 32, q * 32 + 32)
                            for k in range(2):
                                mm(PS[qs, 7, g * P:(g + 1) * P], PTs[j][:, g, k, qs], vc[j][:, k, c * P:(c + 1) * P], start=k == 0, stop=False)
                            last = mm(PS[qs, 7, g * P:(g + 1) * P], PTs[j][0:DS, g, 2, qs], v16[j][:, c * P:(c + 1) * P], start=False, stop=True)
                    last.then_inc(sem(f"spv{j}"), 1)
                turn_keys(0, 0)
                sample_scores(0, 0)
                batch(0, 0, None, (0, 1))
                with e.Fori(0, DB // 2 - 1) as i:
                    batch(i, 1, (i, 0), (i + 1, 0))
                    batch(i + 1, 0, (i, 1), (i + 1, 1))
                batch(DB // 2 - 1, 1, (DB // 2 - 1, 0), None)
                turn_values(DB // 2 - 1, 1)

                def inputs(i, j):
                    m = i * 2 + j
                    e.wait_ge(sem(f"wx_in{j}"), i * 32 + 32)
                    if j == 0:
                        e.wait_ge(sem("xb_ev1"), i * 4)
                        e.wait_ge(sem("gb_ev1"), i * 3)
                    else:
                        e.wait_ge(sem("xb_ev0"), i * 4 + 4)
                        e.wait_ge(sem("gb_ev0"), i * 3 + 3)
                    for k, s in enumerate(("xb_mm", "gb_mm")):
                        for n in range(G3):
                            last = product(PS[:, 3 * k + n, 0:NG], lambda c: wx[j][k][:, c, :], lambda c: hT[:, c, n * NG:(n + 1) * NG])
                            last.then_inc(sem(f"gb_done{j}" if k and n == G3 - 1 else s), 1)

                def gates(i, j):
                    m = i * 2 + j
                    e.wait_ge(sem(f"conv{j}"), i + 1)
                    e.wait_ge(sem(f"bw_in{j}"), i * 64 + 64)
                    for n in range(G3):
                        e.wait_ge(sem("sig"), m * 6 + n * 2)
                        mm(PS[:, 6, 0:NG], bw[j][:, 0, :], xc[j][:, n * NG:(n + 1) * NG], start=True, stop=True)
                        last = mm(PS[:, 7, 0:NG], bw[j][:, 1, :], xc[j][:, n * NG:(n + 1) * NG], start=True, stop=True)
                        last.then_inc(sem(f"ri_done{j}") if n == G3 - 1 else sem("ri_mm"), 1)
                e.wait_ge(sem("so_A"), DB)
                e.wait_ge(sem("so_D"), DB)
                inputs(0, 0)
                with e.Fori(0, CH // 2 - 1) as i:
                    inputs(i, 1)
                    gates(i, 0)
                    inputs(i + 1, 0)
                    gates(i, 1)
                inputs(CH // 2 - 1, 1)
                gates(CH // 2 - 1, 0)
                gates(CH // 2 - 1, 1)

                e.wait_ge(sem("h_cp"), 2 * CH)
                e.wait_ge(sem("sig"), 6 * CH)
                for j in range(2):
                    e.wait_ge(sem(f"tails{j}"), CH)
                for c in range(CH):
                    last = tr(PS[0:36, 6 + c // 4, (c % 4) * P:(c % 4 + 1) * P], hc[:, c, :], ident[:])
                last.then_inc(sem("hc_ps"), 1)
                e.wait_ge(sem("hrow"), 1)
                for j in range(2):
                    e.wait_ge(sem(f"y_made{j}"), CH // 2)
                with e.Fori(0, CH // 2) as i:
                    for j in range(2):
                        e.wait_ge(sem(f"wm_in{j}"), i * 64 + 64)
                        for n in range(G3):
                            s, k = (3 * j + n) % 2, (3 * j + n) // 2
                            e.wait_ge(sem(f"mixd{s}"), i * 3 + k)
                            cols = slice(n * NG, (n + 1) * NG)
                            for q, (w, src) in enumerate(((1, hT), (0, oaT), (3, hT), (2, obT))):
                                last = product(PS[:, 4 * s + q, 0:NG], lambda c: wm[j][w][:, c, :], lambda c: src[:, c, cols])
                                last.then_inc(sem(f"mp_mm{j}") if q % 2 else sem("mg_mm"), 1)
        clear_semaphores()

        with nc.Block() as block:

            @block.sync
            def _(e):
                for k in range(2):
                    e.dma_start(wo[k], w_out[:, :, 512 * k:512 * (k + 1)]).then_inc(sem("wo_in"), 16)
                mod_load(e, G1, 2, "g1_in")
                mod_load(e, A2, 4, "ab2_in")
                mod_load(e, B2, 3, "ab2_in")
                e.dma_start(N2, spread(a["norm2"])).then_inc(sem("ab2_in"), 16)
                e.dma_start(wr[:, :, 0:GR], a["w_rg"][0].rearrange("(c p) n -> p c n", p=P)).then_inc(sem("wr_in"), 16)
                e.dma_start(wr[:, :, GR:], a["w_re"][0].rearrange("(c p) n -> p c n", p=P)).then_inc(sem("wr_in"), 16)
                e.dma_start(br[:, 0:GR], spread(a["b_rg"])).then_inc(sem("wr_in"), 16)
                e.dma_start(br[:, GR:], spread(a["b_re"])).then_inc(sem("wr_in"), 16)
                with e.Fori(0, PT_ // 2) as i:
                    for j in range(2):
                        e.wait_ge(sem(f"x1_made{j}"), i)
                        e.dma_start(xo[j], xp[bass.ds(i * 256 + j * P, P), :]).then_inc(sem(f"xo_in{j}"), 16)
                e.wait_ge(sem("x1_made0"), PT_ // 2)
                e.dma_start(xo[0], xs).then_inc(sem("xo_in0"), 16)
                e.wait_ge(sem("h2_out0"), 16 * (PT_ // 2 + 1))
                e.wait_ge(sem("h2_out1"), 16 * (PT_ // 2))
                e.wait_ge(sem("meta"), 2)
                used = e.value_load(meta[0:1, SLOTS:SLOTS + 1], min_val=1, max_val=SLOTS)
                with e.Fori(0, SLOTS // 2) as i:
                    for j in range(2):
                        with e.If(i * 2 + j < used):
                            e.wait_ge(sem(f"eh3_{j}"), i)
                            ex_id = e.value_load(meta[0:1, bass.ds(i * 2 + j, 1)], min_val=0, max_val=NE - 1)
                            e.dma_start(w1b[j], w1[bass.ds(ex_id, 1)].rearrange("a (c p) f -> p (a c) f", p=P)).then_inc(sem(f"w1_in{j}"), 16)
                            e.dma_start(w3b[j], w3[bass.ds(ex_id, 1)].rearrange("a (c p) f -> p (a c) f", p=P)).then_inc(sem(f"w3_in{j}"), 16)
                            e.wait_ge(sem(f"ey_{j}"), i)
                            e.dma_start(w2b[j], w2[bass.ds(ex_id, 1)].rearrange("a (c p) d -> p (a c) d", p=P)).then_inc(sem(f"w2_in{j}"), 16)
                e.wait_ge(sem("e_all"), 1)
                mod_load(e, G2, 5, "g2_in")
                e.dma_start(NF, spread(a["norm_f"].rearrange("(a d) -> a d", a=1))).then_inc(sem("g2_in"), 16)
                with e.Fori(0, PT_ // 2) as i:
                    for j in range(2):
                        e.wait_ge(sem(f"o_made{j}"), i + 1)
                        e.dma_start(y_p[0, bass.ds(i * 256 + j * P, P), :], out_t[j]).then_inc(sem(f"o_out{j}"), 16)
                e.wait_ge(sem("o_made0"), PT_ // 2 + 1)
                e.dma_start(y_s.rearrange("b t d -> (b t) d"), out_t[0]).then_inc(sem("o_out0"), 16)
                e.wait_ge(sem("o_out0"), 16 * (PT_ // 2 + 1))
                e.wait_ge(sem("o_out1"), 16 * (PT_ // 2))

            @block.gpsimd
            def _(e):

                def stage(j, cols, n):
                    e.wait_ge(sem(f"out_mm{j}"), n)
                    e.tensor_copy(mt[j], mixT[:, :, cols]).then_inc(sem(f"mt{j}"), 1)

                def shift(j, k, n):
                    e.wait_ge(sem(f"h2_sc{j}"), n + 1)
                    e.tensor_tensor(h2[j], h2[j], B2[k], ALU.add).then_inc(sem(f"h2_made{j}"), 1)
                e.wait_ge(sem("ab2_in"), 2 * MOD_LOAD + 16)
                stage(0, bass.ds(0, P), 0)

                def turn(i, last):
                    stage(1, bass.ds(i * 256 + P, P), i)
                    shift(0, 0, i)
                    stage(0, bass.ds(i * 256 + 2 * P, P), i + 1)
                    shift(1, 0, i)
                    if last:
                        shift(0, 1, i + 1)
                with e.Fori(0, PT_ // 2 - 1) as i:
                    turn(i, False)
                turn(PT_ // 2 - 1, True)
                e.wait_ge(sem("out_mm0"), PT_ // 2 + 1)
                e.iota(iotaf, [[1, P]], base=0, channel_multiplier=0, allow_small_or_imprecise_dtypes=True).then_inc(sem("iotas"), 1)
                e.iota(thr, [[P, 9]], base=0, channel_multiplier=0, allow_small_or_imprecise_dtypes=True).then_inc(sem("iotas"), 1)
                e.iota(tokf, [[P, NT]], base=0, channel_multiplier=1, allow_small_or_imprecise_dtypes=True).then_inc(sem("iotas"), 1)
                e.memset(g8, -BIG).then_inc(sem("iotas"), 1)
                count = e.alloc_register("count")
                e.wait_ge(sem("meta"), 2)
                e.wait_ge(sem("h2_out0"), 16 * (PT_ // 2 + 1))
                e.wait_ge(sem("h2_out1"), 16 * (PT_ // 2))

                def gather(col, j):
                    e.tensor_copy(gidx[j][:], rows[:, col]).then_inc(sem(f"gidx{j}"), 1)

                def gather2(j, n):
                    e.reg_mov(count, n)
                    e.wait_ge(sem("meta"), 2)
                    e.wait_ge(sem(f"gidx{j}"), count)
                    e.indirect_dma_start(out=xg[j], out_offset=None, in_=h2_d, in_offset=bass.IndirectOffsetOnAxis(ap=gidx[j][:], axis=0)).then_inc(sem(f"xg_in{j}"), 16)
                gather(bass.ds(0, 1), 0)
                gather2(0, 1)
                used = e.value_load(meta[0:1, SLOTS:SLOTS + 1], min_val=1, max_val=SLOTS)
                with e.Fori(0, SLOTS // 2) as i:
                    for j in range(2):
                        with e.If(i * 2 + j < used):
                            e.wait_ge(sem("tx_mm"), i * 2 + j)
                            gather(bass.ds(i * 2 + j + 1, 1), 1 - j)
                            gather2(1 - j, i + 1 + j)
                e.wait_ge(sem("e_all"), 1)

                def pick(col, j, n):
                    e.wait_ge(sem(f"c_used{j}"), n)
                    for k in range(2):
                        e.tensor_copy(cidx[k][j][:], dest[:, k, col]).then_inc(sem(f"cidx{j}"), 1)
                    e.reg_mov(count, n * 2 + 2)
                    e.wait_ge(sem("e_all"), 1)
                    e.wait_ge(sem(f"cidx{j}"), count)
                    for k, y in enumerate((y0, y1)):
                        e.indirect_dma_start(out=y[j], out_offset=None, in_=yb_d, in_offset=bass.IndirectOffsetOnAxis(ap=cidx[k][j][:], axis=0)).then_inc(sem(f"y_in{j}"), 16)
                with e.Fori(0, PT_ // 2) as i:
                    for j in range(2):
                        pick(bass.ds(i * 2 + j, 1), j, i)
                pick(bass.ds(PT_, 1), 0, PT_ // 2)

            @block.scalar
            def _(e):
                def rms2(j, n):
                    e.wait_ge(sem("x1_made0"), 1)
                    e.wait_ge(sem(f"x1_made{j}"), n + 1)
                    e.wait_ge(sem("h2n"), n * 2 + j)
                    act(junk, x1b[:, bass.ds(n * 2 + j, 1), :].rearrange("p a d -> p (a d)"), ACT.Square, accum_out=ssq[:, j:j + 1]).then_inc(sem("ss2"), 1)
                    e.wait_ge(sem("ss2"), n * 2 + j + 1)
                    act(rms[:, j:j + 1], ssq[:, j:j + 1], ACT.Sqrt, scale=1.0 / D, bias=eps).then_inc(sem(f"rms2{j}"), 1)

                def send(j, rows_, n):
                    e.wait_ge(sem(f"h2_made{j}"), n + 1)
                    e.dma_start(h2_d[rows_, :], h2[j]).then_inc(sem(f"h2_out{j}"), 16)

                def put_h2(j, n):
                    e.wait_ge(sem(f"ht_mm{j}"), n + 1)
                    e.wait_ge(sem(f"lg_mm{j}"), n)
                    act(h2T[j][:, 4:8, :], PS[:, 5, :].rearrange("p (c n) -> p c n", c=4), ACT.Copy).then_inc(sem(f"ht_A{j}"), 1)
                rms2(0, 0)
                with e.Fori(0, PT_ // 2) as i:
                    send(0, bass.ds(i * 256, P), i)
                    rms2(1, i)
                    put_h2(0, i)
                    send(1, bass.ds(i * 256 + P, P), i)
                    rms2(0, i + 1)
                    put_h2(1, i)
                send(0, bass.ds(SEQ, P), PT_ // 2)
                put_h2(0, PT_ // 2)

                e.wait_ge(sem("gd"), 1)
                act(oh4, oh4, ACT.Exp).then_inc(sem("gexp"), 1)
                e.wait_ge(sem("edd"), 1)
                act(ed, ed, ACT.Exp).then_inc(sem("eexp"), 1)

                def put_x(j, s):
                    e.wait_ge(sem("tx_mm"), s + 1)
                    act(xT[j][:, 0:4, :], PS[:, 0, :].rearrange("p (c n) -> p c n", c=4), ACT.Copy).then_inc(sem("xT_A"), 1)
                e.wait_ge(sem("meta"), 2)
                used = e.value_load(meta[0:1, SLOTS:SLOTS + 1], min_val=1, max_val=SLOTS)
                put_x(0, 0)
                with e.Fori(0, SLOTS // 2) as i:
                    for j in range(2):
                        s = i * 2 + j
                        with e.If(s < used):
                            e.wait_ge(sem("eh1"), s + 1)
                            e.wait_ge(sem("eh"), s)
                            act(hs, PS[:, 2, :], ACT.Silu).then_inc(sem("silu"), 1)
                            put_x(1 - j, s + 1)
                            e.wait_ge(sem(f"yb_out{j}"), i * 16)
                            e.wait_ge(sem("ey"), s + 1)
                            act(yo[j][:, 0:512], PS[:, 5, :], ACT.Copy).then_inc(sem("yo_A"), 1)
                            e.wait_ge(sem("yo_A"), s + 1)
                            e.wait_ge(sem("yo_D"), s + 1)
                            e.dma_start(yb_d[bass.ds(s * P, P), :], yo[j]).then_inc(sem(f"yb_out{j}"), 16)
                e.wait_ge(sem("yb_out0"), (used + 1) // 2 * 16)
                e.wait_ge(sem("yb_out1"), used // 2 * 16)
                e.wait_ge(sem("meta"), 2)
                act(small[:, 7:8], ones[:, 0:1], ACT.Copy).then_inc(sem("e_all"), 1)

                def rms3(j, n):
                    e.wait_ge(sem(f"x2_made{j}"), n + 1)
                    e.wait_ge(sem(f"o_out{j}"), n * 16)
                    act(out_t[j], acc[j], ACT.Square, accum_out=ssq[:, j:j + 1]).then_inc(sem(f"ss3{j}"), 1)
                    e.wait_ge(sem(f"ss3{j}"), n + 1)
                    act(rms[:, j:j + 1], ssq[:, j:j + 1], ACT.Sqrt, scale=1.0 / D, bias=eps).then_inc(sem(f"rms3{j}"), 1)
                with e.Fori(0, PT_ // 2) as i:
                    for j in range(2):
                        rms3(j, i)
                rms3(0, PT_ // 2)

            @block.vector
            def _(e):
                st = Steps(e, sem("dve_norm2"))
                e.wait_ge(sem("ab2_in"), 2 * MOD_LOAD + 16)
                e.wait_ge(sem("g1_in"), MOD_LOAD)
                e.wait_ge(sem("wr_in"), 64)
                for k in range(2):
                    stt(out=A2[k], in0=A2[k], scalar=1.0, in1=N2, op0=ALU.add, op1=ALU.mult).then_inc(sem("a2"), 1)
                e.wait_ge(sem("a2"), 2)

                def resid(j, n, k):
                    row = x1b[:, bass.ds(n * 2 + j, 1), :].rearrange("p a d -> p (a d)")
                    e.wait_ge(sem(f"out_mm{j}"), n + 1)
                    tt(row, banks(2 * j, 2), G1[k], ALU.mult).then_inc(sem(f"gmul{j}"), 1)
                    e.wait_ge(sem(f"xo_in{j}"), n * 16 + 16)
                    e.wait_ge(sem(f"gmul{j}"), n + 1)
                    tt(row, row, xo[j], ALU.add).then_inc(sem(f"x1_made{j}"), 1)
                    e.wait_ge(sem(f"rms2{j}"), n + 1)
                    e.wait_ge(sem(f"x1_made{j}"), n + 1)
                    nc.vector.reciprocal(rst[:, j:j + 1], rms[:, j:j + 1]).then_inc(sem("h2n"), 1)
                    e.wait_ge(sem("h2n"), n * 2 + j + 1)
                    e.wait_ge(sem(f"h2_out{j}"), n * 16)
                    e.wait_ge(sem(f"ht_mm{j}"), n)
                    stt(out=h2[j], in0=row, scalar=rst[:, j:j + 1], in1=A2[k], op0=ALU.mult, op1=ALU.mult).then_inc(sem(f"h2_sc{j}"), 1)

                def turned(j, n):
                    e.wait_ge(sem(f"ht_mm{j}"), n + 1)
                    e.wait_ge(sem(f"lg_mm{j}"), n)
                    copy(h2T[j][:, 0:4, :], PS[:, 4, :].rearrange("p (c n) -> p c n", c=4)).then_inc(sem(f"ht_D{j}"), 1)

                def logits(j, n):
                    e.wait_ge(sem(f"lg_mm{j}"), n + 1)
                    tt(lg[:, bass.ds(n * 2 + j, 1), :], PS[:, 6 + j, 0:GR + NE].rearrange("p (a n) -> p a n", a=1),
                       br[:].rearrange("p (a n) -> p a n", a=1), ALU.add).then_inc(sem(f"lg{j}"), 1)
                resid(0, 0, 0)
                resid(1, 0, 0)
                turned(0, 0)
                with e.Fori(0, PT_ // 2 - 1) as i:
                    resid(0, i + 1, 0)
                    turned(1, i)
                    logits(0, i)
                    resid(1, i + 1, 0)
                    turned(0, i + 1)
                    logits(1, i)
                last = PT_ // 2 - 1
                resid(0, last + 1, 1)
                turned(1, last)
                logits(0, last)
                turned(0, last + 1)
                logits(1, last)
                logits(0, last + 1)

                st = Steps(e, sem("dve_route"))

                def step(ins):
                    st.did(ins)
                    st.wait()

                def bc(v, *dims):
                    return v.unsqueeze(len(v.shape)).broadcast_to([P, *dims])

                def number_row(v, *dims):
                    for _k in range(len(dims) - 1):
                        v = v.unsqueeze(1)
                    return v.broadcast_to([P, *dims])
                e.wait_ge(sem("iotas"), 4)
                e.wait_ge(sem("lg0"), PT_ // 2 + 1)
                e.wait_ge(sem("lg1"), PT_ // 2)
                step(copy(g8[:, :, 0:GR], lg[:, :, 0:GR]))
                for t in range(NT):
                    st.did(nc.vector.max(gm[:, t, :], g8[:, t, :]))
                st.wait()
                for t in range(NT):
                    st.did(nc.vector.max_index(gi[:, t, :], gm[:, t, :], g8[:, t, :]))
                st.wait()
                step(copy(gif, gi[:, :, 0]))
                step(tt(oh4, bc(gif, NT, GR), number_row(iotaf[:, 0:GR], NT, GR), ALU.is_equal))
                g4 = lambda v: v.rearrange("p t (g e) -> p t g e", g=GR)
                step(tt(g4(gx), g4(lg[:, :, GR:]), bc(oh4, NT, GR, EG), ALU.mult))
                step(nc.vector.tensor_reduce(e8, gx.rearrange("p t (g e) -> p t e g", g=GR), AX_X, ALU.add))
                for t in range(NT):
                    st.did(nc.vector.max(em[:, t, :], e8[:, t, :]))
                st.wait()
                for t in range(NT):
                    st.did(nc.vector.max_index(ei[:, t, :], em[:, t, :], e8[:, t, :]))
                st.wait()
                tt(oh4, lg[:, :, 0:GR], bc(gm[:, :, 0], NT, GR), ALU.subtract).then_inc(sem("gd"), 1)
                tt(ed, em[:, :, 1], em[:, :, 0], ALU.subtract).then_inc(sem("edd"), 1)
                e.wait_ge(sem("gexp"), 1)
                step(nc.vector.reduce_sum(pg, oh4, AX_X))
                step(nc.vector.reciprocal(pg, pg))
                e.wait_ge(sem("eexp"), 1)
                step(ts(den, ed, 1.0, None, ALU.add))
                step(nc.vector.reciprocal(den, den))
                step(tt(wts[:, 0, :], pg, den, ALU.mult))
                step(tt(wts[:, 1, :], wts[:, 0, :], ed, ALU.mult))
                for k in range(2):
                    step(copy(eidf[:, k, :], ei[:, :, k]))
                    step(stt(out=eidf[:, k, :], in0=gif, scalar=float(EG), in1=eidf[:, k, :], op0=ALU.mult, op1=ALU.add))
                    step(tt(E[k], bc(eidf[:, k, :], NT, NE), number_row(iotaf[:, 0:NE], NT, NE), ALU.is_equal))
                tt(M, E[0], E[1], ALU.add).then_inc(sem("M"), 1)
                e.wait_ge(sem("cnt_mm"), 1)
                step(copy(cs.rearrange("p t e -> p (t e)"), PS[:, 0, 0:NT * NE]))
                step(nc.vector.memset(pre[:, 0, :], 0.0))
                for t in range(1, NT):
                    step(tt(pre[:, t, :], pre[:, t - 1, :], cs[:, t - 1, :], ALU.add))
                step(tt(tot, pre[:, NT - 1, :], cs[:, NT - 1, :], ALU.add))
                step(tt(rk.rearrange("p t e -> p (t e)"), PS[:, 1, 0:NT * NE], pre.rearrange("p t e -> p (t e)"), ALU.add))
                step(tt(cmp9, bc(tot, NE, 9), number_row(thr, NE, 9), ALU.is_gt))
                step(nc.vector.reduce_sum(nb, cmp9, AX_X))
                step(nc.vector.tensor_tensor_scan(endb, ones[:, 0:NE], nb, 0.0, ALU.mult, ALU.add))
                step(tt(startb, endb, nb, ALU.subtract))
                for k in range(2):
                    step(tt(ex, rk, E[k], ALU.mult))
                    step(nc.vector.reduce_sum(rj[:, k, :], ex, AX_X))
                    step(tt(ex, number_row(startb, NT, NE), E[k], ALU.mult))
                    step(nc.vector.reduce_sum(sj[:, k, :], ex, AX_X))
                fl = lambda v: v.rearrange("p k t -> p (k t)")
                step(tt(cmp8, bc(fl(rj), 2 * NT, 8), number_row(thr[:, 1:9], 2 * NT, 8), ALU.is_ge))
                step(nc.vector.reduce_sum(fl(qj), cmp8, AX_X))
                step(tt(slj, sj, qj, ALU.add))
                step(stt(out=roj, in0=qj, scalar=-float(P), in1=rj, op0=ALU.mult, op1=ALU.add))
                step(stt(out=dej, in0=slj, scalar=float(P), in1=roj, op0=ALU.mult, op1=ALU.add))
                step(copy(dest[:], dej))
                step(tt(cmpb, endb[0:1].unsqueeze(1).broadcast_to([1, SLOTS, NE]), iotaf[0:1, 0:SLOTS].unsqueeze(2).broadcast_to([1, SLOTS, NE]), ALU.is_le))
                step(nc.vector.reduce_sum(OS[0][0:1, :], cmpb, AX_X))
                step(copy(meta[0:1, 0:SLOTS], OS[0][0:1, :]))
                copy(meta[0:1, SLOTS:], endb[0:1, NE - 1:NE]).then_inc(sem("meta"), 1)
                for q in range(2 * NT):
                    t, k = q // 2, q % 2
                    if q >= 2:
                        e.wait_ge(sem("tab_mm"), q - 1)
                    ts(OP[q % 2], iotaf, roj[:, k, t:t + 1], None, ALU.is_equal).then_inc(sem("OPS"), 1)
                    ts(OS[q % 2], iotaf[:, 0:SLOTS], slj[:, k, t:t + 1], tokf[:, t:t + 1], ALU.is_equal, ALU.mult).then_inc(sem("OPS"), 1)
                step(nc.vector.memset(rows[:, SLOTS:], 0))
                e.wait_ge(sem("tab_mm"), 2 * NT)
                copy(rows[:, 0:SLOTS], PS[:, 2, 0:SLOTS]).then_inc(sem("meta"), 1)

                def put_x(j, s):
                    e.wait_ge(sem("tx_mm"), s + 1)
                    copy(xT[j][:, 4:8, :], PS[:, 1, :].rearrange("p (c n) -> p c n", c=4)).then_inc(sem("xT_D"), 1)
                e.wait_ge(sem("meta"), 2)
                used = e.value_load(meta[0:1, SLOTS:SLOTS + 1], min_val=1, max_val=SLOTS)
                put_x(0, 0)
                with e.Fori(0, SLOTS // 2) as i:
                    for j in range(2):
                        s = i * 2 + j
                        with e.If(s < used):
                            e.wait_ge(sem(f"eh3_{j}"), i + 1)
                            e.wait_ge(sem("silu"), s + 1)
                            e.wait_ge(sem("eh_T"), s)
                            tt(hh_, hs, PS[:, 3, :], ALU.mult).then_inc(sem("eh"), 1)
                            put_x(1 - j, s + 1)
                            e.wait_ge(sem("eh_T"), s + 1)
                            e.wait_ge(sem("ey"), s)
                            if j:
                                e.wait_ge(sem("ey_0"), i + 1)
                            else:
                                e.wait_ge(sem("ey_1"), i)
                            copy(hhT, PS[:, 4, :].rearrange("p (c n) -> p c n", c=DE // P)).then_inc(sem("ehT"), 1)
                            e.wait_ge(sem(f"yb_out{j}"), i * 16)
                            e.wait_ge(sem(f"ey_{j}"), i + 1)
                            copy(yo[j][:, 512:1024], PS[:, 6, :]).then_inc(sem("yo_D"), 1)

                e.wait_ge(sem("g2_in"), MOD_LOAD + 16)
                st = Steps(e, sem("dve_comb"))

                def combine(j, n, k, t):
                    row = x1b[:, bass.ds(t, 1), :].rearrange("p a d -> p (a d)")
                    e.wait_ge(sem(f"y_in{j}"), n * 32 + 32)
                    st.did(ts(acc[j], y0[j], wts[:, 0, bass.ds(t, 1)], None, ALU.mult))
                    st.wait()
                    stt(out=acc[j], in0=y1[j], scalar=wts[:, 1, bass.ds(t, 1)], in1=acc[j], op0=ALU.mult, op1=ALU.add).then_inc(sem(f"c_used{j}"), 1)
                    e.wait_ge(sem(f"c_used{j}"), n + 1)
                    st.did(tt(acc[j], acc[j], G2[k], ALU.mult))
                    st.wait()
                    tt(acc[j], acc[j], row, ALU.add).then_inc(sem(f"x2_made{j}"), 1)

                def finish(j, n):
                    e.wait_ge(sem(f"rms3{j}"), n + 1)
                    st.did(nc.vector.reciprocal(rst[:, j:j + 1], rms[:, j:j + 1]))
                    st.wait()
                    stt(out=out_t[j], in0=acc[j], scalar=rst[:, j:j + 1], in1=NF, op0=ALU.mult, op1=ALU.mult).then_inc(sem(f"o_made{j}"), 1)
                with e.Fori(0, PT_ // 2) as i:
                    st.turn(i, 6)
                    for j in range(2):
                        combine(j, i, 0, i * 2 + j)
                    for j in range(2):
                        finish(j, i)
                st.turn(PT_ // 2, 6)
                combine(0, PT_ // 2, 1, PT_)
                finish(0, PT_ // 2)

            @block.tensor
            def _(e):
                def out(j, n):
                    e.wait_ge(sem(f"mt{j}"), n + 1)
                    e.wait_ge(sem(f"gmul{j}"), n)
                    for k in range(2):
                        last = product(PS[:, 2 * j + k, :], lambda c: mt[j][:, c, :], lambda c: wo[k][:, c, :])
                    last.then_inc(sem(f"out_mm{j}"), 1)

                def turn_h2(j, n):
                    e.wait_ge(sem(f"h2_made{j}"), n + 1)
                    e.wait_ge(sem(f"ht_A{1 - j}"), n + j)
                    e.wait_ge(sem(f"ht_D{1 - j}"), n + j)
                    for c in range(CH):
                        last = tr(PS[:, 4 + c // 4, (c % 4) * P:(c % 4 + 1) * P], h2[j][:, c * P:(c + 1) * P], ident[:])
                    last.then_inc(sem(f"ht_mm{j}"), 1)

                def route(j, n):
                    e.wait_ge(sem(f"ht_A{j}"), n + 1)
                    e.wait_ge(sem(f"ht_D{j}"), n + 1)
                    e.wait_ge(sem(f"lg{j}"), n)
                    product(PS[:, 6 + j, 0:GR + NE], lambda c: h2T[j][:, c, :], lambda c: wr[:, c, :]).then_inc(sem(f"lg_mm{j}"), 1)
                e.wait_ge(sem("wo_in"), 32)
                e.wait_ge(sem("wr_in"), 64)
                out(0, 0)
                out(1, 0)
                turn_h2(0, 0)
                with e.Fori(0, PT_ // 2 - 1) as i:
                    out(0, i + 1)
                    route(0, i)
                    turn_h2(1, i)
                    out(1, i + 1)
                    route(1, i)
                    turn_h2(0, i + 1)
                last = PT_ // 2 - 1
                out(0, last + 1)
                route(0, last)
                turn_h2(1, last)
                route(1, last)
                turn_h2(0, last + 1)
                route(0, last + 1)

                e.wait_ge(sem("M"), 1)
                mm(PS[:, 0, 0:NT * NE], ones[:], M.rearrange("p t e -> p (t e)"), start=True, stop=True)
                mm(PS[:, 1, 0:NT * NE], upper[:], M.rearrange("p t e -> p (t e)"), start=True, stop=True).then_inc(sem("cnt_mm"), 1)
                for q in range(2 * NT):
                    e.wait_ge(sem("OPS"), 2 * q + 2)
                    mm(PS[:, 2, 0:SLOTS], OP[q % 2], OS[q % 2], start=q == 0, stop=q == 2 * NT - 1).then_inc(sem("tab_mm"), 1)

                def turn_rows(j, s, n):
                    e.wait_ge(sem(f"xg_in{j}"), n * 16)
                    e.wait_ge(sem("xT_A"), s)
                    e.wait_ge(sem("xT_D"), s)
                    for c in range(CH):
                        last = tr(PS[:, c // 4, (c % 4) * P:(c % 4 + 1) * P], xg[j][:, c * P:(c + 1) * P], ident[:])
                    last.then_inc(sem("tx_mm"), 1)
                e.wait_ge(sem("meta"), 2)
                used = e.value_load(meta[0:1, SLOTS:SLOTS + 1], min_val=1, max_val=SLOTS)
                turn_rows(0, 0, 1)
                with e.Fori(0, SLOTS // 2) as i:
                    for j in range(2):
                        s = i * 2 + j
                        with e.If(s < used):
                            e.wait_ge(sem("xT_A"), s + 1)
                            e.wait_ge(sem("xT_D"), s + 1)
                            e.wait_ge(sem("eh"), s)
                            e.wait_ge(sem(f"w1_in{j}"), i * 16 + 16)
                            product(PS[:, 2, :], lambda c: xT[j][:, c, :], lambda c: w1b[j][:, c, :]).then_inc(sem("eh1"), 1)
                            e.wait_ge(sem(f"w3_in{j}"), i * 16 + 16)
                            product(PS[:, 3, :], lambda c: xT[j][:, c, :], lambda c: w3b[j][:, c, :]).then_inc(sem(f"eh3_{j}"), 1)
                            turn_rows(1 - j, s + 1, i + 1 + j)
                            e.wait_ge(sem("eh"), s + 1)
                            e.wait_ge(sem("ehT"), s)
                            for c in range(DE // P):
                                last = tr(PS[:, 4, c * P:(c + 1) * P], hh_[:, c * P:(c + 1) * P], ident[:])
                            last.then_inc(sem("eh_T"), 1)
                            e.wait_ge(sem("ehT"), s + 1)
                            e.wait_ge(sem(f"w2_in{j}"), i * 16 + 16)
                            e.wait_ge(sem("yo_A"), s)
                            for k in range(2):
                                if k:
                                    e.wait_ge(sem("yo_D"), s)
                                for c in range(DE // P):
                                    last = mm(PS[:, 5 + k, :], hhT[:, c, :], w2b[j][:, c, 512 * k:512 * (k + 1)], start=c == 0, stop=c == DE // P - 1)
                                last.then_inc(sem(f"ey_{j}") if k else sem("ey"), 1)


INPUTS = ["x_prompt", "x_sample", "cache_k", "cache_v", "cache_logf", "state_conv", "state_h", "c_prompt", "c_sample",
          "w_mod", "b_mod", "norm1", "w_in", "b_f", "conv_w", "conv_b", "w_r", "b_r", "w_i", "b_i", "rglru_lambda",
          "w_gate", "b_gate", "w_pa", "w_pb", "w_out", "norm2", "w_rg", "b_rg", "w_re", "b_re", "w1", "w3", "w2", "norm_f"]
OUTPUTS = [(1, SEQ, D), (DB, DS, D), (1, 1, SEQ, H, HD), (1, 1, SEQ, H, HD), (1, 1, SEQ, H), (1, 1, 3, D), (1, 1, D),
           (1, DB, DS, H, HD), (1, DB, DS, H, HD), (1, DB, DS, H), (1, DB, 3, D), (1, DB, D)]


def kernel(**inputs):
    import numpy as np
    import concourse.bacc as bacc
    from concourse.bass_utils import run_bass_kernel_spmd

    nc = bacc.Bacc("TRN2", target_bir_lowering=False, num_devices=1)
    arrays, args = {}, {}
    for name in INPUTS:
        arrays[f"in_{name}"] = np.ascontiguousarray(inputs[name])
        args[name] = nc.dram_tensor(f"in_{name}", arrays[f"in_{name}"].shape, F32, kind="ExternalInput").ap()
    outs = [nc.dram_tensor(f"out_{n}", shape, F32, kind="ExternalOutput").ap() for n, shape in enumerate(OUTPUTS)]
    trunk(nc, args, outs)
    result = run_bass_kernel_spmd(nc, [arrays], core_ids=[0]).results[0]
    return tuple(result[f"out_{n}"] for n in range(len(OUTPUTS)))
```

```python
from contextlib import ExitStack

import concourse.bass as bass
from concourse import mybir
from concourse.alu_op_type import AluOpType as ALU

F32 = mybir.dt.float32
I32 = mybir.dt.int32
U32 = mybir.dt.uint32
F32R = mybir.dt.float32r
ACT = mybir.ActivationFunctionType
AX_X = mybir.AxisListType.X

P = 128
D = 1024
CH = D // P
SEQ = 1024
DB, DS = 8, 16
SMP = DB * DS
TOK = SEQ + SMP
NT = TOK // P
PT_ = SEQ // P
PAST = 256
LK = PAST + DS
H, HD = 16, 64
NC_ = DB + 1
G3 = 3
NG = TOK // G3
GR, EG = 4, 8
NE = GR * EG
DE = 512
NA = 2 * TOK
SLOTS = NA // P + NE
EPS = 1e-6
BIG = 3.0e38
W_Q, W_K, W_V, W_F = 0, D, 2 * D, 3 * D
W_X, W_G = 3 * D + H, 4 * D + H
R_CW, R_CB, R_BR, R_BI, R_LAM, R_BG, R_H0, R_CV = 0, 4, 5, 6, 7, 8, 10, 18
NR = 42


class Steps:

    def __init__(self, eng, sem):
        self.eng, self.sem, self.base, self.n = eng, sem, 0, 0

    def turn(self, i, per):
        self.base, self.n = i * per, 0

    def did(self, ins):
        ins.then_inc(self.sem, 1)
        self.n += 1

    def wait(self):
        self.eng.wait_ge(self.sem, self.base + self.n)


def trunk(nc, a, o):
    (y_p, y_s, k_p, v_p, lf_p, cv_p, h_p, k_s, v_s, lf_s, cv_s, h_s) = o
    with ExitStack() as ctx:
        sems = {}

        def sem(name):
            if name not in sems:
                sems[name] = nc.alloc_semaphore(name=name)
            return sems[name]

        def clear_semaphores():
            nc.all_engine_barrier()
            nc.clear_and_free_semaphores(list(sems.values()))
            nc.all_engine_barrier()
            sems.clear()

        at = {}

        def sb(name, shape, dt=F32):
            t = ctx.enter_context(nc.sbuf_tensor(name, shape, dt))
            at[name] = nc.sbuf_base - 4 * shape[1] if dt == F32 and len(shape) == 2 else None
            return t

        def dram(name, shape):
            return nc.dram_tensor(name, shape, F32, kind="Internal").ap()

        RW = CH * TOK
        R1, R2, R3, R4 = (sb(f"region{i}", [P, RW]) for i in range(1, 5))
        WR = sb("weights", [P, 8192])

        def view(region, off, *dims):
            n = 1
            for d in dims:
                n *= d
            assert off + n <= region.shape[1], (off, n)
            v = region[:, off:off + n]
            if len(dims) == 2:
                v = v.rearrange("p (x y) -> p x y", x=dims[0])
            if len(dims) == 3:
                v = v.rearrange("p (x y z) -> p x y z", x=dims[0], y=dims[1])
            return v

        def part(name, region, off, *dims):
            n = 1
            for d in dims:
                n *= d
            t = nc.alloc_sbuf_tensor_at(name, [P, n], F32R, offset=at[region] + 4 * off)
            v = t[:, :]
            if len(dims) == 2:
                v = v.rearrange("p (x y) -> p x y", x=dims[0])
            return v

        hTh, hTl = part("h_hi", "region1", 0, CH, TOK), part("h_lo", "region2", 0, CH, TOK)
        vtok = view(R3, 0, NT, D)
        obT = view(R3, 0, CH, TOK)
        x1b = view(R2, 0, NT, D)


        ident = sb("ident", [P, P])
        upper = sb("upper", [P, P])
        ones = sb("ones", [P, P])
        causal = sb("causal", [P, P])
        causal16 = sb("causal16", [P, DS])
        cT = sb("cT", [P, CH, NC_])
        pT = sb("pT", [P, CH, NR])
        qTs = sb("qTs", [P, CH, SMP])
        kTs = sb("kTs", [P, CH, SMP])
        small = sb("small", [P, 64])
        mixtmp = sb("mixtmp", [P, 3072])
        eps = small[:, 6:7]
        sp4 = small[:, 8:16]

        mod_d = dram("mod_d", [NC_, 6 * D])
        F_d = dram("F_d", [H, SEQ])
        Fs_d = dram("Fs_d", [DB, H // 2, 2, LK])
        h2_d = dram("h2_d", [TOK, D])
        yb_d = dram("yb_d", [SLOTS * P, D])
        oa_d = dram("oa_d", [D, TOK])
        mix_d = dram("mix_d", [D, TOK])

        PS = ctx.enter_context(nc.psum_tensor("PS", [P, 8, 512], F32))

        def banks(b, n, parts=P):
            return PS[0:parts, b:b + n, :].rearrange("p b n -> p (b n)")

        xp, xs = a["x_prompt"][0], a["x_sample"].rearrange("b t d -> (b t) d")
        w_in, w_mod, w_gate, w_pa, w_pb, w_out = (
            a[n][0].rearrange("(c p) n -> p c n", p=P) for n in ("w_in", "w_mod", "w_gate", "w_pa", "w_pb", "w_out"))
        w1, w3, w2 = a["w1"][0], a["w3"][0], a["w2"][0]

        def tcols(t):
            return bass.ds(SEQ, P) if t is None else bass.ds(t * P, P)

        def spread(row, parts=P):
            return row.broadcast_to([parts, row.shape[-1]])

        def cut(rows_, like):
            return rows_ if len(like.shape) == 2 else rows_.rearrange("p (a n) -> p a n", a=like.shape[1])

        def mod_load(e, dst, piece, name):
            cols = bass.ds(piece * D, D)
            e.dma_start(dst[0], cut(spread(mod_d[0:1, cols]), dst[0])).then_inc(sem(name), 16)
            for b in range(DB):
                e.dma_start(dst[1][b * DS:(b + 1) * DS], cut(spread(mod_d[b + 1:b + 2, cols], DS), dst[1])).then_inc(sem(name), 16)
        MOD_LOAD = 16 * NC_

        crow, prow = view(R3, 0, D)[0:NC_, :], view(R3, D, D)[0:NR, :]
        mrow = view(R3, 2 * D, 2, 512)[0:NC_]
        bmod = view(R3, 3 * D, 2, 512)[0:NC_]
        csig = view(R3, 4 * D, D)[0:NC_, :]
        wmod_r = [view(WR, 4096 * j, CH, 512) for j in range(2)]
        A1 = [view(R4, 4 * D, D), view(R4, 5 * D, D)]
        B1 = [view(R4, 6 * D, D), view(R4, 7 * D, D)]
        N1 = view(R4, 8 * D, D)
        xt = [view(R4, D * j, D) for j in range(2)]
        xn = [view(R4, D * (2 + j), D) for j in range(2)]
        ssq, rms, rst = small[:, 0:2], small[:, 2:4], small[:, 4:6]
        wv = wmod_r
        wvh = [part(f"wv_hi{j}", "region4", 4096 * j, CH, 512) for j in range(2)]
        wvl = [part(f"wv_lo{j}", "weights", 4096 * j, CH, 512) for j in range(2)]
        wf = view(mixtmp, 2 * D, CH, P)
        wfh, wfl = part("wf_hi", "region4", 8 * D, CH, P), part("wf_lo", "mixtmp", 2 * D, CH, P)
        bf = sb("bf", [H, 1])
        fz, fa = (view(mixtmp, TOK * k, TOK)[0:H, :] for k in range(2))
        lf = fz
        Fp, onesw = (t[:].rearrange("p c n -> p (c n)")[0:H, :] for t in (qTs, kTs))
        Fs, Fso = (view(R4, DB * LK * k, DB, LK)[0:H] for k in range(2))
        lfT = sb("lfT", [P, NT, H])
        clf = sb("clf", [P, DB, 2, H])
        wq, wk = view(WR, 0, CH, P), view(WR, 1024, CH, P)
        wqh, wkh = part("wq_hi", "weights", 2048 + 4 * TOK, CH, P), part("wk_hi", "mixtmp", (2 + NT) * P, CH, P)
        wql, wkl = part("wq_lo", "weights", 0, CH, P), part("wk_lo", "weights", 1024, CH, P)
        ob = [view(WR, 3072 + 4 * TOK + 2 * P * s, 2 * P) for s in range(2)]
        qb, kb = ([view(WR, 2048 + TOK * (2 * j + k), TOK) for j in range(2)] for k in range(2))
        sP = [view(R4, D * k, D) for k in range(3)]
        PTb = [view(R4, D * (3 + k), D) for k in range(2)]
        Bt = [view(R4, D * (5 + 2 * j), 2, D) for j in range(2)]
        kst = view(mixtmp, 2 * P, NT, P)
        ot = [view(mixtmp, P * k, P) for k in range(2)]
        mn, ls, rl = small[:, 16:32], small[:, 32:48], small[:, 48:64]
        kc = [view(WR, 4096 * j, 2, D) for j in range(2)]
        vc = [view(WR, 4096 * j + 2048, 2, D) for j in range(2)]
        kcT = [view(R4, CH * LK * j, CH, LK) for j in range(2)]
        v16 = [view(R4, 2 * CH * LK + D * j, D)[0:DS, :] for j in range(2)]
        Bs = [view(R4, 2 * CH * LK + 2 * D + 2 * LK * j, 2, LK) for j in range(2)]
        sS = [view(R4, 2 * CH * LK + 2 * D + 4 * LK + 2 * LK * j, 2, LK) for j in range(2)]
        qbd = [view(R4, 2 * CH * LK + 2 * D + 8 * LK + 256 * j, CH, 32) for j in range(2)]
        PTs = [view(mixtmp, 768 * j, 2, 3, P) for j in range(2)]
        oas = view(mixtmp, 2048, CH, SMP)
        osb = [view(mixtmp, 1536 + 2 * P * j, 2, P) for j in range(2)]
        XW = 3 + SEQ + DB * (DS + 3)
        wx = [view(WR, 2048 * k, CH, P) for k in range(2)]
        wxh = [part(f"wx_hi{k}", "weights", 2048 * k + 1024, CH, P) for k in range(2)]
        wxl = [part(f"wx_lo{k}", "weights", 2048 * k, CH, P) for k in range(2)]
        rr, ii, Rr = (view(WR, 4096 + TOK * k, TOK) for k in range(3))
        bw = [view(WR, 4096 + 3 * TOK + 256 * j, 2, P) for j in range(2)]
        xbuf = [view(R4, 1184 * j, XW) for j in range(2)]
        xbs = [xbuf[j][:, 3 + SEQ:].rearrange("p (b t) -> p b t", b=DB) for j in range(2)]
        xc = [view(R4, 2368 + TOK * j, TOK) for j in range(2)]
        gel = [view(R4, 2368 + TOK * (2 + j), TOK) for j in range(2)]
        hb = view(R4, 2368 + 4 * TOK, TOK)
        hc = sb("hc", [P, CH, 36])
        hrow = qTs[:].rearrange("p c n -> p (c n)")[0:36, :]
        t8 = sb("t8", [P, DB])
        sp8 = sb("sp8", [P, CH])
        wm = [view(WR, 2048 * q, CH, P) for q in range(4)]
        wmh = [part(f"wm_hi{q}", "weights", 2048 * q + 1024, CH, P) for q in range(4)]
        wml = [part(f"wm_lo{q}", "weights", 2048 * q, CH, P) for q in range(4)]
        oa = view(R4, 0, CH, NG)
        oal = part("oa_lo", "region4", 0, CH, NG)
        oah, obh = part("oa_hi", "region4", CH * NG, CH, NG), part("ob_hi", "region4", 2 * CH * NG, CH, NG)
        obl = part("ob_lo", "region3", 0, CH, TOK)
        BANK = (0, 2, 1, 3)
        sg = [[view(mixtmp, 1536 * s + NG * k, NG) for k in range(2)] for s in range(2)]
        tm = [[view(mixtmp, 1536 * s + NG * (2 + k), NG) for k in range(2)] for s in range(2)]
        wo = [view(R2, 0, CH, TOK)[:, :, 0:512], view(R4, 4096, CH, 512)]
        woh = [part(f"wo_hi{k}", "weights", 4096 * k, CH, 512) for k in range(2)]
        wol = [part(f"wo_lo{k}", "region4", 4096 * k, CH, 512) for k in range(2)]
        def pieces(chunk, off, width):
            return view(R1, 0, CH, TOK)[:, chunk:chunk + D // width, off:off + width]
        G1, A2 = ([pieces(4 * q + 2 * k, 0, 512) for k in range(2)] for q in range(2))
        B2, xo = ([pieces(4 * k, 512 + 256 * q, 256) for k in range(2)] for q in range(2))
        N2 = view(R4, 8 * D, D)
        mt = [view(R3, D * j, CH, P) for j in range(2)]
        mtl = [part(f"mt_lo{j}", "region3", D * j, CH, P) for j in range(2)]
        mth = [part(f"mt_hi{j}", "region3", D * (7 + j), CH, P) for j in range(2)]
        h2 = [view(R3, D * (2 + j), D) for j in range(2)]
        h2T = [view(R3, D * (4 + j), CH, P) for j in range(2)]
        junk = view(R3, D * 6, D)
        wr = sb("wr", [P, CH, GR + NE])
        br = sb("br", [P, GR + NE])
        lg = sb("lg", [P, NT, GR + NE])
        _o = [0]

        def rt(*dims):
            v = view(WR, _o[0], *dims)
            n = 1
            for d in dims:
                n *= d
            _o[0] += n
            return v
        g8, gm, e8, em = (rt(NT, 8) for _ in range(4))
        gi, ei = rt(NT, 8).bitcast(U32), rt(NT, 8).bitcast(U32)
        gif, pg, ed, den = (rt(NT) for _ in range(4))
        oh4 = rt(NT, GR)
        gx = rt(NT, NE)
        E = [rt(NT, NE) for _ in range(2)]
        M, cs, pre, rk, ex = (rt(NT, NE) for _ in range(5))
        eidf, rj, sj, qj, slj, roj, dej = (rt(2, NT) for _ in range(7))
        cmp9 = rt(NE, 9)
        cmp8 = rt(2 * NT, 8)
        tot, nb, endb, startb = (rt(NE) for _ in range(4))
        iotaf = rt(P)
        thr = rt(9)
        tokf = rt(NT)
        cmpb = rt(SLOTS, NE)[0:1]
        OP = [rt(P) for _ in range(2)]
        OS = [rt(SLOTS) for _ in range(2)]
        wts = sb("wts", [P, 2, NT])
        dest = sb("dest", [P, 2, NT], U32)
        rows = sb("rows", [P, SLOTS + 1], U32)
        meta = sb("meta", [1, SLOTS + 1], I32)
        w1b = [view(R, 0, CH, DE) for R in (R1, R4)]
        w3b = [view(R, 4096, CH, DE) for R in (R1, R4)]
        w2b = [view(R3, 4096 * j, DE // P, D) for j in range(2)]
        xg = [view(WR, D * j, D) for j in range(2)]
        xT = [view(WR, D * (2 + j), CH, P) for j in range(2)]
        yo = [view(WR, D * (4 + j), D) for j in range(2)]
        hs, hh_ = view(WR, D * 6, DE), view(WR, D * 6 + DE, DE)
        hhT = view(WR, D * 7, DE // P, P)
        gidx = [sb(f"gidx{j}", [P, 1], U32) for j in range(2)]
        G2, NF = [view(R, RW - D, D) for R in (R1, R4)], view(R3, RW - D, D)
        RING = 4
        y01 = [[view(R1, D * (RING * k + j), D) for j in range(RING)] for k in range(2)]
        acc, out_t = ([view(R3, D * (RING * k + j), D) for j in range(RING)] for k in range(2))
        ssq3, rms3s, rst3 = (small[:, 16 + RING * k:16 + RING * (k + 1)] for k in range(3))
        PAIRS = [tuple(range(t, min(t + 2, NT))) for t in range(0, NT, 2)]

        copy, tt, ts, stt = nc.vector.tensor_copy, nc.vector.tensor_tensor, nc.vector.tensor_scalar, nc.vector.scalar_tensor_tensor
        act, mm, tr = nc.scalar.activation, nc.tensor.matmul, nc.tensor.transpose

        def lo_of(eng, lo, x, hi):
            return eng.tensor_tensor(lo, x, hi.bitcast(F32), ALU.subtract)

        def product3(out, lh, ll, rh, rl, ready=None):
            for c in range(CH):
                if ready:
                    ready(c)
                mm(out, lh(c), rl(c), start=c == 0, stop=False)
                mm(out, ll(c), rh(c), start=False, stop=False)
                last = mm(out, lh(c), rh(c), start=False, stop=c == CH - 1)
            return last

        def pair_product(keys, n):
            wl, wh = (wkl, wkh) if keys else (wql, wqh)
            cols = slice(n * NG, (n + 1) * NG)
            return product3(PS[:, 1 + 2 * n, 0:NG], lambda c: wh[:, c, :], lambda c: wl[:, c, :],
                            lambda c: hTh[:, c, cols], lambda c: hTl[:, c, cols])

        def product(out, lhs, rhs):
            for c in range(CH):
                last = mm(out, lhs(c), rhs(c), start=c == 0, stop=c == CH - 1)
            return last

        with nc.Block() as block:

            @block.sync
            def _(e):
                e.dma_start(crow[0:1, :], a["c_prompt"]).then_inc(sem("c_in"), 16)
                e.dma_start(crow[1:NC_, :], a["c_sample"]).then_inc(sem("c_in"), 16)


                def mod_weights(j, i):
                    cols = bass.ds(i * 1024 + j * 512, 512)
                    e.wait_ge(sem(f"mod_mm{j}"), i)
                    e.dma_start(wmod_r[j], w_mod[:, :, cols]).then_inc(sem(f"mod_w{j}"), 16)
                    e.wait_ge(sem(f"mod_row{j}"), i)
                    e.dma_start(bmod[:, j, :], spread(a["b_mod"][:, cols], NC_)).then_inc(sem(f"mod_b{j}"), 16)
                for i in range(2):
                    for j in range(2):
                        mod_weights(j, i)
                for r, nm in ((R_CB, "conv_b"), (R_BR, "b_r"), (R_BI, "b_i"), (R_LAM, "rglru_lambda")):
                    e.dma_start(prow[r:r + 1, :], a[nm]).then_inc(sem("p_in"), 16)
                e.dma_start(prow[R_CW:R_CW + 4, :], a["conv_w"][0]).then_inc(sem("p_in"), 16)
                e.dma_start(prow[R_BG:R_BG + 2, :], a["b_gate"].rearrange("a (r d) -> (a r) d", r=2)).then_inc(sem("p_in"), 16)
                e.dma_start(prow[R_H0:R_H0 + DB, :], a["state_h"][0]).then_inc(sem("p_in"), 16)
                e.dma_start(prow[R_CV:NR, :], a["state_conv"][0].rearrange("b k d -> (b k) d")).then_inc(sem("p_in"), 16)
                e.wait_ge(sem("wf_zero"), 1)
                e.dma_start(wf[:, :, 0:H], w_in[:, :, W_F:W_F + H]).then_inc(sem("wf_in"), 16)
                e.dma_start(bf[:], a["b_f"].rearrange("a h -> h a")).then_inc(sem("wf_in"), 16)
                for b in range(DB):
                    e.dma_start(clf[:, b], a["cache_logf"][0, b].rearrange("(t p) h -> p t h", p=P)).then_inc(sem("clf_in"), 16)
                for j in range(2):
                    mod_weights(j, 2)
                for j in range(2):
                    e.wait_ge(sem(f"mod_st{j}"), 16 * 2)
                mod_load(e, A1, 1, "ab1_in")
                mod_load(e, B1, 0, "ab1_in")
                e.dma_start(N1, spread(a["norm1"])).then_inc(sem("ab1_in"), 16)

                def rows_in(j, i):
                    e.wait_ge(sem(f"xn_made{j}"), i)
                    e.dma_start(xt[j], xp[bass.ds(i * 256 + j * P, P), :]).then_inc(sem(f"x_in{j}"), 16)
                with e.Fori(0, PT_ // 2 - 1) as i:
                    for j in range(2):
                        rows_in(j, i)
                    for j in range(2):
                        mod_weights(j, i + 3)
                for j in range(2):
                    rows_in(j, PT_ // 2 - 1)
                e.wait_ge(sem("xn_made0"), PT_ // 2)
                e.dma_start(xt[0], xs).then_inc(sem("x_in0"), 16)
                for n in range(2):
                    e.wait_ge(sem(f"mod_mm{n}"), 6)
                    e.dma_start(wv[n], w_in[:, :, W_V + 512 * n:W_V + 512 * (n + 1)]).then_inc(sem(f"wv_in{n}"), 16)
                e.wait_ge(sem("lfT"), 1)
                e.dma_start(lf_p[0, 0].rearrange("(t p) h -> p t h", p=P), lfT[:, 0:PT_, :]).then_inc(sem("lf_out"), 16)
                e.dma_start(lf_s[0].rearrange("b t h -> (b t) h"), lfT[:, PT_, :]).then_inc(sem("lf_out"), 16)
                e.wait_ge(sem("Fp"), 1)
                e.dma_start(F_d, Fp).then_inc(sem("F_out"), 16)
                e.wait_ge(sem("v_mm"), NT)
                e.dma_start(wq, w_in[:, :, W_Q:W_Q + P]).then_inc(sem("w0_in"), 16)
                e.dma_start(wk, w_in[:, :, W_K:W_K + P]).then_inc(sem("w0_in"), 16)
                e.wait_ge(sem("v_evA"), NT)
                e.wait_ge(sem("v_evD"), NT)
                e.dma_start(v_p[0, 0].rearrange("(t p) h d -> p t (h d)", p=P), vtok[:, 0:PT_, :]).then_inc(sem("v_out"), 16)
                e.dma_start(v_s[0].rearrange("b t h d -> (b t) (h d)"), vtok[:, PT_, :]).then_inc(sem("v_out"), 16)
                e.wait_ge(sem("F_made"), DB)
                for g in range(2):
                    e.dma_start(Fs_d[:, :, g, :].rearrange("b h l -> h b l"), Fso[g * H // 2:(g + 1) * H // 2]).then_inc(sem("F_out"), 16)
                e.wait_ge(sem("F_out"), 48)
                for j in range(2):
                    e.wait_ge(sem(f"mod_st{j}"), 16 * 6)
                e.wait_ge(sem("v_out"), 32)
                e.wait_ge(sem("lf_out"), 32)

            @block.gpsimd
            def _(e):
                st = Steps(e, sem("pool_setup"))
                st.did(e.memset(ident[:], 0.0))
                st.did(e.memset(upper[:], 1.0))
                st.did(e.memset(causal[:], 0.0))
                st.did(e.memset(ones[:], 1.0))
                st.did(e.memset(eps, EPS))
                e.memset(wf, 0.0).then_inc(sem("wf_zero"), 1)
                st.wait()
                st.did(e.affine_select(out=ident[:], in_=ident[:], compare_op=ALU.not_equal, fill=1.0, base=0,
                                       pattern=[[-1, P]], channel_multiplier=1))
                st.did(e.affine_select(out=upper[:], in_=upper[:], compare_op=ALU.is_gt, fill=0.0, base=0,
                                       pattern=[[1, P]], channel_multiplier=-1))
                st.did(e.affine_select(out=causal[:], in_=causal[:], compare_op=ALU.is_ge, fill=BIG, base=0,
                                       pattern=[[-1, P]], channel_multiplier=1))

            @block.scalar
            def _(e):
                e.wait_ge(sem("c_in"), 32)
                act(csig, crow, ACT.Sigmoid).then_inc(sem("c_sig"), 1)

                def mod_out(j, i):
                    e.wait_ge(sem(f"mod_row{j}"), i + 1)
                    e.dma_start(mod_d[:, bass.ds(i * 1024 + j * 512, 512)], mrow[:, j, :]).then_inc(sem(f"mod_st{j}"), 16)
                for i in range(2):
                    for j in range(2):
                        mod_out(j, i)

                def rms_tile(j, n):
                    e.wait_ge(sem(f"x_in{j}"), n * 16 + 16)
                    e.wait_ge(sem(f"xn_T{j}"), n)
                    act(xn[j], xt[j], ACT.Square, accum_out=ssq[:, j:j + 1]).then_inc(sem(f"ssq{j}"), 1)
                    e.wait_ge(sem(f"ssq{j}"), n + 1)
                    act(rms[:, j:j + 1], ssq[:, j:j + 1], ACT.Sqrt, scale=1.0 / D, bias=eps).then_inc(sem(f"rms{j}"), 1)

                def put_h(cols, j, n):
                    e.wait_ge(sem("pool_setup"), 8)
                    e.wait_ge(sem(f"xn_T{j}"), n + 1)
                    act(hTh[:, :, cols], banks(4 + 2 * j, 2).rearrange("p (c n) -> p c n", c=CH), ACT.Copy).then_inc(sem(f"h_evA{j}"), 1)
                e.wait_ge(sem("pool_setup"), 8)
                with e.Fori(0, PT_ // 2) as i:
                    for j in range(2):
                        rms_tile(j, i)
                    for j in range(2):
                        mod_out(j, i + 2)
                        put_h(bass.ds(i * 256 + j * P, P), j, i)
                rms_tile(0, PT_ // 2)
                put_h(bass.ds(SEQ, P), 0, PT_ // 2)

                e.wait_ge(sem("pT"), 1)
                act(t8[:], pT[:, :, R_LAM], ACT.Abs).then_inc(sem("sp"), 1)
                e.wait_ge(sem("sp"), 1)
                act(t8[:], t8[:], ACT.Exp, scale=-1.0).then_inc(sem("sp"), 1)
                e.wait_ge(sem("sp"), 2)
                act(t8[:], t8[:], ACT.Ln, bias=ones[:, 0:1]).then_inc(sem("sp"), 1)

                e.wait_ge(sem("xn_T0"), PT_ // 2 + 1)
                e.wait_ge(sem("xn_T1"), PT_ // 2)
                def split_v(n):
                    e.wait_ge(sem(f"wv_in{n}"), 16)
                    for c in range(0, CH, 2):
                        act(wvh[n][:, c:c + 2, :], wv[n][:, c:c + 2, :], ACT.Copy).then_inc(sem("wv_hi"), 1)
                e.wait_ge(sem("wf_in"), 32)
                act(wfh, wf, ACT.Copy).then_inc(sem("wf_hi"), 1)
                split_v(0)
                for j in range(2):
                    e.wait_ge(sem(f"mod_st{j}"), 16 * 6)
                for q in range(0, 2 * NT, 2):
                    n, t = q // NT, q % NT
                    e.wait_ge(sem("v_mm"), q + 1)
                    act(vtok[:, t, 512 * n:512 * (n + 1)], PS[:, q % 4, :], ACT.Copy).then_inc(sem("v_evA"), 1)
                    if q == 0:
                        for n in range(G3):
                            e.wait_ge(sem("f_mm"), n + 1)
                            act(fz[:, n * NG:(n + 1) * NG], PS[0:H, 4 + n, 0:NG], ACT.Identity, bias=bf[:]).then_inc(sem("fz"), 1)
                        e.wait_ge(sem("fz"), 3)
                        act(fa, fz, ACT.Abs).then_inc(sem("fa"), 1)
                        e.wait_ge(sem("fa"), 1)
                        act(fa, fa, ACT.Exp, scale=-1.0).then_inc(sem("fa"), 1)
                        e.wait_ge(sem("fa"), 2)
                        act(fa, fa, ACT.Ln, bias=ones[0:H, 0:1]).then_inc(sem("fa"), 1)
                    if q == 2:
                        split_v(1)
                e.wait_ge(sem("v_mm"), 2 * NT)
                e.wait_ge(sem("lf"), 1)
                e.wait_ge(sem("w0_in"), 32)
                act(wqh, wq, ACT.Copy).then_inc(sem("w0_hi"), 1)
                act(wkh, wk, ACT.Copy).then_inc(sem("w0_hi"), 1)
                e.wait_ge(sem("clf_ps"), 1)
                act(Fs[:, :, 0:PAST], banks(0, 4, H).rearrange("p (b n) -> p b n", b=DB), ACT.Copy).then_inc(sem("Fs_old"), 1)
                for n in range(G3):
                    e.wait_ge(sem("q0_mm"), n + 1)
                    act(qb[0][:, n * NG:(n + 1) * NG], PS[:, 1 + 2 * n, 0:NG], ACT.Copy, scale=-(HD ** -0.5)).then_inc(sem("q0_ev"), 1)

            @block.vector
            def _(e):
                e.wait_ge(sem("c_sig"), 1)
                tt(crow, crow, csig, ALU.mult).then_inc(sem("c_silu"), 1)
                e.wait_ge(sem("cT_ps"), 1)
                copy(cT[:].rearrange("p c r -> p (c r)"), PS[:, 0, 0:CH * NC_]).then_inc(sem("cT"), 1)

                def mod_rows(j, i):
                    e.wait_ge(sem(f"mod_b{j}"), i * 16 + 16)
                    e.wait_ge(sem(f"mod_st{j}"), i * 16)
                    e.wait_ge(sem(f"mod_mm{j}"), i + 1)
                    tt(mrow[:, j, :], PS[0:NC_, 2 + j, :], bmod[:, j, :], ALU.add).then_inc(sem(f"mod_row{j}"), 1)
                for i in range(2):
                    for j in range(2):
                        mod_rows(j, i)
                e.wait_ge(sem("pT_ps"), 1)
                copy(pT[:].rearrange("p c r -> p (c r)"), PS[:, 1, 0:CH * NR]).then_inc(sem("pT"), 1)

                e.wait_ge(sem("ab1_in"), 2 * MOD_LOAD + 16)
                for k in range(2):
                    stt(out=A1[k], in0=A1[k], scalar=1.0, in1=N1, op0=ALU.add, op1=ALU.mult).then_inc(sem("a1"), 1)
                e.wait_ge(sem("a1"), 2)
                st = Steps(e, sem("dve_norm1"))

                def norm_tile(j, k, n):
                    e.wait_ge(sem(f"rms{j}"), n + 1)
                    st.did(nc.vector.reciprocal(rst[:, j:j + 1], rms[:, j:j + 1]))
                    st.wait()
                    st.did(stt(out=xn[j], in0=xt[j], scalar=rst[:, j:j + 1], in1=A1[k], op0=ALU.mult, op1=ALU.mult))
                    st.wait()
                    tt(xn[j], xn[j], B1[k], ALU.add).then_inc(sem(f"xn_made{j}"), 1)

                def put_h(cols, j, n):
                    e.wait_ge(sem(f"h_evA{j}"), n + 1)
                    lo_of(nc.vector, hTl[:, :, cols], banks(4 + 2 * j, 2).rearrange("p (c n) -> p c n", c=CH), hTh[:, :, cols]).then_inc(sem(f"h_evD{j}"), 1)
                with e.Fori(0, PT_ // 2) as i:
                    st.turn(i, 4)
                    for j in range(2):
                        norm_tile(j, 0, i)
                    for j in range(2):
                        mod_rows(j, i + 2)
                        put_h(bass.ds(i * 256 + j * P, P), j, i)
                st.turn(PT_ // 2, 4)
                norm_tile(0, 1, PT_ // 2)
                put_h(bass.ds(SEQ, P), 0, PT_ // 2)

                e.wait_ge(sem("sp"), 3)
                ts(sp4, pT[:, :, R_LAM], -1.0, 0.0, ALU.mult, ALU.max).then_inc(sem("spd"), 1)
                e.wait_ge(sem("spd"), 1)
                tt(sp4, sp4, t8[:], ALU.add).then_inc(sem("spd"), 1)
                e.wait_ge(sem("spd"), 2)
                ts(sp8[:], sp4, -8.0, None, ALU.mult).then_inc(sem("spd"), 1)
                e.wait_ge(sem("spd"), 3)
                ts(sp4, sp4, 4.0, None, ALU.mult).then_inc(sem("sp4"), 1)

                e.wait_ge(sem("wf_hi"), 1)
                lo_of(nc.vector, wfl, wf, wfh).then_inc(sem("wf_lo"), 1)

                def split_v(n):
                    for c in range(0, CH, 2):
                        e.wait_ge(sem("wv_hi"), n * 4 + c // 2 + 1)
                        lo_of(nc.vector, wvl[n][:, c:c + 2, :], wv[n][:, c:c + 2, :], wvh[n][:, c:c + 2, :]).then_inc(sem("wv_lo"), 1)
                split_v(0)
                nc.vector.memset(onesw, 1.0).then_inc(sem("onesw"), 1)
                for j in range(2):
                    e.wait_ge(sem(f"mod_st{j}"), 16 * 6)
                for q in range(1, 2 * NT, 2):
                    n, t = q // NT, q % NT
                    e.wait_ge(sem("v_mm"), q + 1)
                    copy(vtok[:, t, 512 * n:512 * (n + 1)], PS[:, q % 4, :]).then_inc(sem("v_evD"), 1)
                    if q == 1:
                        e.wait_ge(sem("fa"), 1)
                        ts(lf, fz, 0.0, None, ALU.min).then_inc(sem("lf0"), 1)
                        e.wait_ge(sem("fa"), 3)
                        e.wait_ge(sem("lf0"), 1)
                        tt(lf, lf, fa, ALU.subtract).then_inc(sem("lf"), 1)
                    if q == 3:
                        split_v(1)
                    if q == 7:
                        e.wait_ge(sem("lfT_ps"), 1)
                        copy(lfT[:].rearrange("p t h -> p (t h)"), PS[:, 7, 0:NT * H]).then_inc(sem("lfT"), 1)
                        e.wait_ge(sem("lf"), 1)
                        e.wait_ge(sem("onesw"), 1)
                        nc.vector.tensor_tensor_scan(Fp, onesw, lf[:, 0:SEQ], 0.0, ALU.mult, ALU.add).then_inc(sem("Fp"), 1)
                e.wait_ge(sem("w0_hi"), 1)
                lo_of(nc.vector, wql, wq, wqh).then_inc(sem("w0_lo"), 1)
                e.wait_ge(sem("w0_hi"), 2)
                lo_of(nc.vector, wkl, wk, wkh).then_inc(sem("w0_lo"), 1)
                copy(Fs[:, :, PAST:LK], lf[:, SEQ:TOK].rearrange("p (b t) -> p b t", b=DB)).then_inc(sem("Fs_new"), 1)
                e.wait_ge(sem("Fs_old"), 1)
                e.wait_ge(sem("Fs_new"), 1)
                for b in range(DB):
                    nc.vector.tensor_tensor_scan(Fso[:, b, :], onesw[:, 0:LK], Fs[:, b, :], 0.0, ALU.mult, ALU.add).then_inc(sem("F_made"), 1)
                for n in range(G3):
                    e.wait_ge(sem("k0_mm"), n + 1)
                    copy(kb[0][:, n * NG:(n + 1) * NG], PS[:, 1 + 2 * n, 0:NG]).then_inc(sem("k0_ev"), 1)

            @block.tensor
            def _(e):
                e.wait_ge(sem("pool_setup"), 8)
                e.wait_ge(sem("c_silu"), 1)
                for c in range(CH):
                    last = tr(PS[:, 0, c * NC_:(c + 1) * NC_], crow[:, c * P:(c + 1) * P], ident[0:NC_, 0:NC_])
                last.then_inc(sem("cT_ps"), 1)
                e.wait_ge(sem("cT"), 1)

                def modulation(j, i):
                    e.wait_ge(sem(f"mod_row{j}"), i)
                    e.wait_ge(sem(f"mod_w{j}"), i * 16 + 16)
                    product(PS[0:NC_, 2 + j, :], lambda c: cT[:, c, :], lambda c: wmod_r[j][:, c, :]).then_inc(sem(f"mod_mm{j}"), 1)
                for i in range(2):
                    for j in range(2):
                        modulation(j, i)
                e.wait_ge(sem("p_in"), 16 * 8)
                for c in range(CH):
                    last = tr(PS[:, 1, c * NR:(c + 1) * NR], prow[:, c * P:(c + 1) * P], ident[0:NR, 0:NR])
                last.then_inc(sem("pT_ps"), 1)

                def turn_tile(j, n):
                    e.wait_ge(sem(f"xn_made{j}"), n + 1)
                    e.wait_ge(sem(f"h_evA{j}"), n)
                    e.wait_ge(sem(f"h_evD{j}"), n)
                    for c in range(CH):
                        last = tr(PS[:, 4 + 2 * j + c // 4, (c % 4) * P:(c % 4 + 1) * P], xn[j][:, c * P:(c + 1) * P], ident[:])
                    last.then_inc(sem(f"xn_T{j}"), 1)
                with e.Fori(0, PT_ // 2) as i:
                    for j in range(2):
                        modulation(j, i + 2)
                        turn_tile(j, i)
                turn_tile(0, PT_ // 2)

                for s, n in (("h_evA0", 5), ("h_evD0", 5), ("h_evA1", 4), ("h_evD1", 4)):
                    e.wait_ge(sem(s), n)
                e.wait_ge(sem("pT"), 1)
                e.wait_ge(sem("wf_lo"), 1)
                for n in range(G3):
                    cols = slice(n * NG, (n + 1) * NG)
                    product3(PS[:, 4 + n, 0:NG], lambda c: wfh[:, c, :], lambda c: wfl[:, c, :],
                             lambda c: hTh[:, c, cols], lambda c: hTl[:, c, cols]).then_inc(sem("f_mm"), 1)
                for n in range(2):
                    for t in range(NT):
                        q = n * NT + t
                        if q >= 4:
                            e.wait_ge(sem("v_evD" if q % 2 else "v_evA"), (q - 4) // 2 + 1)
                        cols = slice(t * P, (t + 1) * P)
                        product3(PS[:, q % 4, :], lambda c: hTh[:, c, cols], lambda c: hTl[:, c, cols],
                                 lambda c: wvh[n][:, c, :], lambda c: wvl[n][:, c, :],
                                 lambda c: e.wait_ge(sem("wv_lo"), n * 4 + c // 2 + 1) if t == 0 else None).then_inc(sem("v_mm"), 1)
                        if q == 6:
                            e.wait_ge(sem("lf"), 1)
                            for k in range(NT):
                                last = tr(PS[:, 7, k * H:(k + 1) * H], lf[:, k * P:(k + 1) * P], ident[0:H, 0:H])
                            last.then_inc(sem("lfT_ps"), 1)
                e.wait_ge(sem("clf_in"), 16 * DB)
                e.wait_ge(sem("v_evA"), NT)
                e.wait_ge(sem("v_evD"), NT)
                for b in range(DB):
                    for k in range(2):
                        last = tr(PS[0:H, b // 2, (b % 2) * PAST + k * P:(b % 2) * PAST + (k + 1) * P], clf[:, b, k, :], ident[:])
                last.then_inc(sem("clf_ps"), 1)
                e.wait_ge(sem("Fs_old"), 1)
                for g in range(2 * G3):
                    if g % G3 == 0:
                        e.wait_ge(sem("w0_lo"), g // G3 + 1)
                    if g >= G3:
                        e.wait_ge(sem("q0_ev"), g - G3 + 1)
                    pair_product(g >= G3, g % G3).then_inc(sem("k0_mm" if g >= G3 else "q0_mm"), 1)
        clear_semaphores()

        with nc.Block() as block:

            @block.sync
            def _(e):
                count = e.alloc_register("count")
                for hh in range(P // DS):
                    e.dma_start(causal16[hh * DS:(hh + 1) * DS, :], causal[0:DS, 0:DS]).then_inc(sem("c16_in"), 16)
                def pair_weights(p):
                    e.dma_start(wq, w_in[:, :, bass.ds(p * P + W_Q, P)]).then_inc(sem("qk_w"), 16)
                    e.dma_start(wk, w_in[:, :, bass.ds(p * P + W_K, P)]).then_inc(sem("qk_w"), 16)

                def pair_sums(p, j):
                    for hh in range(2):
                        e.dma_start(Bt[j][:, hh, :], spread(F_d[bass.ds(p * 2 + hh, 1), :])).then_inc(sem(f"Bt_in{j}"), 16)

                def pair(i, j, more):
                    p = i * 2 + j
                    if more:
                        e.wait_ge(sem("kg_mm"), p * 3)
                        pair_weights(p + 1)
                    e.reg_mov(count, p + 1)
                    e.wait_ge(sem("kst_A"), p * 2 + 2)
                    e.wait_ge(sem("kst_D"), count)
                    e.dma_start(k_p[0, 0].rearrange("(t p) h d -> p t (h d)", p=P)[:, :, bass.ds(p * P, P)], kst[:, 0:PT_, :]).then_inc(sem("k_out"), 16)
                    e.dma_start(k_s[0].rearrange("b t h d -> (b t) (h d)")[:, bass.ds(p * P, P)], kst[:, PT_, :]).then_inc(sem("k_out"), 16)
                    e.dma_start(yb_d[bass.ds(p * (NE * P // CH) + NA, NE * P // CH), :].rearrange("(p s) (k n) -> p (s k) n", p=P, n=P),
                                ones[:].rearrange("p (a n) -> p a n", a=1).broadcast_to([P, NE, P])).then_inc(sem("yb_fill"), 16)
                    for r in range(4):
                        e.reg_mov(count, p * 8 + 2 * r + 2)
                        e.wait_ge(sem("k_out"), 32)
                        e.wait_ge(sem("ot_ev"), count)
                        e.dma_start(oa_d[bass.ds(p * P, P), (6 - 2 * r) * P:(8 - 2 * r) * P], ob[r % 2]).then_inc(sem(f"oa_st{r % 2}"), 16)
                    if more == 2:
                        e.wait_ge(sem("ttr"), p * 16 + 16)
                        pair_sums(p + 2, j)
                pair_sums(0, 0)
                pair_sums(1, 1)
                with e.Fori(0, CH // 2 - 1) as i:
                    pair(i, 0, 2)
                    pair(i, 1, 2)
                pair(CH // 2 - 1, 0, 1)
                pair(CH // 2 - 1, 1, 0)
                e.wait_ge(sem("k_out"), CH * 32)
                e.wait_ge(sem("yb_fill"), 16 * CH)
                e.wait_ge(sem("ot_ev"), CH * 8)
                e.wait_ge(sem("qs_cp"), CH * 2)
                for s in range(2):
                    e.wait_ge(sem(f"oa_st{s}"), CH * 2 * 16)

                def sample_loads(i, j, first):
                    b = i * 2 + j
                    if not first:
                        e.wait_ge(sem("kc_ps"), b * 2 - 2)
                    e.dma_start(kc[j], a["cache_k"][0, bass.ds(b, 1)].rearrange("a (t p) h d -> p (a t) (h d)", p=P)).then_inc(sem(f"sk_in{j}"), 16)
                    if not first:
                        e.wait_ge(sem("s_ttr"), b * 2 - 2)
                    e.dma_start(Bs[j].rearrange("p g l -> p (g l)"),
                                Fs_d[bass.ds(b, 1)].rearrange("a h g l -> (a h) (g l)").unsqueeze(1).broadcast_to([H // 2, DS, 2 * LK])).then_inc(sem(f"sB_in{j}"), 16)
                    if not first:
                        e.wait_ge(sem(f"spv{j}"), i)
                    e.dma_start(vc[j], a["cache_v"][0, bass.ds(b, 1)].rearrange("a (t p) h d -> p (a t) (h d)", p=P)).then_inc(sem(f"sv_in{j}"), 16)
                    e.dma_start(v16[j], v_s[0, bass.ds(b, 1)].rearrange("a t h d -> (a t) (h d)")).then_inc(sem(f"sv_in{j}"), 16)
                for j in range(2):
                    sample_loads(0, j, True)
                with e.Fori(1, DB // 2) as i:
                    for j in range(2):
                        sample_loads(i, j, False)
                def panels(m):
                    for k, (s, off) in enumerate((("xb_mm", W_X), ("gb_mm", W_G))):
                        if m is not None:
                            e.wait_ge(sem(s), m * 3)
                        e.dma_start(wx[k], w_in[:, :, bass.ds((0 if m is None else m) * P + off, P)]).then_inc(sem(f"wx_in{k}"), 16)

                def blocks(i, j):
                    e.wait_ge(sem(f"ri_done{j}"), i)
                    for k, nm in enumerate(("w_r", "w_i")):
                        for q in range(2):
                            e.dma_start(bw[j][q * HD:(q + 1) * HD, k, q * HD:(q + 1) * HD],
                                        a[nm][0, bass.ds((i * 2 + j) * 2 + q, 1)].rearrange("a c d -> (a c) d")).then_inc(sem(f"bw_in{j}"), 16)
                e.wait_ge(sem("spv0"), DB // 2)
                panels(None)
                e.wait_ge(sem("so_A"), DB)
                e.wait_ge(sem("so_D"), DB)
                e.dma_start(oa_d.rearrange("(c p) t -> p c t", p=P)[:, :, SEQ:TOK], oas).then_inc(sem("oas_st"), 16)
                e.wait_ge(sem("bw_zero"), 2)
                with e.Fori(0, CH // 2 - 1) as i:
                    for j in range(2):
                        blocks(i, j)
                        panels(i * 2 + j + 1)
                blocks(CH // 2 - 1, 0)
                panels(CH - 1)
                blocks(CH // 2 - 1, 1)
                e.wait_ge(sem("oas_st"), 16)

                def panel(n, m, q):
                    w, off = ((w_gate, 0), (w_gate, D), (w_pa, 0), (w_pb, 0))[q]
                    e.dma_start(wm[q], w[:, :, bass.ds(m * P + off, P)]).then_inc(sem(f"wm_in{q}"), 16)

                def group(n):
                    e.dma_start(oa, oa_d.rearrange("(c p) t -> p c t", p=P)[:, :, n * NG:(n + 1) * NG]).then_inc(sem("oa_in"), 16)
                for q, s in enumerate(("xb_mm", "gb_mm")):
                    e.wait_ge(sem(s), CH * 3)
                    panel(0, 0, q)
                for j in range(2):
                    e.wait_ge(sem(f"y_made{j}"), CH // 2)
                    e.wait_ge(sem(f"tails{j}"), CH)
                for q in (2, 3):
                    panel(0, 0, q)
                    if q == 2:
                        group(0)
                for n in range(G3):
                    if n:
                        for q in range(4):
                            e.wait_ge(sem(f"wm_mm{q}"), n * CH)
                            panel(n, 0, q)
                            if q == 2:
                                group(n)

                    def panels4(m):
                        for q in range(4):
                            e.wait_ge(sem(f"wm_mm{q}"), n * CH + m)
                            panel(n, m, q)
                    early = ((G1, 2), (A2, 4), (B2, 3)) if n == G3 - 1 else ()
                    if early:
                        e.dma_start(wo[0], w_out[:, :, 0:512]).then_inc(sem("early_in"), 16)
                    for m, (dst, piece) in enumerate(early, 1):
                        panels4(m)
                        mod_load(e, dst, piece, "early_in")
                    with e.Fori(1 + len(early), CH) as m:
                        panels4(m)
                e.wait_ge(sem("early_in"), 16 + 3 * MOD_LOAD)

            @block.gpsimd
            def _(e):
                def split_qk(p):
                    for k, (hi_, w, lo_) in enumerate(((wqh, wq, wql), (wkh, wk, wkl))):
                        e.wait_ge(sem("qk_hi"), p * 2 + k - 1)
                        lo_of(e, lo_, w, hi_).then_inc(sem("qk_lo"), 1)

                def pair(i, j, more):
                    p = i * 2 + j
                    if more:
                        split_qk(p + 1)
                    e.wait_ge(sem("q_ev"), p * 3)
                    e.tensor_copy(qTs[:, bass.ds(p, 1), :], qb[j][:, SEQ:TOK].rearrange("p (a n) -> p a n", a=1)).then_inc(sem("qs_cp"), 1)
                    e.wait_ge(sem("k_ev"), p * 3)
                    e.tensor_copy(kTs[:, bass.ds(p, 1), :], kb[j][:, SEQ:TOK].rearrange("p (a n) -> p a n", a=1)).then_inc(sem("qs_cp"), 1)
                with e.Fori(0, CH // 2 - 1) as i:
                    for j in range(2):
                        pair(i, j, True)
                pair(CH // 2 - 1, 0, True)
                pair(CH // 2 - 1, 1, False)
                e.wait_ge(sem("ot_ev"), CH * 8)
                e.wait_ge(sem("k_out"), CH * 32)
                for j in range(2):
                    e.memset(qbd[j], 0.0).then_inc(sem("qbd_zero"), 1)
                e.wait_ge(sem("qbd_zero"), 2)
                e.wait_ge(sem("qs_cp"), CH * 2)
                with e.Fori(0, DB // 2) as i:
                    for j in range(2):
                        b = i * 2 + j
                        e.wait_ge(sem(f"sqk{j}"), i * 2)
                        cols = bass.ds(b * DS, DS)
                        e.wait_ge(sem(f"qbd{1 - j}"), (i + j) * 3)
                        e.tensor_copy(qbd[j][0:HD, :, 0:DS], qTs[0:HD, :, cols]).then_inc(sem(f"qbd{j}"), 1)
                        e.tensor_copy(qbd[j][HD:P, :, DS:2 * DS], qTs[HD:P, :, cols]).then_inc(sem(f"qbd{j}"), 1)
                        e.wait_ge(sem(f"qbd{j}"), i * 3 + 2)
                        e.tensor_copy(kcT[j][:, :, PAST:LK], kTs[:, :, cols]).then_inc(sem(f"qbd{j}"), 1)
                def split_x(k, m):
                    e.wait_ge(sem(f"wx_hi{k}"), m + 1)
                    lo_of(e, wxl[k], wx[k], wxh[k]).then_inc(sem(f"wx_lo{k}"), 1)
                for k in range(2):
                    split_x(k, 0)
                e.wait_ge(sem("so_A"), DB)
                e.wait_ge(sem("so_D"), DB)
                for j in range(2):
                    e.memset(bw[j], 0.0).then_inc(sem("bw_zero"), 1)
                    e.memset(xbuf[j][:, 0:3], 0.0).then_inc(sem("bw_zero2"), 1)

                def pads(i, j):
                    m = i * 2 + j
                    e.wait_ge(sem(f"conv{j}"), i)
                    e.tensor_copy(xbs[j][:, :, 0:3], pT[:, bass.ds(m, 1), R_CV:NR].rearrange("p a (b k) -> p (a b) k", b=DB)).then_inc(sem(f"xpad{j}"), 1)
                    e.wait_ge(sem(f"xb_ev{j}"), i * 4 + 4)
                    e.wait_ge(sem(f"xpad{j}"), i + 1)
                    e.tensor_copy(hc[:, bass.ds(m, 1), 9:12], xbuf[j][:, SEQ:SEQ + 3].rearrange("p (a n) -> p a n", a=1)).then_inc(sem(f"tails{j}"), 1)
                    e.wait_ge(sem(f"tails{j}"), i * 2 + 1)
                    e.tensor_copy(hc[:, bass.ds(m, 1), 12:36].rearrange("p a (b k) -> p (a b) k", b=DB), xbs[j][:, :, DS:DS + 3]).then_inc(sem(f"tails{j}"), 1)
                    e.wait_ge(sem(f"tails{j}"), i * 2 + 2)
                pads(0, 0)
                for k in range(2):
                    split_x(k, 1)
                with e.Fori(0, CH // 2 - 1) as i:
                    pads(i, 1)
                    for k in range(2):
                        split_x(k, i * 2 + 2)
                    pads(i + 1, 0)
                    for k in range(2):
                        split_x(k, i * 2 + 3)
                pads(CH // 2 - 1, 1)
                count = e.alloc_register("count")
                for n in range(G3):
                    with e.Fori(0, CH // 2) as i:
                        for j in range(2):
                            e.wait_ge(sem(f"mixd{j}"), n * CH // 2 + i + 1)
                            e.tensor_tensor(tm[j][0], tm[j][0], tm[j][1], ALU.add).then_inc(sem(f"mixa{j}"), 1)
                            e.reg_mov(count, n * CH // 2 + i + 1)
                            e.wait_ge(sem("hrow"), 1)
                            e.wait_ge(sem(f"mixa{j}"), count)
                            e.dma_start(mix_d[bass.ds(i * 256 + j * P, P), n * NG:(n + 1) * NG], tm[j][0]).then_inc(sem(f"mix_st{j}"), 16)
                for j in range(2):
                    e.wait_ge(sem(f"mix_st{j}"), G3 * CH // 2 * 16)

            @block.scalar
            def _(e):
                count = e.alloc_register("count")
                def split_qk(p):
                    for hi_, w in ((wqh, wq), (wkh, wk)):
                        e.wait_ge(sem("qk_w"), p * 32)
                        act(hi_, w, ACT.Copy).then_inc(sem("qk_hi"), 1)

                def put_q(i, j, n):
                    e.wait_ge(sem("qg_mm"), (i * 2 + j) * 3 + n - 2)
                    act(qb[j][:, n * NG:(n + 1) * NG], PS[:, 1 + 2 * n, 0:NG], ACT.Copy, scale=-(HD ** -0.5)).then_inc(sem("q_ev"), 1)

                def pair(i, j, more):
                    p = i * 2 + j
                    following = (i, 1) if j == 0 else (i + 1, 0)
                    e.wait_ge(sem("kt_ps"), p * 3 + 1)
                    e.wait_ge(sem("k_out"), p * 32)
                    act(kst[:, 0:4, :], PS[:, 4, :].rearrange("p (t n) -> p t n", t=4), ACT.Copy).then_inc(sem("kst_A"), 1)
                    e.wait_ge(sem("kt_ps"), p * 3 + 3)
                    act(kst[:, 8, :], PS[:, 7, 0:P], ACT.Copy).then_inc(sem("kst_A"), 1)

                    def norm(u):
                        k, hh = u // 2, u % 2
                        e.wait_ge(sem("recip"), p * 16 + u + 1)
                        e.wait_ge(sem("pv_mm"), p * 16 + u + 1)
                        if k >= 2:
                            e.wait_ge(sem("ot_mm"), p * 8 + k - 1)
                        act(ot[k % 2][:, hh * HD:(hh + 1) * HD], PS[:, 6, (u % 4) * HD:(u % 4 + 1) * HD], ACT.Copy, scale=rl[:, u:u + 1]).then_inc(sem("norm"), 1)
                    for u in range(16):
                        n = (8 - u // 2) * P
                        e.wait_ge(sem("ttr"), p * 16 + u + 1)
                        act(sP[u % 3][:, 0:n], sP[u % 3][:, 0:n], ACT.Exp, scale=-1.0, bias=mn[:, u:u + 1], accum_out=ls[:, u:u + 1]).then_inc(sem("exp"), 1)
                        if u >= 1 and 7 - (u - 1) // 2 >= 4:
                            m = (8 - (u - 1) // 2) * P - 512
                            e.wait_ge(sem("t1_mm"), p * 8 + u)
                            if u >= 3:
                                e.wait_ge(sem("pv_mm"), p * 16 + u - 2)
                            act(PTb[(u - 1) % 2][:, 512:512 + m], PS[:, 5, 0:m], ACT.Copy).then_inc(sem("evB"), 1)
                        if u >= 2:
                            norm(u - 2)
                        if more and u == 4:
                            split_qk(p + 1)
                        if more and 11 <= u < 14:
                            if u == 11:
                                e.wait_ge(sem("qs_cp"), p * 2)
                            put_q(*following, u - 11)
                    norm(14)
                    norm(15)
                with e.Fori(0, CH // 2 - 1) as i:
                    pair(i, 0, True)
                    pair(i, 1, True)
                pair(CH // 2 - 1, 0, True)
                pair(CH // 2 - 1, 1, False)

                e.wait_ge(sem("qs_cp"), CH * 2)

                def put_keys(i, j):
                    e.wait_ge(sem("kc_ps"), (i * 2 + j) * 2 + 1)
                    act(kcT[j][:, 0:4, 0:PAST], banks(0, 2).rearrange("p (c n) -> p c n", c=4), ACT.Copy).then_inc(sem("kc_A"), 1)

                def exps(i, j):
                    for g in range(2):
                        e.wait_ge(sem("s_ttr"), (i * 2 + j) * 2 + g + 1)
                        act(sS[j][:, g, :], sS[j][:, g, :], ACT.Exp, scale=-1.0, bias=mn[:, 2 * j + g:2 * j + g + 1],
                            accum_out=ls[:, 2 * j + g:2 * j + g + 1]).then_inc(sem("s_exp"), 1)

                def put_o(i, j):
                    b = i * 2 + j
                    e.reg_mov(count, b + 1)
                    e.wait_ge(sem("ot_ev"), CH * 8)
                    e.wait_ge(sem("ot2_mm"), count)
                    act(oas[0:HD, :, bass.ds(b * DS, DS)], PS[0:HD, 7, 256:512].rearrange("p (c n) -> p c n", c=CH)[:, :, 0:DS], ACT.Copy).then_inc(sem("so_A"), 1)

                def batch(i, j, before, nxt):
                    b = i * 2 + j
                    if nxt:
                        put_keys(*nxt)
                    for g in range(2):
                        e.wait_ge(sem("s_tp"), b * 2 + g + 1)
                        act(PTs[j][:, g, 0:2, :], PS[:, 6, 0:2 * P].rearrange("p (k n) -> p k n", k=2), ACT.Copy).then_inc(sem("s_ptA"), 1)
                    if before:
                        put_o(*before)
                    if nxt:
                        exps(*nxt)
                    e.wait_ge(sem(f"spv{j}"), i + 1)
                    if before:
                        e.wait_ge(sem("so_D"), b)
                    act(osb[j].rearrange("p g n -> p (g n)"), PS[:, 7, 0:256], ACT.Copy).then_inc(sem("o_ev"), 1)
                put_keys(0, 0)
                exps(0, 0)
                batch(0, 0, None, (0, 1))
                with e.Fori(0, DB // 2 - 1) as i:
                    batch(i, 1, (i, 0), (i + 1, 0))
                    batch(i + 1, 0, (i, 1), (i + 1, 1))
                batch(DB // 2 - 1, 1, (DB // 2 - 1, 0), None)
                def split_x(k, m):
                    e.wait_ge(sem(f"wx_in{k}"), m * 16 + 16)
                    act(wxh[k], wx[k], ACT.Copy).then_inc(sem(f"wx_hi{k}"), 1)
                for k in range(2):
                    split_x(k, 0)
                put_o(DB // 2 - 1, 1)

                def gates(i, j):
                    m = i * 2 + j
                    e.wait_ge(sem("scan"), m)
                    for n in range(G3):
                        b = (6, 0, 6)[n]
                        e.reg_mov(count, m * 2 + n + 1 if n < 2 else i + 1)
                        e.wait_ge(sem("bw_zero2"), 2)
                        e.wait_ge(sem("ri_mm" if n < 2 else f"ri_done{j}"), count)
                        cols = slice(n * NG, (n + 1) * NG)
                        act(rr[:, cols], PS[:, b, 0:NG], ACT.Sigmoid, bias=pT[:, bass.ds(m, 1), R_BR]).then_inc(sem("sig"), 1)
                        act(ii[:, cols], PS[:, b + 1, 0:NG], ACT.Sigmoid, bias=pT[:, bass.ds(m, 1), R_BI]).then_inc(sem("sig"), 1)
                    e.reg_mov(count, m * 6 + 6)
                    e.wait_ge(sem("bw_zero2"), 2)
                    e.wait_ge(sem("sig"), count)
                    act(Rr, rr, ACT.Exp, scale=sp8[:, bass.ds(m, 1)]).then_inc(sem("decay"), 1)
                    e.reg_mov(count, m + 1)
                    e.wait_ge(sem("bw_zero2"), 2)
                    e.wait_ge(sem("decay"), count)
                    act(rr, rr, ACT.Tanh, scale=sp4[:, bass.ds(m, 1)]).then_inc(sem("tanh"), 1)
                    e.wait_ge(sem("tanh"), m + 1)
                    act(rr, rr, ACT.Sqrt).then_inc(sem("root"), 1)

                def step(new, old, more=True):
                    if new:
                        i, j = new
                        m = i * 2 + j
                        e.wait_ge(sem(f"conv{j}"), i)
                        e.wait_ge(sem(f"tails{j}"), i * 2)
                        for n in range(G3):
                            e.wait_ge(sem("xb_mm"), m * 3 + n + 1)
                            if n < 2:
                                act(xbuf[j][:, 3 + n * NG:3 + (n + 1) * NG], PS[:, n, 0:NG], ACT.Copy).then_inc(sem(f"xb_ev{j}"), 1)
                            else:
                                act(xbuf[j][:, 3 + n * NG:3 + SEQ], PS[:, n, 0:SEQ - n * NG], ACT.Copy).then_inc(sem(f"xb_ev{j}"), 1)
                                act(xbs[j][:, :, 3:3 + DS], PS[:, n, SEQ - n * NG:NG].rearrange("p (b t) -> p b t", b=DB), ACT.Copy).then_inc(sem(f"xb_ev{j}"), 1)
                        if more:
                            split_x(0, m + 1)
                    if old:
                        gates(*old)
                    if new:
                        e.wait_ge(sem(f"y_made{j}"), i)
                        for n in range(G3):
                            e.wait_ge(sem("gb_mm"), m * 3 + n + 1)
                            act(gel[j][:, n * NG:(n + 1) * NG], PS[:, 3 + n, 0:NG], ACT.Gelu_apprx_tanh).then_inc(sem(f"gb_ev{j}"), 1)
                        if more:
                            split_x(1, m + 1)
                e.wait_ge(sem("bw_zero2"), 2)
                step((0, 0), None)
                with e.Fori(0, CH // 2 - 1) as i:
                    step((i, 1), (i, 0))
                    step((i + 1, 0), (i, 1))
                step((CH // 2 - 1, 1), (CH // 2 - 1, 0), False)

                def split_m(q, m):
                    e.wait_ge(sem(f"wm_in{q}"), m * 16 + 16)
                    act(wmh[q], wm[q], ACT.Copy).then_inc(sem(f"wm_hi{q}"), 1)
                split_m(0, 0)
                split_m(1, 0)
                step(None, (CH // 2 - 1, 1))
                e.wait_ge(sem("oas_st"), 16)
                e.wait_ge(sem("hc_ps"), 1)
                act(hrow, banks(6, 2, 36), ACT.Copy).then_inc(sem("hrow"), 1)
                e.wait_ge(sem("hrow"), 1)
                e.dma_start(h_p[0], hrow[0:1, :]).then_inc(sem("hc_out"), 16)
                e.dma_start(h_s[0], hrow[1:9, :]).then_inc(sem("hc_out"), 16)
                e.dma_start(cv_p[0, 0], hrow[9:12, :]).then_inc(sem("hc_out"), 16)
                e.dma_start(cv_s[0].rearrange("b k d -> (b k) d"), hrow[12:36, :]).then_inc(sem("hc_out"), 16)
                split_m(2, 0)

                def gate(n, i, j, q):
                    m = n * CH + i * 2 + j
                    e.reg_mov(count, m + 1)
                    e.wait_ge(sem("hrow"), 1)
                    e.wait_ge(sem(f"wm_mm{q}"), count)
                    act(sg[j][q], PS[:, 4 * j + BANK[q], 0:NG], ACT.Sigmoid, bias=pT[:, bass.ds(i * 2 + j, 1), R_BG + q]).then_inc(sem("sg"), 1)

                def chunk(n, i, j, more=True):
                    m = n * CH + i * 2 + j
                    split_m(3, m)
                    e.wait_ge(sem(f"mixd{j}"), n * CH // 2 + i)
                    gate(n, i, j, 0)
                    if more:
                        split_m(0, m + 1)
                    gate(n, i, j, 1)
                    if more:
                        split_m(1, m + 1)
                        split_m(2, m + 1)
                for n in range(G3):
                    e.wait_ge(sem("oa_in"), n * 16 + 16)
                    for c in range(0, CH, 2):
                        act(oah[:, c:c + 2, :], oa[:, c:c + 2, :], ACT.Copy).then_inc(sem("oa_hi"), 1)
                    e.wait_ge(sem("wm_mm3"), n * CH) if n else e.wait_ge(sem("y_made1"), CH // 2)
                    for c in range(0, CH, 2):
                        act(obh[:, c:c + 2, :], obT[:, c:c + 2, n * NG:(n + 1) * NG], ACT.Copy).then_inc(sem("ob_hi"), 1)
                    last = n == G3 - 1
                    with e.Fori(0, CH // 2 - last) as i:
                        for j in range(2):
                            chunk(n, i, j)
                chunk(G3 - 1, CH // 2 - 1, 0)
                chunk(G3 - 1, CH // 2 - 1, 1, False)
                e.wait_ge(sem("hc_out"), 64)

            @block.vector
            def _(e):
                count, count2 = e.alloc_register("count"), e.alloc_register("count2")
                def put_k(i, j, n):
                    e.wait_ge(sem("kg_mm"), (i * 2 + j) * 3 + n - 2)
                    copy(kb[j][:, n * NG:(n + 1) * NG], PS[:, 1 + 2 * n, 0:NG]).then_inc(sem("k_ev"), 1)

                def pair(i, j, more):
                    p = i * 2 + j
                    following = (i, 1) if j == 0 else (i + 1, 0)
                    e.wait_ge(sem("kt_ps"), p * 3 + 2)
                    e.wait_ge(sem("k_out"), p * 32)
                    copy(kst[:, 4:8, :], PS[:, 5, :].rearrange("p (t n) -> p t n", t=4)).then_inc(sem("kst_D"), 1)
                    e.wait_ge(sem(f"Bt_in{j}"), i * 32 + 32)

                    def recip_and_turned(u):
                        m = min(8 - u // 2, 4) * P
                        e.wait_ge(sem("exp"), p * 16 + u + 1)
                        nc.vector.reciprocal(rl[:, u:u + 1], ls[:, u:u + 1]).then_inc(sem("recip"), 1)
                        e.wait_ge(sem("t0_mm"), p * 16 + u + 1)
                        if u >= 2:
                            e.wait_ge(sem("pv_mm"), p * 16 + u - 1)
                        copy(PTb[u % 2][:, 0:m], PS[:, 4, 0:m]).then_inc(sem("evA"), 1)

                    def put_o(k):
                        e.wait_ge(sem("ot_mm"), p * 8 + k + 1)
                        s = k // 2 % 2
                        if k % 2 == 0:
                            e.wait_ge(sem(f"oa_st{s}"), (p * 2 + k // 4) * 16)
                        copy(ob[s][:, (1 - k % 2) * P:(2 - k % 2) * P], PS[:, 7, (k % 4) * P:(k % 4 + 1) * P]).then_inc(sem("ot_ev"), 1)
                    for u in range(16):
                        r, hh = 7 - u // 2, u % 2
                        n = (r + 1) * P
                        if u < 2:
                            e.wait_ge(sem("kst_D"), p + 1)
                        else:
                            e.wait_ge(sem("ttr"), p * 16 + u - 1)
                        tt(Bt[j][:, hh, r * P:n], Bt[j][:, hh, r * P:n], causal[:], ALU.add).then_inc(sem("mask"), 1)
                        if u >= 3:
                            e.wait_ge(sem("t0_mm"), p * 16 + u - 2)
                        if 3 <= u < 11:
                            e.wait_ge(sem("t1_mm"), p * 8 + u - 2)
                        e.reg_mov(count, p * 16 + u + 1)
                        e.wait_ge(sem(f"Bt_in{j}"), 32)
                        e.wait_ge(sem("mask"), count)
                        e.wait_ge(sem("s_mm"), count)
                        nc.vector.tensor_tensor_reduce(out=sP[u % 3][:, 0:n], in0=banks(2 * (u % 2), 2)[:, 0:n], in1=Bt[j][:, hh, 0:n], scale=1.0, scalar=BIG,
                                                       op0=ALU.add, op1=ALU.min, accum_out=mn[:, u:u + 1]).then_inc(sem("ttr"), 1)
                        if u >= 1:
                            recip_and_turned(u - 1)
                        if u >= 4 and u % 2 == 0:
                            put_o((u - 4) // 2)
                        if more and u >= 14:
                            if u == 14:
                                e.wait_ge(sem("qs_cp"), p * 2)
                            put_k(*following, u - 14)
                    recip_and_turned(15)
                    if more:
                        put_k(*following, 2)
                    put_o(6)
                    put_o(7)
                with e.Fori(0, CH // 2 - 1) as i:
                    pair(i, 0, True)
                    pair(i, 1, True)
                pair(CH // 2 - 1, 0, True)
                pair(CH // 2 - 1, 1, False)

                e.wait_ge(sem("c16_in"), 16 * (P // DS))

                def put_keys(i, j):
                    b = i * 2 + j
                    e.wait_ge(sem("kc_ps"), b * 2 + 2)
                    copy(kcT[j][:, 4:8, 0:PAST], banks(2, 2).rearrange("p (c n) -> p c n", c=4)).then_inc(sem("kc_D"), 1)
                    e.wait_ge(sem(f"sB_in{j}"), i * 16 + 16)
                    tt(Bs[j][:, :, PAST:LK], Bs[j][:, :, PAST:LK], causal16[:].rearrange("p (a n) -> p a n", a=1).broadcast_to([P, 2, DS]), ALU.add).then_inc(sem("s_mask"), 1)

                def scores(i, j):
                    for g in range(2):
                        q = 2 * j + g
                        e.reg_mov(count, i * 2 + j + 1)
                        e.reg_mov(count2, i * 2 + g + 1)
                        e.wait_ge(sem("c16_in"), 16 * (P // DS))
                        e.wait_ge(sem("s_mask"), count)
                        e.wait_ge(sem(f"sqk{j}"), count2)
                        nc.vector.tensor_tensor_reduce(out=sS[j][:, g, :], in0=PS[:, 4 + g, 0:LK], in1=Bs[j][:, g, :], scale=1.0, scalar=BIG,
                                                       op0=ALU.add, op1=ALU.min, accum_out=mn[:, q:q + 1]).then_inc(sem("s_ttr"), 1)

                def put_probs(b, j, g):
                    e.wait_ge(sem("s_ptA"), b * 2 + g + 1)
                    e.wait_ge(sem("s_tp"), b * 2 + g + 1)
                    copy(PTs[j][0:DS, g, 2, :], PS[0:DS, 6, 2 * P:3 * P]).then_inc(sem("s_ptD"), 1)

                def put_o(i, j):
                    b = i * 2 + j
                    e.wait_ge(sem("ot2_mm"), b + 1)
                    copy(oas[HD:P, :, bass.ds(b * DS, DS)], PS[HD:P, 7, 256:512].rearrange("p (c n) -> p c n", c=CH)[:, :, DS:2 * DS]).then_inc(sem("so_D"), 1)

                def batch(i, j, before, nxt):
                    b = i * 2 + j
                    for g in range(2):
                        q = 2 * j + g
                        e.wait_ge(sem("s_exp"), b * 2 + g + 1)
                        nc.vector.reciprocal(rl[:, q:q + 1], ls[:, q:q + 1]).then_inc(sem("s_rl"), 1)
                        e.wait_ge(sem("s_rl"), b * 2 + g + 1)
                        ts(sS[j][:, g, :], sS[j][:, g, :], rl[:, q:q + 1], None, ALU.mult).then_inc(sem("s_pn"), 1)
                    if nxt:
                        put_keys(*nxt)
                    put_probs(b, j, 0)
                    if nxt:
                        scores(*nxt)
                    put_probs(b, j, 1)
                    if before:
                        put_o(*before)
                put_keys(0, 0)
                scores(0, 0)
                batch(0, 0, None, (0, 1))
                with e.Fori(0, DB // 2 - 1) as i:
                    batch(i, 1, (i, 0), (i + 1, 0))
                    batch(i + 1, 0, (i, 1), (i + 1, 1))
                batch(DB // 2 - 1, 1, (DB // 2 - 1, 0), None)
                put_o(DB // 2 - 1, 1)

                st = Steps(e, sem("dve_rnn"))

                def conv(i, j):
                    m = i * 2 + j
                    e.wait_ge(sem(f"xb_ev{j}"), i * 4 + 4)
                    e.wait_ge(sem(f"xpad{j}"), i + 1)
                    par = lambda r: pT[:, bass.ds(m, 1), r]
                    xcs = xc[j][:, SEQ:TOK].rearrange("p (b t) -> p b t", b=DB)
                    for k in range(4):
                        if k:
                            st.wait()
                        for dst, src in ((xc[j][:, 0:SEQ], xbuf[j][:, k:k + SEQ]), (xcs, xbs[j][:, :, k:k + DS])):
                            if k == 0:
                                st.did(ts(dst, src, par(R_CW), par(R_CB), ALU.mult, ALU.add))
                            elif k < 3 or dst is not xcs:
                                st.did(stt(out=dst, in0=src, scalar=par(R_CW + k), in1=dst, op0=ALU.mult, op1=ALU.add))
                            else:
                                stt(out=dst, in0=src, scalar=par(R_CW + k), in1=dst, op0=ALU.mult, op1=ALU.add).then_inc(sem(f"conv{j}"), 1)
                CONV = 7

                def recur(i, j):
                    m = i * 2 + j
                    e.wait_ge(sem("decay"), m + 1)
                    st.did(tt(ii, ii, xc[j], ALU.mult))
                    st.wait()
                    st.did(stt(out=ii, in0=Rr, scalar=1.0, in1=ii, op0=ALU.add, op1=ALU.mult))
                    e.wait_ge(sem("root"), m + 1)
                    st.wait()
                    st.did(tt(ii, ii, rr, ALU.mult))
                    st.wait()
                    a0 = Rr[:, SEQ:TOK].rearrange("p (b t) -> p b t", b=DB)[:, :, 0]
                    b0 = ii[:, SEQ:TOK].rearrange("p (b t) -> p b t", b=DB)[:, :, 0]
                    st.did(tt(t8[:], a0, pT[:, bass.ds(m, 1), R_H0:R_H0 + DB].rearrange("p a b -> p (a b)"), ALU.mult))
                    st.wait()
                    st.did(tt(b0, b0, t8[:], ALU.add))
                    st.did(nc.vector.memset(a0, 0.0))
                    st.wait()
                    e.wait_ge(sem("h_cp"), m * 2)
                    nc.vector.tensor_tensor_scan(hb, Rr, ii, 0.0, ALU.mult, ALU.add).then_inc(sem("scan"), 1)
                    e.wait_ge(sem("scan"), m + 1)
                    copy(hc[:, bass.ds(m, 1), 0:1], hb[:, SEQ - 1:SEQ].rearrange("p (a n) -> p a n", a=1)).then_inc(sem("h_cp"), 1)
                    copy(hc[:, bass.ds(m, 1), 1:9], hb[:, SEQ:TOK].rearrange("p (a b t) -> p a b t", a=1, b=DB)[:, :, :, DS - 1]).then_inc(sem("h_cp"), 1)
                    e.wait_ge(sem(f"gb_ev{j}"), i * 3 + 3)
                    e.wait_ge(sem("scan"), m + 1)
                    tt(obT[:, bass.ds(m, 1), :], hb.rearrange("p (a n) -> p a n", a=1), gel[j].rearrange("p (a n) -> p a n", a=1), ALU.mult).then_inc(sem(f"y_made{j}"), 1)
                RECUR = 6
                PER = 2 * (CONV + RECUR)
                conv(0, 0)
                with e.Fori(0, CH // 2 - 1) as i:
                    st.base, st.n = i * PER + CONV, 0
                    conv(i, 1)
                    recur(i, 0)
                    conv(i + 1, 0)
                    recur(i, 1)
                st.base, st.n = (CH // 2 - 1) * PER + CONV, 0
                conv(CH // 2 - 1, 1)
                recur(CH // 2 - 1, 0)

                def split_m(q, m):
                    e.wait_ge(sem(f"wm_hi{q}"), m + 1)
                    lo_of(nc.vector, wml[q], wm[q], wmh[q]).then_inc(sem(f"wm_lo{q}"), 1)
                split_m(0, 0)
                split_m(1, 0)
                recur(CH // 2 - 1, 1)

                split_m(2, 0)

                def gated(n, i, j, q):
                    m = n * CH + i * 2 + j
                    e.wait_ge(sem("sg"), m * 2 + q + 1)
                    e.wait_ge(sem(f"wm_mm{q + 2}"), m + 1)
                    tt(tm[j][q], PS[:, 4 * j + BANK[q + 2], 0:NG], sg[j][q], ALU.mult).then_inc(sem(f"mixd{j}" if q else "mixp"), 1)

                def chunk(n, i, j, more=True):
                    m = n * CH + i * 2 + j
                    split_m(3, m)
                    if more:
                        split_m(0, m + 1)
                        split_m(1, m + 1)
                    e.wait_ge(sem(f"mix_st{j}"), (n * CH // 2 + i) * 16)
                    gated(n, i, j, 0)
                    if more:
                        split_m(2, m + 1)
                    gated(n, i, j, 1)
                for n in range(G3):
                    for c in range(0, CH, 2):
                        e.wait_ge(sem("oa_hi"), n * 4 + c // 2 + 1)
                        lo_of(nc.vector, oal[:, c:c + 2, :], oa[:, c:c + 2, :], oah[:, c:c + 2, :]).then_inc(sem("oa_lo"), 1)
                    cols = slice(n * NG, (n + 1) * NG)
                    for c in range(0, CH, 2):
                        e.wait_ge(sem("ob_hi"), n * 4 + c // 2 + 1)
                        lo_of(nc.vector, obl[:, c:c + 2, cols], obT[:, c:c + 2, cols], obh[:, c:c + 2, :]).then_inc(sem("ob_lo"), 1)
                    last = n == G3 - 1
                    with e.Fori(0, CH // 2 - last) as i:
                        for j in range(2):
                            chunk(n, i, j)
                chunk(G3 - 1, CH // 2 - 1, 0)
                chunk(G3 - 1, CH // 2 - 1, 1, False)

            @block.tensor
            def _(e):
                def project(i, j, g):
                    p = i * 2 + j
                    n = g % G3
                    if g % G3 == 0:
                        e.wait_ge(sem("qk_lo"), p * 2 + g // G3 - 1)
                    if g >= G3:
                        e.wait_ge(sem("q_ev"), p * 3 + n - 2)
                    pair_product(g >= G3, n).then_inc(sem("kg_mm" if g >= G3 else "qg_mm"), 1)

                def pair(i, j, more):
                    p = i * 2 + j
                    e.wait_ge(sem("k_ev"), p * 3)
                    e.wait_ge(sem("evA"), p * 16)
                    e.wait_ge(sem("evB"), p * 8)
                    e.wait_ge(sem("ot_ev"), p * 8)
                    for t in range(NT):
                        last = tr(PS[:, (4, 5, 7)[t // 4], (t % 4) * P:(t % 4 + 1) * P], kb[j][:, t * P:(t + 1) * P], ident[:])
                        if t in (3, 7, 8):
                            last.then_inc(sem("kt_ps"), 1)
                    e.wait_ge(sem("q_ev"), p * 3)

                    def scores(u):
                        k, hh = u // 2, u % 2
                        i, rows_ = 7 - k, slice(hh * HD, (hh + 1) * HD)
                        if u >= 2:
                            e.wait_ge(sem("ttr"), p * 16 + u - 1)
                        n = (i + 1) * P
                        for c0 in range(0, n, 512):
                            c1 = min(n, c0 + 512)
                            last = mm(PS[:, 2 * (u % 2) + c0 // 512, 0:c1 - c0], qb[j][rows_, i * P:(i + 1) * P], kb[j][rows_, c0:c1], start=True, stop=True)
                        last.then_inc(sem("s_mm"), 1)

                    def turn_probs(u):
                        i = 7 - u // 2
                        e.wait_ge(sem("exp"), p * 16 + u + 1)
                        e.wait_ge(sem("evA"), p * 16 + u)
                        if u == 0:
                            e.wait_ge(sem("kst_A"), p * 2 + 1)
                            e.wait_ge(sem("kst_D"), p + 1)
                        elif i >= 4:
                            e.wait_ge(sem("evB"), p * 8 + u)
                        for b in range(i + 1):
                            last = tr(PS[:, 4 + b // 4, (b % 4) * P:(b % 4 + 1) * P], sP[u % 3][:, b * P:(b + 1) * P], ident[:])
                            if b == min(i, 3):
                                last.then_inc(sem("t0_mm"), 1)
                        if i >= 4:
                            last.then_inc(sem("t1_mm"), 1)

                    def values(u):
                        k, hh = u // 2, u % 2
                        i = 7 - k
                        e.wait_ge(sem("evA"), p * 16 + u + 1)
                        if i >= 4:
                            e.wait_ge(sem("evB"), p * 8 + u + 1)
                        e.wait_ge(sem("norm"), p * 16 + u)
                        for b in range(i + 1):
                            last = mm(PS[:, 6, (u % 4) * HD:(u % 4 + 1) * HD], PTb[u % 2][:, b * P:(b + 1) * P],
                                      vtok[:, b, bass.ds(p * P + hh * HD, HD)], start=b == 0, stop=b == i)
                        last.then_inc(sem("pv_mm"), 1)

                    def turn_out(k):
                        e.wait_ge(sem("norm"), p * 16 + 2 * k + 2)
                        e.wait_ge(sem("ot_ev"), p * 8 + k)
                        if k == 0:
                            e.wait_ge(sem("kst_A"), p * 2 + 2)
                        tr(PS[:, 7, (k % 4) * P:(k % 4 + 1) * P], ot[k % 2], ident[:]).then_inc(sem("ot_mm"), 1)

                    following = (i, 1) if j == 0 else (i + 1, 0)
                    scores(0)
                    scores(1)
                    for u in range(16):
                        turn_probs(u)
                        if u + 2 < 16:
                            scores(u + 2)
                        if u >= 1:
                            values(u - 1)
                        if u >= 3 and u % 2 == 1:
                            turn_out((u - 3) // 2)
                        if more and u >= 10:
                            project(*following, u - 10)
                    values(15)
                    turn_out(7)
                with e.Fori(0, CH // 2 - 1) as i:
                    pair(i, 0, True)
                    pair(i, 1, True)
                pair(CH // 2 - 1, 0, True)
                pair(CH // 2 - 1, 1, False)

                e.wait_ge(sem("ot_ev"), CH * 8)
                e.wait_ge(sem("norm"), CH * 16)

                def turn_keys(i, j):
                    e.wait_ge(sem(f"sk_in{j}"), i * 16 + 16)
                    e.wait_ge(sem("kc_A"), i * 2 + j)
                    e.wait_ge(sem("kc_D"), i * 2 + j)
                    for c in range(CH):
                        for k in range(2):
                            o_ = (c % 2) * PAST + k * P
                            last = tr(PS[:, c // 2, o_:o_ + P], kc[j][:, k, c * P:(c + 1) * P], ident[:])
                        if c in (3, 7):
                            last.then_inc(sem("kc_ps"), 1)

                def sample_scores(i, j):
                    e.wait_ge(sem("kc_A"), i * 2 + j + 1)
                    e.wait_ge(sem("kc_D"), i * 2 + j + 1)
                    e.wait_ge(sem(f"qbd{j}"), i * 3 + 3)
                    for g in range(2):
                        e.wait_ge(sem("s_ttr"), i * 4 + j * 2 + g)
                        for q in range(4):
                            last = mm(PS[32 * q:32 * q + 32, 4 + g, 0:LK], qbd[j][:, 4 * g + q, :], kcT[j][:, 4 * g + q, :], start=True, stop=True)
                        last.then_inc(sem(f"sqk{j}"), 1)

                def turn_sample_probs(i, j, g):
                    e.wait_ge(sem("s_pn"), i * 4 + j * 2 + g + 1)
                    e.wait_ge(sem("s_ptA"), i * 4 + j * 2 + g)
                    e.wait_ge(sem("s_ptD"), i * 4 + j * 2 + g)
                    for k in range(2):
                        tr(PS[:, 6, k * P:(k + 1) * P], sS[j][:, g, k * P:(k + 1) * P], ident[:])
                    tr(PS[0:DS, 6, 2 * P:3 * P], sS[j][:, g, PAST:LK], ident[:]).then_inc(sem("s_tp"), 1)

                def turn_values(i, j):
                    e.wait_ge(sem("o_ev"), i * 2 + j + 1)
                    e.wait_ge(sem("so_A"), i * 2 + j)
                    e.wait_ge(sem("so_D"), i * 2 + j)
                    for g in range(2):
                        last = tr(PS[:, 7, 256 + g * P:256 + (g + 1) * P], osb[j][:, g, :], ident[:])
                    last.then_inc(sem("ot2_mm"), 1)

                def batch(i, j, before, nxt):
                    if nxt:
                        turn_keys(*nxt)
                    turn_sample_probs(i, j, 0)
                    if before:
                        turn_values(*before)
                    if nxt:
                        sample_scores(*nxt)
                    turn_sample_probs(i, j, 1)
                    e.wait_ge(sem(f"sv_in{j}"), i * 32 + 32)
                    if before:
                        e.wait_ge(sem("so_A"), i * 2 + j)
                        e.wait_ge(sem("so_D"), i * 2 + j)
                    for g in range(2):
                        e.wait_ge(sem("s_ptA"), i * 4 + j * 2 + g + 1)
                        e.wait_ge(sem("s_ptD"), i * 4 + j * 2 + g + 1)
                        for q in range(4):
                            c, qs = 4 * g + q, slice(q * 32, q * 32 + 32)
                            for k in range(2):
                                mm(PS[qs, 7, g * P:(g + 1) * P], PTs[j][:, g, k, qs], vc[j][:, k, c * P:(c + 1) * P], start=k == 0, stop=False)
                            last = mm(PS[qs, 7, g * P:(g + 1) * P], PTs[j][0:DS, g, 2, qs], v16[j][:, c * P:(c + 1) * P], start=False, stop=True)
                    last.then_inc(sem(f"spv{j}"), 1)
                turn_keys(0, 0)
                sample_scores(0, 0)
                batch(0, 0, None, (0, 1))
                with e.Fori(0, DB // 2 - 1) as i:
                    batch(i, 1, (i, 0), (i + 1, 0))
                    batch(i + 1, 0, (i, 1), (i + 1, 1))
                batch(DB // 2 - 1, 1, (DB // 2 - 1, 0), None)
                turn_values(DB // 2 - 1, 1)

                def gates(i, j, n):
                    m = i * 2 + j
                    b = (6, 0, 6)[n]
                    if n == 0:
                        e.wait_ge(sem(f"conv{j}"), i + 1)
                        e.wait_ge(sem(f"bw_in{j}"), i * 64 + 64)
                    if n != 1:
                        e.wait_ge(sem("sig"), m * 6 + n)
                    for k in range(2):
                        last = mm(PS[:, b + k, 0:NG], bw[j][:, k, :], xc[j][:, n * NG:(n + 1) * NG], start=True, stop=True)
                    last.then_inc(sem(f"ri_done{j}") if n == G3 - 1 else sem("ri_mm"), 1)

                def step(new, old):
                    if new:
                        i, j = new
                        m = i * 2 + j

                    def project(k, n):
                        cols = slice(n * NG, (n + 1) * NG)
                        product3(PS[:, 3 * k + n, 0:NG], lambda c: wxh[k][:, c, :], lambda c: wxl[k][:, c, :],
                                 lambda c: hTh[:, c, cols], lambda c: hTl[:, c, cols]).then_inc(sem(("xb_mm", "gb_mm")[k]), 1)
                    if new:
                        e.wait_ge(sem("wx_lo0"), m + 1)
                        e.wait_ge(sem(f"xb_ev{1 - j}"), (i + j) * 4)
                        if old:
                            e.wait_ge(sem("sig"), (m - 1) * 6)
                        for n in range(G3):
                            project(0, n)
                    if old:
                        gates(*old, 0)
                        if new:
                            e.wait_ge(sem(f"xb_ev{j}"), i * 4 + 2)
                        gates(*old, 1)
                    if new:
                        e.wait_ge(sem("wx_lo1"), m + 1)
                        e.wait_ge(sem(f"gb_ev{1 - j}"), (i + j) * 3)
                        project(1, 0)
                    if old:
                        gates(*old, 2)
                    if new:
                        for n in (1, 2):
                            project(1, n)
                e.wait_ge(sem("so_A"), DB)
                e.wait_ge(sem("so_D"), DB)
                step((0, 0), None)
                with e.Fori(0, CH // 2 - 1) as i:
                    step((i, 1), (i, 0))
                    step((i + 1, 0), (i, 1))
                step((CH // 2 - 1, 1), (CH // 2 - 1, 0))
                step(None, (CH // 2 - 1, 1))

                def panel(n, i, j, q):
                    m = n * CH + i * 2 + j
                    e.wait_ge(sem(f"wm_lo{q}"), m + 1)

                    def ready(c):
                        if q >= 2 and c % 2 == 0:
                            e.wait_ge(sem(("oa_lo", "ob_lo")[q - 2]), n * 4 + c // 2 + 1)
                    cols = slice(n * NG, (n + 1) * NG)
                    xh, xl = ((hTh[:, :, cols], hTl[:, :, cols]), (hTh[:, :, cols], hTl[:, :, cols]),
                              (oah, oal), (obh, obl[:, :, cols]))[q]
                    product3(PS[:, 4 * j + BANK[q], 0:NG], lambda c: wmh[q][:, c, :], lambda c: wml[q][:, c, :],
                             lambda c: xh[:, c, :], lambda c: xl[:, c, :], ready).then_inc(sem(f"wm_mm{q}"), 1)

                def chunk(n, i, j, first=False):
                    e.wait_ge(sem(f"mixd{j}"), n * CH // 2 + i)
                    for q in range(4):
                        if first and q == 2:
                            e.wait_ge(sem("h_cp"), 2 * CH)
                            e.wait_ge(sem("sig"), 6 * CH)
                            for jj in range(2):
                                e.wait_ge(sem(f"tails{jj}"), CH)
                            for c in range(CH):
                                last = tr(PS[0:36, 6 + c // 4, (c % 4) * P:(c % 4 + 1) * P], hc[:, c, :], ident[:])
                            last.then_inc(sem("hc_ps"), 1)
                        panel(n, i, j, q)
                for s, k in (("xb_ev1", 16), ("gb_ev1", 12), ("sig", 6 * CH)):
                    e.wait_ge(sem(s), k)
                for n in range(G3):
                    if n == 0:
                        chunk(0, 0, 0, True)
                        e.wait_ge(sem("hrow"), 1)
                        chunk(0, 0, 1)
                    with e.Fori(0 if n else 1, CH // 2) as i:
                        for j in range(2):
                            chunk(n, i, j)
        clear_semaphores()

        with nc.Block() as block:

            @block.sync
            def _(e):
                def mix_tile(at):
                    return mix_d.rearrange("(c p) t -> p c t", p=P)[:, :, bass.ds(at, P)]
                def rows_in(j, at):
                    e.dma_start(xo[j], cut(xp[bass.ds(at, P), :], xo[j])).then_inc(sem(f"xo_in{j}"), 16)
                e.dma_start(mt[0], mix_tile(0)).then_inc(sem("mt0"), 16)
                e.dma_start(mt[1], mix_tile(P)).then_inc(sem("mt1"), 16)
                e.dma_start(wo[1], w_out[:, :, 512:1024]).then_inc(sem("wo_in1"), 16)
                e.dma_start(N2, spread(a["norm2"])).then_inc(sem("n2_in"), 16)
                for j in range(2):
                    rows_in(j, j * P)
                e.dma_start(wr[:, :, 0:GR], a["w_rg"][0].rearrange("(c p) n -> p c n", p=P)).then_inc(sem("wr_in"), 16)
                e.dma_start(wr[:, :, GR:], a["w_re"][0].rearrange("(c p) n -> p c n", p=P)).then_inc(sem("wr_in"), 16)
                e.dma_start(br[:, 0:GR], spread(a["b_rg"])).then_inc(sem("wr_in"), 16)
                e.dma_start(br[:, GR:], spread(a["b_re"])).then_inc(sem("wr_in"), 16)
                with e.Fori(1, PT_ // 2) as i:
                    for j in range(2):
                        e.wait_ge(sem(f"out_mm{j}"), i)
                        e.dma_start(mt[j], mix_tile(i * 256 + j * P)).then_inc(sem(f"mt{j}"), 16)
                        e.wait_ge(sem(f"x1_made{j}"), i)
                        rows_in(j, i * 256 + j * P)
                e.wait_ge(sem("out_mm0"), PT_ // 2)
                e.dma_start(mt[0], mix_tile(SEQ)).then_inc(sem("mt0"), 16)
                e.wait_ge(sem("x1_made0"), PT_ // 2)
                e.dma_start(xo[0], cut(xs, xo[0])).then_inc(sem("xo_in0"), 16)
                e.wait_ge(sem("h2_out0"), 16 * (PT_ // 2 + 1))
                e.wait_ge(sem("h2_out1"), 16 * (PT_ // 2))
                mod_load(e, G2, 5, "g2_in")
                e.dma_start(NF, spread(a["norm_f"].rearrange("(a d) -> a d", a=1))).then_inc(sem("g2_in"), 16)
                e.wait_ge(sem("meta"), 1)
                used = e.value_load(meta[0:1, SLOTS:SLOTS + 1], min_val=1, max_val=SLOTS)
                def expert_weights(s, j, n, first=False):
                    if not first:
                        e.wait_ge(sem(f"eh3_{j}"), n)
                    ex_id = e.value_load(meta[0:1, bass.ds(s, 1)], min_val=0, max_val=NE - 1)
                    e.dma_start(w1b[j], w1[bass.ds(ex_id, 1)].rearrange("a (c p) f -> p (a c) f", p=P)).then_inc(sem(f"w1_in{j}"), 16)
                    e.dma_start(w3b[j], w3[bass.ds(ex_id, 1)].rearrange("a (c p) f -> p (a c) f", p=P)).then_inc(sem(f"w3_in{j}"), 16)
                    if first:
                        e.wait_ge(sem("xg_in0"), 16)
                    else:
                        e.wait_ge(sem(f"ey_{j}"), n)
                    e.dma_start(w2b[j], w2[bass.ds(ex_id, 1)].rearrange("a (c p) d -> p (a c) d", p=P)).then_inc(sem(f"w2_in{j}"), 16)
                expert_weights(0, 0, 0, True)
                with e.Fori(0, SLOTS // 2) as i:
                    with e.If(i * 2 + 1 < used):
                        expert_weights(i * 2 + 1, 1, i)
                    with e.If(i * 2 + 2 < used):
                        expert_weights(i * 2 + 2, 0, i + 1)
                for t in range(NT):
                    e.wait_ge(sem("o_made"), t + 1)
                    to = y_s.rearrange("b t d -> (b t) d") if t == PT_ else y_p[0, t * P:(t + 1) * P, :]
                    e.dma_start(to, out_t[t % RING]).then_inc(sem(f"o_out{t % RING}"), 16)
                for j in range(RING):
                    e.wait_ge(sem(f"o_out{j}"), 16 * len(range(j, NT, RING)))

            @block.gpsimd
            def _(e):
                def split_mt(j, n):
                    e.wait_ge(sem(f"mt_hi{j}"), n + 1)
                    lo_of(e, mtl[j], mt[j], mth[j]).then_inc(sem(f"mt_lo{j}"), 1)
                split_mt(0, 0)
                split_mt(1, 0)

                def shift(j, k, n):
                    e.wait_ge(sem(f"h2_sc{j}"), n + 1)
                    e.tensor_tensor(cut(h2[j], B2[k]), cut(h2[j], B2[k]), B2[k], ALU.add).then_inc(sem(f"h2_made{j}"), 1)

                def turn(i, last):
                    split_mt(0, i + 1)
                    shift(0, 0, i)
                    shift(1, 0, i)
                    if last:
                        shift(0, 1, i + 1)
                    else:
                        split_mt(1, i + 1)
                with e.Fori(0, PT_ // 2 - 1) as i:
                    turn(i, False)
                turn(PT_ // 2 - 1, True)
                e.wait_ge(sem("out_mm0"), PT_ // 2 + 1)
                e.iota(iotaf, [[1, P]], base=0, channel_multiplier=0, allow_small_or_imprecise_dtypes=True).then_inc(sem("iotas"), 1)
                e.iota(thr, [[P, 9]], base=0, channel_multiplier=0, allow_small_or_imprecise_dtypes=True).then_inc(sem("iotas"), 1)
                e.iota(tokf, [[P, NT]], base=0, channel_multiplier=1, allow_small_or_imprecise_dtypes=True).then_inc(sem("iotas"), 1)
                e.memset(g8, -BIG).then_inc(sem("iotas"), 1)
                count = e.alloc_register("count3")
                e.wait_ge(sem("meta"), 2)
                e.wait_ge(sem("h2_out0"), 16 * (PT_ // 2 + 1))
                e.wait_ge(sem("h2_out1"), 16 * (PT_ // 2))

                def gather(col, j):
                    e.tensor_copy(gidx[j][:], rows[:, col]).then_inc(sem(f"gidx{j}"), 1)

                def gather2(j, n):
                    e.reg_mov(count, n)
                    e.wait_ge(sem("meta"), 2)
                    e.wait_ge(sem(f"gidx{j}"), count)
                    e.indirect_dma_start(out=xg[j], out_offset=None, in_=h2_d, in_offset=bass.IndirectOffsetOnAxis(ap=gidx[j][:], axis=0)).then_inc(sem(f"xg_in{j}"), 16)
                gather(bass.ds(0, 1), 0)
                gather2(0, 1)
                used = e.value_load(meta[0:1, SLOTS:SLOTS + 1], min_val=1, max_val=SLOTS)
                with e.Fori(0, SLOTS // 2) as i:
                    for j in range(2):
                        with e.If(i * 2 + j < used):
                            e.wait_ge(sem("tx_mm"), i * 2 + j)
                            gather(bass.ds(i * 2 + j + 1, 1), 1 - j)
                            gather2(1 - j, i + 1 + j)
                e.wait_ge(sem("g2_in"), MOD_LOAD + 16)
                e.wait_ge(sem("yb_out0"), (used + 1) // 2 * 16)
                e.wait_ge(sem("yb_out1"), used // 2 * 16)
                e.tensor_tensor(small[:, 7:8], ones[:, 0:1], ones[:, 0:1], ALU.add).then_inc(sem("y_all"), 1)
                e.wait_ge(sem("y_all"), 1)

                def pick(t):
                    if t >= RING:
                        e.wait_ge(sem("c_used"), t - RING + 1)
                    for k in range(2):
                        e.indirect_dma_start(out=y01[k][t % RING], out_offset=None, in_=yb_d,
                                             in_offset=bass.IndirectOffsetOnAxis(ap=dest[:, k, t:t + 1], axis=0)).then_inc(sem(f"y_in{t % RING}"), 16)
                for t in range(RING):
                    pick(t)
                for t in range(NT):
                    e.wait_ge(sem("c_used"), t + 1)
                    e.tensor_tensor(acc[t % RING], acc[t % RING], G2[t == PT_], ALU.mult).then_inc(sem("c_g"), 1)
                    if t + RING < NT:
                        pick(t + RING)

            @block.scalar
            def _(e):
                def split_wo(k, first, end):
                    for c in range(first, end, 2):
                        act(woh[k][:, c:c + 2, :], wo[k][:, c:c + 2, :], ACT.Copy).then_inc(sem("wo_hi"), 1)

                def split_mt(j, n):
                    e.wait_ge(sem(f"mt{j}"), n * 16 + 16)
                    act(mth[j], mt[j], ACT.Copy).then_inc(sem(f"mt_hi{j}"), 1)
                split_wo(0, 0, 4)
                split_mt(0, 0)
                split_wo(0, 4, CH)
                split_mt(1, 0)
                e.wait_ge(sem("wo_in1"), 16)
                split_wo(1, 0, CH)

                def rms2(j, n):
                    e.wait_ge(sem("x1_made0"), 1)
                    e.wait_ge(sem(f"x1_made{j}"), n + 1)
                    e.wait_ge(sem("h2n"), n * 2 + j)
                    act(junk, x1b[:, bass.ds(n * 2 + j, 1), :].rearrange("p a d -> p (a d)"), ACT.Square, accum_out=ssq[:, j:j + 1]).then_inc(sem("ss2"), 1)
                    e.wait_ge(sem("ss2"), n * 2 + j + 1)
                    act(rms[:, j:j + 1], ssq[:, j:j + 1], ACT.Sqrt, scale=1.0 / D, bias=eps).then_inc(sem(f"rms2{j}"), 1)

                def send(j, rows_, n):
                    e.wait_ge(sem(f"h2_made{j}"), n + 1)
                    e.dma_start(h2_d[rows_, :], h2[j]).then_inc(sem(f"h2_out{j}"), 16)

                def put_h2(j, n):
                    e.wait_ge(sem(f"ht_mm{j}"), n + 1)
                    e.wait_ge(sem(f"lg_mm{j}"), n)
                    act(h2T[j][:, 4:8, :], PS[:, 5, :].rearrange("p (c n) -> p c n", c=4), ACT.Copy).then_inc(sem(f"ht_A{j}"), 1)
                rms2(0, 0)

                def turn(i, last=False):
                    split_mt(0, i + 1)
                    send(0, bass.ds(i * 256, P), i)
                    rms2(1, i)
                    put_h2(0, i)
                    if not last:
                        split_mt(1, i + 1)
                    send(1, bass.ds(i * 256 + P, P), i)
                    rms2(0, i + 1)
                    put_h2(1, i)
                with e.Fori(0, PT_ // 2 - 1) as i:
                    turn(i)
                turn(PT_ // 2 - 1, True)
                send(0, bass.ds(SEQ, P), PT_ // 2)
                put_h2(0, PT_ // 2)

                e.wait_ge(sem("gd"), 1)
                act(oh4, oh4, ACT.Exp).then_inc(sem("gexp"), 1)
                e.wait_ge(sem("edd"), 1)
                act(ed, ed, ACT.Exp).then_inc(sem("eexp"), 1)

                def put_x(j, s):
                    e.wait_ge(sem("tx_mm"), s + 1)
                    act(xT[j][:, 0:4, :], PS[:, 0, :].rearrange("p (c n) -> p c n", c=4), ACT.Copy).then_inc(sem("xT_A"), 1)
                e.wait_ge(sem("meta"), 2)
                used = e.value_load(meta[0:1, SLOTS:SLOTS + 1], min_val=1, max_val=SLOTS)
                put_x(0, 0)
                with e.Fori(0, SLOTS // 2) as i:
                    for j in range(2):
                        s = i * 2 + j
                        with e.If(s < used):
                            e.wait_ge(sem("eh1"), s + 1)
                            e.wait_ge(sem("eh"), s)
                            act(hs, PS[:, 2, :], ACT.Silu).then_inc(sem("silu"), 1)
                            put_x(1 - j, s + 1)
                            e.wait_ge(sem(f"yb_out{j}"), i * 16)
                            e.wait_ge(sem("ey"), s + 1)
                            act(yo[j][:, 0:512], PS[:, 5, :], ACT.Copy).then_inc(sem("yo_A"), 1)
                            e.wait_ge(sem("yo_A"), s + 1)
                            e.wait_ge(sem("yo_D"), s + 1)
                            e.dma_start(yb_d[bass.ds(s * P, P), :], yo[j]).then_inc(sem(f"yb_out{j}"), 16)
                def first(t):
                    j = t % RING
                    if t >= RING:
                        e.wait_ge(sem("o_made"), t - RING + 1)
                    e.wait_ge(sem(f"y_in{j}"), (t // RING + 1) * 32)
                    act(acc[j], y01[0][j], ACT.Copy, scale=wts[:, 0, t:t + 1]).then_inc(sem("y0w"), 1)

                def squares(t):
                    j = t % RING
                    e.wait_ge(sem("x2_made"), t + 1)
                    if t >= RING:
                        e.wait_ge(sem(f"o_out{j}"), 16 * (t // RING))
                    act(out_t[j], acc[j], ACT.Square, accum_out=ssq3[:, j:j + 1]).then_inc(sem("ss3"), 1)

                def root(t):
                    j = t % RING
                    e.wait_ge(sem("ss3"), t + 1)
                    act(rms3s[:, j:j + 1], ssq3[:, j:j + 1], ACT.Sqrt, scale=1.0 / D, bias=eps).then_inc(sem("rms3"), 1)
                for t in PAIRS[0]:
                    first(t)
                for n, pair in enumerate(PAIRS):
                    for t in (PAIRS[n + 1] if n + 1 < len(PAIRS) else ()):
                        first(t)
                    for t in pair:
                        squares(t)
                    for t in pair:
                        root(t)

            @block.vector
            def _(e):
                for k in range(2):
                    for c in range(0, CH, 2):
                        e.wait_ge(sem("wo_hi"), k * 4 + c // 2 + 1)
                        lo_of(nc.vector, wol[k][:, c:c + 2, :], wo[k][:, c:c + 2, :], woh[k][:, c:c + 2, :]).then_inc(sem("wo_lo"), 1)
                e.wait_ge(sem("n2_in"), 16)
                for b in range(2):
                    stt(out=A2[b], in0=A2[b], scalar=1.0, in1=cut(N2, A2[b]), op0=ALU.add, op1=ALU.mult).then_inc(sem("a2"), 1)
                e.wait_ge(sem("a2"), 2)

                def resid(j, n, k):
                    row = x1b[:, bass.ds(n * 2 + j, 1), :].rearrange("p a d -> p (a d)")
                    e.wait_ge(sem(f"out_mm{j}"), n + 1)
                    tt(cut(row, G1[k]), PS[:, 2 * j:2 * j + 2, :], G1[k], ALU.mult).then_inc(sem(f"gmul{j}"), 1)
                    e.wait_ge(sem(f"xo_in{j}"), n * 16 + 16)
                    e.wait_ge(sem(f"gmul{j}"), n + 1)
                    tt(cut(row, xo[j]), cut(row, xo[j]), xo[j], ALU.add).then_inc(sem(f"x1_made{j}"), 1)
                    e.wait_ge(sem(f"rms2{j}"), n + 1)
                    e.wait_ge(sem(f"x1_made{j}"), n + 1)
                    nc.vector.reciprocal(rst[:, j:j + 1], rms[:, j:j + 1]).then_inc(sem("h2n"), 1)
                    e.wait_ge(sem("h2n"), n * 2 + j + 1)
                    e.wait_ge(sem(f"h2_out{j}"), n * 16)
                    e.wait_ge(sem(f"ht_mm{j}"), n)
                    stt(out=cut(h2[j], A2[k]), in0=cut(row, A2[k]), scalar=rst[:, j:j + 1], in1=A2[k], op0=ALU.mult, op1=ALU.mult).then_inc(sem(f"h2_sc{j}"), 1)

                def turned(j, n):
                    e.wait_ge(sem(f"ht_mm{j}"), n + 1)
                    e.wait_ge(sem(f"lg_mm{j}"), n)
                    copy(h2T[j][:, 0:4, :], PS[:, 4, :].rearrange("p (c n) -> p c n", c=4)).then_inc(sem(f"ht_D{j}"), 1)

                def logits(j, n):
                    e.wait_ge(sem("wr_in"), 64)
                    e.wait_ge(sem(f"lg_mm{j}"), n + 1)
                    tt(lg[:, bass.ds(n * 2 + j, 1), :], PS[:, 6 + j, 0:GR + NE].rearrange("p (a n) -> p a n", a=1),
                       br[:].rearrange("p (a n) -> p a n", a=1), ALU.add).then_inc(sem(f"lg{j}"), 1)
                resid(0, 0, 0)
                resid(1, 0, 0)
                turned(0, 0)
                with e.Fori(0, PT_ // 2 - 1) as i:
                    resid(0, i + 1, 0)
                    turned(1, i)
                    logits(0, i)
                    resid(1, i + 1, 0)
                    turned(0, i + 1)
                    logits(1, i)
                last = PT_ // 2 - 1
                resid(0, last + 1, 1)
                turned(1, last)
                logits(0, last)
                turned(0, last + 1)
                logits(1, last)
                logits(0, last + 1)

                st = Steps(e, sem("dve_route"))

                def step(ins):
                    st.did(ins)
                    st.wait()

                def bc(v, *dims):
                    return v.unsqueeze(len(v.shape)).broadcast_to([P, *dims])

                def number_row(v, *dims):
                    for _k in range(len(dims) - 1):
                        v = v.unsqueeze(1)
                    return v.broadcast_to([P, *dims])
                e.wait_ge(sem("iotas"), 4)
                e.wait_ge(sem("lg0"), PT_ // 2 + 1)
                e.wait_ge(sem("lg1"), PT_ // 2)
                step(copy(g8[:, :, 0:GR], lg[:, :, 0:GR]))
                for t in range(NT):
                    st.did(nc.vector.max(gm[:, t, :], g8[:, t, :]))
                st.wait()
                for t in range(NT):
                    st.did(nc.vector.max_index(gi[:, t, :], gm[:, t, :], g8[:, t, :]))
                st.wait()
                step(copy(gif, gi[:, :, 0]))
                step(tt(oh4, bc(gif, NT, GR), number_row(iotaf[:, 0:GR], NT, GR), ALU.is_equal))
                g4 = lambda v: v.rearrange("p t (g e) -> p t g e", g=GR)
                step(tt(g4(gx), g4(lg[:, :, GR:]), bc(oh4, NT, GR, EG), ALU.mult))
                step(nc.vector.tensor_reduce(e8, gx.rearrange("p t (g e) -> p t e g", g=GR), AX_X, ALU.add))
                for t in range(NT):
                    st.did(nc.vector.max(em[:, t, :], e8[:, t, :]))
                st.wait()
                for t in range(NT):
                    st.did(nc.vector.max_index(ei[:, t, :], em[:, t, :], e8[:, t, :]))
                st.wait()
                tt(oh4, lg[:, :, 0:GR], bc(gm[:, :, 0], NT, GR), ALU.subtract).then_inc(sem("gd"), 1)
                tt(ed, em[:, :, 1], em[:, :, 0], ALU.subtract).then_inc(sem("edd"), 1)
                e.wait_ge(sem("gexp"), 1)
                step(nc.vector.reduce_sum(pg, oh4, AX_X))
                step(nc.vector.reciprocal(pg, pg))
                e.wait_ge(sem("eexp"), 1)
                step(ts(den, ed, 1.0, None, ALU.add))
                step(nc.vector.reciprocal(den, den))
                step(tt(wts[:, 0, :], pg, den, ALU.mult))
                step(tt(wts[:, 1, :], wts[:, 0, :], ed, ALU.mult))
                for k in range(2):
                    step(copy(eidf[:, k, :], ei[:, :, k]))
                    step(stt(out=eidf[:, k, :], in0=gif, scalar=float(EG), in1=eidf[:, k, :], op0=ALU.mult, op1=ALU.add))
                    step(tt(E[k], bc(eidf[:, k, :], NT, NE), number_row(iotaf[:, 0:NE], NT, NE), ALU.is_equal))
                tt(M, E[0], E[1], ALU.add).then_inc(sem("M"), 1)
                e.wait_ge(sem("cnt_mm"), 1)
                step(copy(cs.rearrange("p t e -> p (t e)"), PS[:, 0, 0:NT * NE]))
                step(nc.vector.memset(pre[:, 0, :], 0.0))
                for t in range(1, NT):
                    step(tt(pre[:, t, :], pre[:, t - 1, :], cs[:, t - 1, :], ALU.add))
                step(tt(tot, pre[:, NT - 1, :], cs[:, NT - 1, :], ALU.add))
                step(tt(rk.rearrange("p t e -> p (t e)"), PS[:, 1, 0:NT * NE], pre.rearrange("p t e -> p (t e)"), ALU.add))
                step(tt(cmp9, bc(tot, NE, 9), number_row(thr, NE, 9), ALU.is_gt))
                step(nc.vector.reduce_sum(nb, cmp9, AX_X))
                step(nc.vector.tensor_tensor_scan(endb, ones[:, 0:NE], nb, 0.0, ALU.mult, ALU.add))
                step(tt(startb, endb, nb, ALU.subtract))
                for k in range(2):
                    step(tt(ex, rk, E[k], ALU.mult))
                    step(nc.vector.reduce_sum(rj[:, k, :], ex, AX_X))
                    step(tt(ex, number_row(startb, NT, NE), E[k], ALU.mult))
                    step(nc.vector.reduce_sum(sj[:, k, :], ex, AX_X))
                fl = lambda v: v.rearrange("p k t -> p (k t)")
                step(tt(cmp8, bc(fl(rj), 2 * NT, 8), number_row(thr[:, 1:9], 2 * NT, 8), ALU.is_ge))
                step(nc.vector.reduce_sum(fl(qj), cmp8, AX_X))
                step(tt(slj, sj, qj, ALU.add))
                step(stt(out=roj, in0=qj, scalar=-float(P), in1=rj, op0=ALU.mult, op1=ALU.add))
                step(stt(out=dej, in0=slj, scalar=float(P), in1=roj, op0=ALU.mult, op1=ALU.add))
                step(copy(dest[:], dej))
                step(tt(cmpb, endb[0:1].unsqueeze(1).broadcast_to([1, SLOTS, NE]), iotaf[0:1, 0:SLOTS].unsqueeze(2).broadcast_to([1, SLOTS, NE]), ALU.is_le))
                step(nc.vector.reduce_sum(OS[0][0:1, :], cmpb, AX_X))
                step(copy(meta[0:1, 0:SLOTS], OS[0][0:1, :]))
                copy(meta[0:1, SLOTS:], endb[0:1, NE - 1:NE]).then_inc(sem("meta"), 1)
                for q in range(2 * NT):
                    t, k = q // 2, q % 2
                    if q >= 2:
                        e.wait_ge(sem("tab_mm"), q - 1)
                    ts(OP[q % 2], iotaf, roj[:, k, t:t + 1], None, ALU.is_equal).then_inc(sem("OPS"), 1)
                    ts(OS[q % 2], iotaf[:, 0:SLOTS], slj[:, k, t:t + 1], tokf[:, t:t + 1], ALU.is_equal, ALU.mult).then_inc(sem("OPS"), 1)
                step(nc.vector.memset(rows[:, SLOTS:], 0))
                e.wait_ge(sem("tab_mm"), 2 * NT)
                copy(rows[:, 0:SLOTS], PS[:, 2, 0:SLOTS]).then_inc(sem("meta"), 1)

                def put_x(j, s):
                    e.wait_ge(sem("tx_mm"), s + 1)
                    copy(xT[j][:, 4:8, :], PS[:, 1, :].rearrange("p (c n) -> p c n", c=4)).then_inc(sem("xT_D"), 1)
                e.wait_ge(sem("meta"), 2)
                used = e.value_load(meta[0:1, SLOTS:SLOTS + 1], min_val=1, max_val=SLOTS)
                put_x(0, 0)
                with e.Fori(0, SLOTS // 2) as i:
                    for j in range(2):
                        s = i * 2 + j
                        with e.If(s < used):
                            e.wait_ge(sem(f"eh3_{j}"), i + 1)
                            e.wait_ge(sem("silu"), s + 1)
                            e.wait_ge(sem("eh_T"), s)
                            tt(hh_, hs, PS[:, 3, :], ALU.mult).then_inc(sem("eh"), 1)
                            put_x(1 - j, s + 1)
                            e.wait_ge(sem("eh_T"), s + 1)
                            e.wait_ge(sem("ey"), s)
                            if j:
                                e.wait_ge(sem("ey_0"), i + 1)
                            else:
                                e.wait_ge(sem("ey_1"), i)
                            copy(hhT, PS[:, 4, :].rearrange("p (c n) -> p c n", c=DE // P)).then_inc(sem("ehT"), 1)
                            e.wait_ge(sem(f"yb_out{j}"), i * 16)
                            e.wait_ge(sem(f"ey_{j}"), i + 1)
                            copy(yo[j][:, 512:1024], PS[:, 6, :]).then_inc(sem("yo_D"), 1)

                e.wait_ge(sem("g2_in"), MOD_LOAD + 16)
                st = Steps(e, sem("dve_comb"))

                def combine(t):
                    j = t % RING
                    e.wait_ge(sem(f"y_in{j}"), (t // RING + 1) * 32)
                    e.wait_ge(sem("y0w"), t + 1)
                    stt(out=acc[j], in0=y01[1][j], scalar=wts[:, 1, t:t + 1], in1=acc[j], op0=ALU.mult, op1=ALU.add).then_inc(sem("c_used"), 1)

                def residual(t):
                    j = t % RING
                    e.wait_ge(sem("c_g"), t + 1)
                    tt(acc[j], acc[j], x1b[:, t, :], ALU.add).then_inc(sem("x2_made"), 1)

                def finish(t):
                    j = t % RING
                    e.wait_ge(sem("rms3"), t + 1)
                    st.did(nc.vector.reciprocal(rst3[:, j:j + 1], rms3s[:, j:j + 1]))
                    st.wait()
                    stt(out=out_t[j], in0=acc[j], scalar=rst3[:, j:j + 1], in1=NF, op0=ALU.mult, op1=ALU.mult).then_inc(sem("o_made"), 1)
                for t in PAIRS[0]:
                    combine(t)
                for n, pair in enumerate(PAIRS):
                    for t in pair:
                        residual(t)
                    for t in (PAIRS[n + 1] if n + 1 < len(PAIRS) else ()):
                        combine(t)
                    for t in pair:
                        finish(t)

            @block.tensor
            def _(e):
                def half(j, k, first=False):
                    def ready(c):
                        if c % 2 == 0:
                            e.wait_ge(sem("wo_lo"), k * 4 + c // 2 + 1)
                    return product3(PS[:, 2 * j + k, :], lambda c: mth[j][:, c, :], lambda c: mtl[j][:, c, :],
                                    lambda c: woh[k][:, c, :], lambda c: wol[k][:, c, :], ready if first else None)

                def out(j, n):
                    e.wait_ge(sem(f"mt_lo{j}"), n + 1)
                    e.wait_ge(sem(f"gmul{j}"), n)
                    half(j, 0)
                    half(j, 1).then_inc(sem(f"out_mm{j}"), 1)

                def turn_h2(j, n):
                    e.wait_ge(sem(f"h2_made{j}"), n + 1)
                    e.wait_ge(sem(f"ht_A{1 - j}"), n + j)
                    e.wait_ge(sem(f"ht_D{1 - j}"), n + j)
                    for c in range(CH):
                        last = tr(PS[:, 4 + c // 4, (c % 4) * P:(c % 4 + 1) * P], h2[j][:, c * P:(c + 1) * P], ident[:])
                    last.then_inc(sem(f"ht_mm{j}"), 1)

                def route(j, n):
                    e.wait_ge(sem(f"ht_A{j}"), n + 1)
                    e.wait_ge(sem(f"ht_D{j}"), n + 1)
                    e.wait_ge(sem(f"lg{j}"), n)
                    product(PS[:, 6 + j, 0:GR + NE], lambda c: h2T[j][:, c, :], lambda c: wr[:, c, :]).then_inc(sem(f"lg_mm{j}"), 1)
                for j in range(2):
                    for k in range(2):
                        e.wait_ge(sem(f"mt_lo{j}"), 1)
                        last = half(j, k, True)
                        if k:
                            last.then_inc(sem(f"out_mm{j}"), 1)
                e.wait_ge(sem("wr_in"), 64)
                turn_h2(0, 0)
                with e.Fori(0, PT_ // 2 - 1) as i:
                    out(0, i + 1)
                    route(0, i)
                    turn_h2(1, i)
                    out(1, i + 1)
                    route(1, i)
                    turn_h2(0, i + 1)
                last = PT_ // 2 - 1
                out(0, last + 1)
                route(0, last)
                turn_h2(1, last)
                route(1, last)
                turn_h2(0, last + 1)
                route(0, last + 1)

                e.wait_ge(sem("M"), 1)
                mm(PS[:, 0, 0:NT * NE], ones[:], M.rearrange("p t e -> p (t e)"), start=True, stop=True)
                mm(PS[:, 1, 0:NT * NE], upper[:], M.rearrange("p t e -> p (t e)"), start=True, stop=True).then_inc(sem("cnt_mm"), 1)
                for q in range(2 * NT):
                    e.wait_ge(sem("OPS"), 2 * q + 2)
                    mm(PS[:, 2, 0:SLOTS], OP[q % 2], OS[q % 2], start=q == 0, stop=q == 2 * NT - 1).then_inc(sem("tab_mm"), 1)

                def turn_rows(j, s, n):
                    e.wait_ge(sem(f"xg_in{j}"), n * 16)
                    e.wait_ge(sem("xT_A"), s)
                    e.wait_ge(sem("xT_D"), s)
                    for c in range(CH):
                        last = tr(PS[:, c // 4, (c % 4) * P:(c % 4 + 1) * P], xg[j][:, c * P:(c + 1) * P], ident[:])
                    last.then_inc(sem("tx_mm"), 1)
                e.wait_ge(sem("meta"), 2)
                used = e.value_load(meta[0:1, SLOTS:SLOTS + 1], min_val=1, max_val=SLOTS)
                turn_rows(0, 0, 1)
                with e.Fori(0, SLOTS // 2) as i:
                    for j in range(2):
                        s = i * 2 + j
                        with e.If(s < used):
                            e.wait_ge(sem("xT_A"), s + 1)
                            e.wait_ge(sem("xT_D"), s + 1)
                            e.wait_ge(sem("eh"), s)
                            e.wait_ge(sem(f"w1_in{j}"), i * 16 + 16)
                            product(PS[:, 2, :], lambda c: xT[j][:, c, :], lambda c: w1b[j][:, c, :]).then_inc(sem("eh1"), 1)
                            e.wait_ge(sem(f"w3_in{j}"), i * 16 + 16)
                            product(PS[:, 3, :], lambda c: xT[j][:, c, :], lambda c: w3b[j][:, c, :]).then_inc(sem(f"eh3_{j}"), 1)
                            turn_rows(1 - j, s + 1, i + 1 + j)
                            e.wait_ge(sem("eh"), s + 1)
                            e.wait_ge(sem("ehT"), s)
                            for c in range(DE // P):
                                last = tr(PS[:, 4, c * P:(c + 1) * P], hh_[:, c * P:(c + 1) * P], ident[:])
                            last.then_inc(sem("eh_T"), 1)
                            e.wait_ge(sem("ehT"), s + 1)
                            e.wait_ge(sem(f"w2_in{j}"), i * 16 + 16)
                            e.wait_ge(sem("yo_A"), s)
                            for k in range(2):
                                if k:
                                    e.wait_ge(sem("yo_D"), s)
                                for c in range(DE // P):
                                    last = mm(PS[:, 5 + k, :], hhT[:, c, :], w2b[j][:, c, 512 * k:512 * (k + 1)], start=c == 0, stop=c == DE // P - 1)
                                last.then_inc(sem(f"ey_{j}") if k else sem("ey"), 1)


INPUTS = ["x_prompt", "x_sample", "cache_k", "cache_v", "cache_logf", "state_conv", "state_h", "c_prompt", "c_sample",
          "w_mod", "b_mod", "norm1", "w_in", "b_f", "conv_w", "conv_b", "w_r", "b_r", "w_i", "b_i", "rglru_lambda",
          "w_gate", "b_gate", "w_pa", "w_pb", "w_out", "norm2", "w_rg", "b_rg", "w_re", "b_re", "w1", "w3", "w2", "norm_f"]
OUTPUTS = [(1, SEQ, D), (DB, DS, D), (1, 1, SEQ, H, HD), (1, 1, SEQ, H, HD), (1, 1, SEQ, H), (1, 1, 3, D), (1, 1, D),
           (1, DB, DS, H, HD), (1, DB, DS, H, HD), (1, DB, DS, H), (1, DB, 3, D), (1, DB, D)]


def kernel(**inputs):
    import numpy as np
    import concourse.bacc as bacc
    from concourse.bass_utils import run_bass_kernel_spmd

    nc = bacc.Bacc("TRN2", target_bir_lowering=False, num_devices=1)
    arrays, args = {}, {}
    for name in INPUTS:
        arrays[f"in_{name}"] = np.ascontiguousarray(inputs[name])
        args[name] = nc.dram_tensor(f"in_{name}", arrays[f"in_{name}"].shape, F32, kind="ExternalInput").ap()
    outs = [nc.dram_tensor(f"out_{n}", shape, F32, kind="ExternalOutput").ap() for n, shape in enumerate(OUTPUTS)]
    trunk(nc, args, outs)
    result = run_bass_kernel_spmd(nc, [arrays], core_ids=[0]).results[0]
    return tuple(result[f"out_{n}"] for n in range(len(OUTPUTS)))
```
